# Optimizing a Trainium2 kernel written in Bass

```python
import math
import jax, jax.numpy as jnp
from jax import lax
import numpy as np
import jax
import jax.numpy as jnp

D_MODEL = 1024
BATCH = 1
SEQ = 256
DEPTH = 1

D_MIX = D_MODEL
D_LRU = D_MIX // 2
D_ATTN = D_MIX - D_LRU
N_LRU_BLOCKS = 8
LRU_BLOCK = D_LRU // N_LRU_BLOCKS
CONV_WIDTH = 4
LRU_C = 8.0
N_HEADS = 8
HEAD_DIM = D_ATTN // N_HEADS
MOBA_BLOCK = 256
MOBA_TOPK = 3
Q_CHUNK = 32
REL_BUCKETS = 32
REL_MAX_DIST = 128
N_GROUPS = 4
EXPERTS_PER_GROUP = 8
N_EXPERTS = N_GROUPS * EXPERTS_PER_GROUP
EXPERT_TOPK = 2
D_EXPERT = 256
MOE_ROWS = 128
LN_EPS = 1e-5
DEEPNORM_ALPHA = (2.0 * DEPTH) ** 0.25
DEEPNORM_BETA = (8.0 * DEPTH) ** -0.25
N_MOD = 6
D_IN_PROJ = 2 * D_LRU + 3 * D_ATTN


def _normalize(x):
    xf = x.astype(jnp.float32)
    mu = jnp.mean(xf, axis=-1, keepdims=True)
    var = jnp.mean(jnp.square(xf - mu), axis=-1, keepdims=True)
    return (xf - mu) * lax.rsqrt(var + LN_EPS)

def layernorm(x, g, b):
    return (_normalize(x) * g + b).astype(x.dtype)

def rmsnorm(x, g):
    xf = x.astype(jnp.float32)
    y = xf * lax.rsqrt(jnp.mean(jnp.square(xf), axis=-1, keepdims=True) + LN_EPS)
    return (y * g).astype(x.dtype)

def modulate(x, shift, scale):
    return (_normalize(x) * (1.0 + scale) + shift).astype(x.dtype)

def causal_depthwise_conv(x, w, b):
    s = x.shape[1]
    xp = jnp.pad(x, ((0, 0), (CONV_WIDTH - 1, 0), (0, 0)))
    return sum(w[k] * xp[:, k:k + s] for k in range(CONV_WIDTH)) + b

def rg_lru(xc, w_a, b_a, w_x, b_x, lam):
    bsz, s, _ = xc.shape
    xb = xc.reshape(bsz, s, N_LRU_BLOCKS, LRU_BLOCK)
    r = jax.nn.sigmoid(jnp.einsum('bsni,nij->bsnj', xb, w_a) + b_a).reshape(bsz, s, D_LRU)
    i = jax.nn.sigmoid(jnp.einsum('bsni,nij->bsnj', xb, w_x) + b_x).reshape(bsz, s, D_LRU)
    log_a = -LRU_C * r.astype(jnp.float32) * jax.nn.softplus(-lam.astype(jnp.float32))
    a = jnp.exp(log_a)
    mult = jnp.sqrt(-jnp.expm1(2.0 * log_a))
    u = mult * (i * xc).astype(jnp.float32)

    def combine(left, right):
        a1, b1 = left
        a2, b2 = right
        return a1 * a2, a2 * b1 + b2

    _, h = lax.associative_scan(combine, (a, u), axis=1)
    return h.astype(xc.dtype)

def t5_bucket(rel):
    n = jnp.maximum(rel, 0)
    max_exact = REL_BUCKETS // 2
    large = max_exact + (jnp.log(jnp.maximum(n, 1).astype(jnp.float32) / max_exact)
                         / math.log(REL_MAX_DIST / max_exact)
                         * (REL_BUCKETS - max_exact)).astype(jnp.int32)
    large = jnp.minimum(large, REL_BUCKETS - 1)
    return jnp.where(n < max_exact, n, large)

def moba_attention(q, k, v, rel_bias):
    bsz, s, h, dh = q.shape
    nb = -(-s // MOBA_BLOCK)
    sp = nb * MOBA_BLOCK
    pad = ((0, 0), (0, sp - s), (0, 0), (0, 0))
    qp = jnp.pad(q, pad).transpose(0, 2, 1, 3)
    kp = jnp.pad(k, pad).transpose(0, 2, 1, 3)
    vp = jnp.pad(v, pad).transpose(0, 2, 1, 3)
    scale = HEAD_DIM ** -0.5
    k_blocks = kp.reshape(bsz, h, nb, MOBA_BLOCK, dh)
    v_blocks = vp.reshape(bsz, h, nb, MOBA_BLOCK, dh)
    k_mean = jnp.mean(k_blocks, axis=3)

    own_all = jnp.arange(sp) // MOBA_BLOCK
    past = jnp.arange(nb)[None, :] < own_all[:, None]
    gate = jnp.einsum('bhqd,bhnd->bhqn', qp, k_mean).astype(jnp.float32)
    gate = jnp.where(past, gate, -jnp.inf)
    if nb < MOBA_TOPK:
        gate = jnp.pad(gate, ((0, 0), (0, 0), (0, 0), (0, MOBA_TOPK - nb)), constant_values=-jnp.inf)
    _, sel = lax.top_k(gate, MOBA_TOPK)

    table_h = rel_bias.T
    b_idx = jnp.arange(bsz)
    h_idx = jnp.arange(h)
    kv_offsets = jnp.arange(MOBA_BLOCK)

    def chunk(ci):
        start = ci * Q_CHUNK
        qc = lax.dynamic_slice_in_dim(qp, start, Q_CHUNK, axis=2)
        selc = lax.dynamic_slice_in_dim(sel, start, Q_CHUNK, axis=2)
        qpos = start + jnp.arange(Q_CHUNK)
        own = start // MOBA_BLOCK
        valid = selc < own
        selg = jnp.minimum(selc, nb - 1)
        kg = k_blocks[b_idx[:, None, None, None], h_idx[None, :, None, None], selg]
        vg = v_blocks[b_idx[:, None, None, None], h_idx[None, :, None, None], selg]
        kpos_p = selg[..., None] * MOBA_BLOCK + kv_offsets
        s_p = jnp.einsum('bhqd,bhqnkd->bhqnk', qc, kg).astype(jnp.float32) * scale
        s_p = s_p + table_h[h_idx[None, :, None, None, None], t5_bucket(qpos[:, None, None] - kpos_p)]
        s_p = jnp.where(valid[..., None], s_p, -jnp.inf)
        ko = lax.dynamic_slice_in_dim(kp, own * MOBA_BLOCK, MOBA_BLOCK, axis=2)
        vo = lax.dynamic_slice_in_dim(vp, own * MOBA_BLOCK, MOBA_BLOCK, axis=2)
        rel_o = qpos[:, None] - (own * MOBA_BLOCK + kv_offsets)[None, :]
        s_o = jnp.einsum('bhqd,bhkd->bhqk', qc, ko).astype(jnp.float32) * scale
        s_o = s_o + table_h[:, t5_bucket(rel_o)]
        s_o = jnp.where(rel_o >= 0, s_o, -jnp.inf)
        logits = jnp.concatenate([s_p.reshape(bsz, h, Q_CHUNK, MOBA_TOPK * MOBA_BLOCK), s_o], axis=-1)
        p = jax.nn.softmax(logits, axis=-1)
        p_p = p[..., :MOBA_TOPK * MOBA_BLOCK].reshape(bsz, h, Q_CHUNK, MOBA_TOPK, MOBA_BLOCK).astype(v.dtype)
        p_o = p[..., MOBA_TOPK * MOBA_BLOCK:].astype(v.dtype)
        return (jnp.einsum('bhqnk,bhqnkd->bhqd', p_p, vg)
                + jnp.einsum('bhqk,bhkd->bhqd', p_o, vo))

    outs = lax.map(chunk, jnp.arange(sp // Q_CHUNK))
    out = outs.transpose(1, 2, 0, 3, 4).reshape(bsz, h, sp, dh)[:, :, :s]
    return out.transpose(0, 2, 1, 3).reshape(bsz, s, h * dh)

def hybrid_mixer(u, w_in, conv_w, conv_b, w_gate_a, b_gate_a, w_gate_x, b_gate_x,
                 lru_lambda, rel_bias, norm_lru_g, norm_attn_g, w_out):
    bsz, s, _ = u.shape
    proj = u @ w_in
    x_lru, y_lru, q, k, v = jnp.split(
        proj, [D_LRU, 2 * D_LRU, 2 * D_LRU + D_ATTN, 2 * D_LRU + 2 * D_ATTN], axis=-1)
    h = rg_lru(causal_depthwise_conv(x_lru, conv_w, conv_b),
               w_gate_a, b_gate_a, w_gate_x, b_gate_x, lru_lambda)
    lru_out = h * jax.nn.gelu(y_lru)
    attn_out = moba_attention(q.reshape(bsz, s, N_HEADS, HEAD_DIM),
                              k.reshape(bsz, s, N_HEADS, HEAD_DIM),
                              v.reshape(bsz, s, N_HEADS, HEAD_DIM), rel_bias)
    merged = jnp.concatenate([rmsnorm(lru_out, norm_lru_g), rmsnorm(attn_out, norm_attn_g)], axis=-1)
    return merged @ w_out

def hierarchical_moe(u, w_rg, b_rg, w_re, b_re, w1, w3, w2):
    bsz, s, d = u.shape
    nc = s // MOE_ROWS
    xt = u.reshape(bsz, nc, MOE_ROWS, d).transpose(1, 0, 2, 3).reshape(nc, bsz * MOE_ROWS, d)

    def body(xc):
        g_prob = jax.nn.softmax((xc @ w_rg + b_rg).astype(jnp.float32), axis=-1)
        g_top, g_idx = lax.top_k(g_prob, 1)
        e_logits = (xc @ w_re + b_re).astype(jnp.float32).reshape(-1, N_GROUPS, EXPERTS_PER_GROUP)
        e_in = jnp.take_along_axis(e_logits, g_idx[:, :, None], axis=1)[:, 0]
        e_top, e_loc = lax.top_k(jax.nn.softmax(e_in, axis=-1), EXPERT_TOPK)
        e_top = e_top / jnp.sum(e_top, axis=-1, keepdims=True)
        weights = g_top * e_top
        e_glob = g_idx * EXPERTS_PER_GROUP + e_loc
        gate = jnp.sum(jax.nn.one_hot(e_glob, N_EXPERTS, dtype=jnp.float32) * weights[..., None], axis=1)
        hdn = jax.nn.silu(jnp.einsum('td,edf->tef', xc, w1)) * jnp.einsum('td,edf->tef', xc, w3)
        return jnp.einsum('tef,efd->td', hdn * gate[:, :, None].astype(hdn.dtype), w2)

    ys = lax.map(body, xt)
    return ys.reshape(nc, bsz, MOE_ROWS, d).transpose(1, 0, 2, 3).reshape(bsz, s, d)

def first_inputs(seed: int = 0) -> dict:
    key = jax.random.key(seed)
    ks = jax.random.split(key, 28)
    f32 = jnp.float32
    L = DEPTH

    def nrm(k, shape, scale):
        return jax.random.normal(k, shape, f32) * scale

    a_c = jax.random.uniform(ks[11], (L, D_LRU), f32, 0.9, 0.999)
    a_base = a_c ** (1.0 / LRU_C)
    return {
        'x': nrm(ks[0], (BATCH, SEQ, D_MODEL), 1.0),
        'c': nrm(ks[1], (BATCH, D_MODEL), 1.0),
        'w_ada': nrm(ks[2], (L, D_MODEL, N_MOD * D_MODEL), 0.5 * D_MODEL ** -0.5),
        'b_ada': nrm(ks[3], (L, N_MOD * D_MODEL), 0.02),
        'w_in': nrm(ks[4], (L, D_MODEL, D_IN_PROJ), D_MODEL ** -0.5),
        'conv_w': nrm(ks[5], (L, CONV_WIDTH, D_LRU), CONV_WIDTH ** -0.5),
        'conv_b': nrm(ks[6], (L, D_LRU), 0.02),
        'w_gate_a': nrm(ks[7], (L, N_LRU_BLOCKS, LRU_BLOCK, LRU_BLOCK), LRU_BLOCK ** -0.5),
        'b_gate_a': nrm(ks[8], (L, N_LRU_BLOCKS, LRU_BLOCK), 0.02),
        'w_gate_x': nrm(ks[9], (L, N_LRU_BLOCKS, LRU_BLOCK, LRU_BLOCK), LRU_BLOCK ** -0.5),
        'b_gate_x': nrm(ks[10], (L, N_LRU_BLOCKS, LRU_BLOCK), 0.02),
        'lru_lambda': jnp.log(a_base) - jnp.log1p(-a_base),
        'rel_bias': nrm(ks[12], (REL_BUCKETS, N_HEADS), 0.5),
        'norm_lru_g': 1.0 + nrm(ks[13], (L, D_LRU), 0.05),
        'norm_attn_g': 1.0 + nrm(ks[14], (L, D_ATTN), 0.05),
        'w_out': nrm(ks[15], (L, D_MIX, D_MODEL), DEEPNORM_BETA * D_MIX ** -0.5),
        'ln1_g': 1.0 + nrm(ks[16], (L, D_MODEL), 0.05),
        'ln1_b': nrm(ks[17], (L, D_MODEL), 0.02),
        'w_router_group': nrm(ks[18], (L, D_MODEL, N_GROUPS), D_MODEL ** -0.5),
        'b_router_group': nrm(ks[19], (L, N_GROUPS), 0.01),
        'w_router_expert': nrm(ks[20], (L, D_MODEL, N_EXPERTS), D_MODEL ** -0.5),
        'b_router_expert': nrm(ks[21], (L, N_EXPERTS), 0.01),
        'w1': nrm(ks[22], (L, N_EXPERTS, D_MODEL, D_EXPERT), D_MODEL ** -0.5),
        'w3': nrm(ks[23], (L, N_EXPERTS, D_MODEL, D_EXPERT), D_MODEL ** -0.5),
        'w2': nrm(ks[24], (L, N_EXPERTS, D_EXPERT, D_MODEL), DEEPNORM_BETA * D_EXPERT ** -0.5),
        'ln2_g': 1.0 + nrm(ks[25], (L, D_MODEL), 0.05),
        'ln2_b': nrm(ks[26], (L, D_MODEL), 0.02),
    }

def first_block(x, c, w_ada, b_ada, w_in, conv_w, conv_b, w_gate_a, b_gate_a, w_gate_x, b_gate_x,
              lru_lambda, rel_bias, norm_lru_g, norm_attn_g, w_out, ln1_g, ln1_b,
              w_router_group, b_router_group, w_router_expert, b_router_expert,
              w1, w3, w2, ln2_g, ln2_b):
    bsz, _, d = x.shape
    silu_c = jax.nn.silu(c)
    for l in range(DEPTH):
        mod = (silu_c @ w_ada[l] + b_ada[l]).reshape(bsz, N_MOD, d)
        sh1, sc1, g1, sh2, sc2, g2 = [mod[:, j, None, :] for j in range(N_MOD)]
        u = modulate(x, sh1, sc1)
        mix = hybrid_mixer(u, w_in[l], conv_w[l], conv_b[l], w_gate_a[l], b_gate_a[l],
                           w_gate_x[l], b_gate_x[l], lru_lambda[l], rel_bias,
                           norm_lru_g[l], norm_attn_g[l], w_out[l])
        x = layernorm(DEEPNORM_ALPHA * x + g1 * mix, ln1_g[l], ln1_b[l])
        u2 = modulate(x, sh2, sc2)
        ffn = hierarchical_moe(u2, w_router_group[l], b_router_group[l], w_router_expert[l],
                               b_router_expert[l], w1[l], w3[l], w2[l])
        x = layernorm(DEEPNORM_ALPHA * x + g2 * ffn, ln2_g[l], ln2_b[l])
    return x


DEPTH_2 = 4

N_MIXERS = 3
N_SUB = 3
NORM_EPS = 1e-6
D_FF = 2816
MACARON_W = 0.5
N_A = (DEPTH_2 + 2) // 3
N_B = (DEPTH_2 + 1) // 3
N_C = DEPTH_2 // 3
N_A_VRES = max(N_A - 1, 0)

RW_HEAD = 64
RW_HEADS = D_MODEL // RW_HEAD
RW_DECAY_LORA = max(32, int(round(1.8 * D_MODEL ** 0.5 / 32)) * 32)
RW_AAA_LORA = max(32, int(round(1.8 * D_MODEL ** 0.5 / 32)) * 32)
RW_MV_LORA = max(32, int(round(1.3 * D_MODEL ** 0.5 / 32)) * 32)
RW_GATE_LORA = max(32, int(round(0.6 * D_MODEL ** 0.8 / 32)) * 32)
RW_GN_EPS = 64e-5

MB_D_INNER = 2 * D_MODEL
MB_HEADDIM = 64
MB_HEADS = MB_D_INNER // MB_HEADDIM
MB_GROUPS = 8
MB_STATE = 128
MB_CONV = 4
MB_CHUNK = 128
MB_CONV_DIM = MB_D_INNER + 2 * MB_GROUPS * MB_STATE
MB_IN_DIM = MB_D_INNER + MB_CONV_DIM + MB_HEADS

SW_HEAD_DIM = 64
SW_Q_HEADS = D_MODEL // SW_HEAD_DIM
SW_KV_HEADS = 4
SW_WINDOW = 128
SW_BLOCK = 128
NEG_INF = -1e30


def rms_norm(x, g, eps=NORM_EPS):
    xf = x.astype(jnp.float32)
    y = xf * lax.rsqrt(jnp.mean(xf * xf, axis=-1, keepdims=True) + eps)
    return (y * g.astype(jnp.float32)).astype(x.dtype)

def adaln(x, g, shift, scale):
    return rms_norm(x, g) * (1 + scale[:, None, :]) + shift[:, None, :]

def swiglu(h, w_in, w_out):
    a, b = jnp.split(h @ w_in, 2, axis=-1)
    return (jax.nn.silu(a) * b) @ w_out

def token_shift(h):
    return jnp.pad(h, ((0, 0), (1, 0), (0, 0)))[:, :-1]

def rwkv7_time_mix(h, mu, w_rkv, w_o, w0, w1, w2, a0, a1, a2, g1, g2,
                   k_k, k_a, r_k, ln_w, ln_b, v_first, vres):
    f32 = jnp.float32
    bsz, seq, d = h.shape
    H, N = RW_HEADS, RW_HEAD
    dx = token_shift(h) - h
    xr, xw, xk, xv, xa, xg = [h + dx * mu[j] for j in range(6)]
    r = xr @ w_rkv[0]
    k = xk @ w_rkv[1]
    v = xv @ w_rkv[2]
    w = -jax.nn.softplus(-(w0 + jnp.tanh(xw @ w1) @ w2)) - 0.5
    decay = jnp.exp(-jnp.exp(w.astype(f32)))
    a = jax.nn.sigmoid(a0 + (xa @ a1) @ a2)
    if vres is None:
        v_first = v
    else:
        v0, v1, v2 = vres
        v = v + (v_first - v) * jax.nn.sigmoid(v0 + (xv @ v1) @ v2)
    g = jax.nn.sigmoid(xg @ g1) @ g2

    def heads(t):
        return t.reshape(bsz, seq, H, N).astype(f32)

    kk = heads(k * k_k)
    kk = kk / jnp.maximum(jnp.sqrt(jnp.sum(kk * kk, axis=-1, keepdims=True)), 1e-12)
    k = k * (1 + (a - 1) * k_a)
    rh, kh, vh, wh, ah = heads(r), heads(k), heads(v), heads(decay), heads(a)

    def step(state, inp):
        r_t, w_t, k_t, v_t, kk_t, a_t = inp
        sa = jnp.einsum('bhvk,bhk->bhv', state, -kk_t)
        state = (state * w_t[:, :, None, :]
                 + sa[..., None] * (kk_t * a_t)[:, :, None, :]
                 + v_t[..., None] * k_t[:, :, None, :])
        return state, jnp.einsum('bhvk,bhk->bhv', state, r_t)

    def tm(t):
        return jnp.swapaxes(t, 0, 1)

    state0 = jnp.zeros((bsz, H, N, N), f32)
    _, y = lax.scan(step, state0, (tm(rh), tm(wh), tm(kh), tm(vh), tm(kk), tm(ah)))
    y = tm(y)
    mean = jnp.mean(y, axis=-1, keepdims=True)
    var = jnp.mean(jnp.square(y - mean), axis=-1, keepdims=True)
    y = ((y - mean) * lax.rsqrt(var + RW_GN_EPS)).reshape(bsz, seq, d) * ln_w + ln_b
    bonus = jnp.sum(rh * kh * r_k, axis=-1, keepdims=True) * vh
    out = ((y + bonus.reshape(bsz, seq, d)) * g).astype(h.dtype) @ w_o
    return out, v_first

def causal_dwconv(x, w, b):
    k_w, ch = w.shape
    out = lax.conv_general_dilated(x, w[:, None, :].astype(x.dtype), window_strides=(1,),
                                   padding=[(k_w - 1, 0)],
                                   dimension_numbers=('NWC', 'WIO', 'NWC'),
                                   feature_group_count=ch)
    return out + b

def ssd_chunked(x, dt, A, Bm, Cm):
    f32 = jnp.float32
    bsz, seq, H, P = x.shape
    G, N = Bm.shape[2], Bm.shape[3]
    hg = H // G
    L = MB_CHUNK
    nc = seq // L
    X = (x.astype(f32) * dt[..., None]).reshape(bsz, nc, L, G, hg, P)
    dA = (dt * A).reshape(bsz, nc, L, G, hg)
    Bc = Bm.astype(f32).reshape(bsz, nc, L, G, N)
    Cc = Cm.astype(f32).reshape(bsz, nc, L, G, N)
    X, dA, Bc, Cc = [jnp.moveaxis(t, 1, 0) for t in (X, dA, Bc, Cc)]
    mask = jnp.tril(jnp.ones((L, L), dtype=bool))[None, :, :, None, None]

    def step(state, inp):
        Xc, dAc, Bk, Ck = inp
        acum = jnp.cumsum(dAc, axis=1)
        seg = acum[:, :, None] - acum[:, None, :]
        lmat = jnp.exp(jnp.where(mask, seg, -jnp.inf))
        cb = jnp.einsum('blgn,bsgn->blsg', Ck, Bk)
        y_diag = jnp.einsum('blsgh,bsghp->blghp', cb[..., None] * lmat, Xc)
        y_off = jnp.einsum('blgn,bghpn->blghp', Ck, state) * jnp.exp(acum)[..., None]
        decay_end = jnp.exp(acum[:, -1:] - acum)
        new_state = (state * jnp.exp(acum[:, -1])[..., None, None]
                     + jnp.einsum('blgn,blghp->bghpn', Bk, Xc * decay_end[..., None]))
        return new_state, y_diag + y_off

    state0 = jnp.zeros((bsz, G, hg, P, N), f32)
    _, y = lax.scan(step, state0, (X, dA, Bc, Cc))
    return jnp.moveaxis(y, 0, 1).reshape(bsz, seq, H, P)

def mamba2_ssd_mix(h, w_in, conv_w, conv_b, dt_bias, A_log, D_skip, norm_g, w_out):
    f32 = jnp.float32
    bsz, seq, _ = h.shape
    zxbcdt = h @ w_in
    z, xbc, dt = jnp.split(zxbcdt, [MB_D_INNER, MB_D_INNER + MB_CONV_DIM], axis=-1)
    xbc = jax.nn.silu(causal_dwconv(xbc, conv_w, conv_b))
    xs, Bm, Cm = jnp.split(xbc, [MB_D_INNER, MB_D_INNER + MB_GROUPS * MB_STATE], axis=-1)
    dt = jax.nn.softplus((dt + dt_bias).astype(f32))
    A = -jnp.exp(A_log.astype(f32))
    xs = xs.reshape(bsz, seq, MB_HEADS, MB_HEADDIM)
    y = ssd_chunked(xs, dt, A,
                    Bm.reshape(bsz, seq, MB_GROUPS, MB_STATE),
                    Cm.reshape(bsz, seq, MB_GROUPS, MB_STATE))
    y = y + xs.astype(f32) * D_skip.astype(f32)[:, None]
    y = y.reshape(bsz, seq, MB_D_INNER) * jax.nn.silu(z.astype(f32))
    y = rms_norm(y.reshape(bsz, seq, MB_GROUPS, -1), norm_g.reshape(MB_GROUPS, -1))
    return y.reshape(bsz, seq, MB_D_INNER).astype(h.dtype) @ w_out

def swa_sink_attention(h, w_qkv, q_norm, k_norm, sinks, w_o):
    f32 = jnp.float32
    bsz, seq, _ = h.shape
    Hq, Hk, Dh, T = SW_Q_HEADS, SW_KV_HEADS, SW_HEAD_DIM, SW_BLOCK
    G = Hq // Hk
    nb = seq // T
    q, k, v = jnp.split(h @ w_qkv, [Hq * Dh, (Hq + Hk) * Dh], axis=-1)
    q = rms_norm(q.reshape(bsz, seq, Hq, Dh), q_norm).reshape(bsz, nb, T, Hk, G, Dh)
    k = rms_norm(k.reshape(bsz, seq, Hk, Dh), k_norm).reshape(bsz, nb, T, Hk, Dh)
    v = v.reshape(bsz, nb, T, Hk, Dh)

    def with_prev(t):
        prev = jnp.pad(t, ((0, 0), (1, 0), (0, 0), (0, 0), (0, 0)))[:, :-1]
        return jnp.concatenate([prev, t], axis=2)

    kb, vb = with_prev(k), with_prev(v)
    qi = jnp.arange(T)[:, None]
    si = jnp.arange(2 * T)[None, :]
    rel = qi + T - si
    band = (rel >= 0) & (rel < SW_WINDOW)
    mask = band[None] & ((jnp.arange(nb)[:, None, None] > 0) | (si >= T)[None])
    scale = Dh ** -0.5
    sink = sinks.astype(f32).reshape(Hk, G)[None, :, :, None, None]

    def block(args):
        qb, kbb, vbb, mb = args
        s = jnp.einsum('bqkgd,bskd->bkgqs', qb, kbb).astype(f32) * scale
        s = jnp.where(mb, s, NEG_INF)
        m = jnp.maximum(jnp.max(s, axis=-1, keepdims=True), sink)
        p = jnp.exp(s - m)
        denom = jnp.sum(p, axis=-1, keepdims=True) + jnp.exp(sink - m)
        return jnp.einsum('bkgqs,bskd->bqkgd', (p / denom).astype(vbb.dtype), vbb)

    o = lax.map(block, (jnp.moveaxis(q, 1, 0), jnp.moveaxis(kb, 1, 0),
                        jnp.moveaxis(vb, 1, 0), mask))
    o = jnp.moveaxis(o, 0, 1).reshape(bsz, seq, Hq * Dh)
    return o @ w_o

def second_inputs(seed: int = 0) -> dict:
    key = jax.random.key(seed)
    ks = iter(jax.random.split(key, 64))

    def nrm(shape, scale=1.0):
        return scale * jax.random.normal(next(ks), shape, jnp.float32)

    def unif(shape, lo, hi):
        return jax.random.uniform(next(ks), shape, jnp.float32, lo, hi)

    D = D_MODEL
    dt0 = jnp.exp(unif((N_B, MB_HEADS), math.log(1e-3), math.log(1e-1)))
    return {
        'x': nrm((BATCH, SEQ, D)),
        'c': nrm((BATCH, D)),
        'ada_w': nrm((DEPTH_2, D, N_SUB * 3 * D), 0.5 * D ** -0.5),
        'ada_b': nrm((DEPTH_2, N_SUB * 3 * D), 0.02),
        'norm_g': 1.0 + nrm((DEPTH_2, N_SUB, D), 0.05),
        'ffn_w_in': nrm((DEPTH_2, 2, D, 2 * D_FF), D ** -0.5),
        'ffn_w_out': nrm((DEPTH_2, 2, D_FF, D), D_FF ** -0.5),
        'rw_mu': unif((N_A, 6, D), 0.0, 1.0),
        'rw_w_rkv': nrm((N_A, 3, D, D), D ** -0.5),
        'rw_w_o': nrm((N_A, D, D), D ** -0.5),
        'rw_w0': unif((N_A, D), -6.5, -1.5),
        'rw_w1': nrm((N_A, D, RW_DECAY_LORA), D ** -0.5),
        'rw_w2': nrm((N_A, RW_DECAY_LORA, D), 0.1 * RW_DECAY_LORA ** -0.5),
        'rw_a0': nrm((N_A, D), 0.1),
        'rw_a1': nrm((N_A, D, RW_AAA_LORA), D ** -0.5),
        'rw_a2': nrm((N_A, RW_AAA_LORA, D), 0.5 * RW_AAA_LORA ** -0.5),
        'rw_g1': nrm((N_A, D, RW_GATE_LORA), D ** -0.5),
        'rw_g2': nrm((N_A, RW_GATE_LORA, D), RW_GATE_LORA ** -0.5),
        'rw_k_k': 0.85 + nrm((N_A, D), 0.05),
        'rw_k_a': 1.0 + nrm((N_A, D), 0.05),
        'rw_r_k': nrm((N_A, RW_HEADS, RW_HEAD), 0.1),
        'rw_ln_w': 1.0 + nrm((N_A, D), 0.05),
        'rw_ln_b': nrm((N_A, D), 0.02),
        'rw_v0': 1.0 + nrm((N_A_VRES, D), 0.1),
        'rw_v1': nrm((N_A_VRES, D, RW_MV_LORA), D ** -0.5),
        'rw_v2': nrm((N_A_VRES, RW_MV_LORA, D), 0.5 * RW_MV_LORA ** -0.5),
        'mb_w_in': nrm((N_B, D, MB_IN_DIM), D ** -0.5),
        'mb_conv_w': nrm((N_B, MB_CONV, MB_CONV_DIM), 0.5),
        'mb_conv_b': nrm((N_B, MB_CONV_DIM), 0.02),
        'mb_dt_bias': dt0 + jnp.log(-jnp.expm1(-dt0)),
        'mb_A_log': jnp.log(unif((N_B, MB_HEADS), 1.0, 16.0)),
        'mb_D': 1.0 + nrm((N_B, MB_HEADS), 0.1),
        'mb_norm_g': 1.0 + nrm((N_B, MB_D_INNER), 0.05),
        'mb_w_out': nrm((N_B, MB_D_INNER, D), MB_D_INNER ** -0.5),
        'sw_w_qkv': nrm((N_C, D, (SW_Q_HEADS + 2 * SW_KV_HEADS) * SW_HEAD_DIM), D ** -0.5),
        'sw_q_norm': 1.0 + nrm((N_C, SW_HEAD_DIM), 0.05),
        'sw_k_norm': 1.0 + nrm((N_C, SW_HEAD_DIM), 0.05),
        'sw_sinks': nrm((N_C, SW_Q_HEADS), 0.5),
        'sw_w_o': nrm((N_C, SW_Q_HEADS * SW_HEAD_DIM, D), (SW_Q_HEADS * SW_HEAD_DIM) ** -0.5),
    }

def second_block(x, c, ada_w, ada_b, norm_g, ffn_w_in, ffn_w_out,
              rw_mu, rw_w_rkv, rw_w_o, rw_w0, rw_w1, rw_w2, rw_a0, rw_a1, rw_a2,
              rw_g1, rw_g2, rw_k_k, rw_k_a, rw_r_k, rw_ln_w, rw_ln_b,
              rw_v0, rw_v1, rw_v2,
              mb_w_in, mb_conv_w, mb_conv_b, mb_dt_bias, mb_A_log, mb_D, mb_norm_g, mb_w_out,
              sw_w_qkv, sw_q_norm, sw_k_norm, sw_sinks, sw_w_o):
    bsz, _, d = x.shape
    c_act = jax.nn.silu(c)
    v_first = None
    for i in range(DEPTH_2):
        mod = (c_act @ ada_w[i] + ada_b[i]).reshape(bsz, N_SUB, 3, d)
        shift, scale, gate = mod[:, :, 0], mod[:, :, 1], mod[:, :, 2]

        h = adaln(x, norm_g[i, 0], shift[:, 0], scale[:, 0])
        x = x + MACARON_W * gate[:, 0, None] * swiglu(h, ffn_w_in[i, 0], ffn_w_out[i, 0])

        h = adaln(x, norm_g[i, 1], shift[:, 1], scale[:, 1])
        kind, j = i % N_MIXERS, i // N_MIXERS
        if kind == 0:
            vres = None if v_first is None else (rw_v0[j - 1], rw_v1[j - 1], rw_v2[j - 1])
            y, v_first = rwkv7_time_mix(h, rw_mu[j], rw_w_rkv[j], rw_w_o[j], rw_w0[j], rw_w1[j],
                                        rw_w2[j], rw_a0[j], rw_a1[j], rw_a2[j], rw_g1[j],
                                        rw_g2[j], rw_k_k[j], rw_k_a[j], rw_r_k[j],
                                        rw_ln_w[j], rw_ln_b[j], v_first, vres)
        elif kind == 1:
            y = mamba2_ssd_mix(h, mb_w_in[j], mb_conv_w[j], mb_conv_b[j], mb_dt_bias[j],
                               mb_A_log[j], mb_D[j], mb_norm_g[j], mb_w_out[j])
        else:
            y = swa_sink_attention(h, sw_w_qkv[j], sw_q_norm[j], sw_k_norm[j],
                                   sw_sinks[j], sw_w_o[j])
        x = x + gate[:, 1, None] * y

        h = adaln(x, norm_g[i, 2], shift[:, 2], scale[:, 2])
        x = x + MACARON_W * gate[:, 2, None] * swiglu(h, ffn_w_in[i, 1], ffn_w_out[i, 1])
    return x


def setup_inputs(seed=0):
    out = dict(first_inputs(seed))
    for name, value in second_inputs(seed + 1).items():
        if name != "x":
            out[name + "_2"] = value
    return out


def reference(
    x, c, w_ada, b_ada, w_in, conv_w, conv_b, w_gate_a, b_gate_a, w_gate_x, b_gate_x,
    lru_lambda, rel_bias, norm_lru_g, norm_attn_g, w_out, ln1_g, ln1_b, w_router_group,
    b_router_group, w_router_expert, b_router_expert, w1, w3, w2, ln2_g, ln2_b, c_2, ada_w_2,
    ada_b_2, norm_g_2, ffn_w_in_2, ffn_w_out_2, rw_mu_2, rw_w_rkv_2, rw_w_o_2, rw_w0_2, rw_w1_2,
    rw_w2_2, rw_a0_2, rw_a1_2, rw_a2_2, rw_g1_2, rw_g2_2, rw_k_k_2, rw_k_a_2, rw_r_k_2,
    rw_ln_w_2, rw_ln_b_2, rw_v0_2, rw_v1_2, rw_v2_2, mb_w_in_2, mb_conv_w_2, mb_conv_b_2,
    mb_dt_bias_2, mb_A_log_2, mb_D_2, mb_norm_g_2, mb_w_out_2, sw_w_qkv_2, sw_q_norm_2,
    sw_k_norm_2, sw_sinks_2, sw_w_o_2,
):
    x = first_block(
        x, c, w_ada, b_ada, w_in, conv_w, conv_b, w_gate_a, b_gate_a, w_gate_x, b_gate_x,
        lru_lambda, rel_bias, norm_lru_g, norm_attn_g, w_out, ln1_g, ln1_b, w_router_group,
        b_router_group, w_router_expert, b_router_expert, w1, w3, w2, ln2_g, ln2_b,
    )
    return second_block(
        x, c_2, ada_w_2, ada_b_2, norm_g_2, ffn_w_in_2, ffn_w_out_2, rw_mu_2, rw_w_rkv_2,
        rw_w_o_2, rw_w0_2, rw_w1_2, rw_w2_2, rw_a0_2, rw_a1_2, rw_a2_2, rw_g1_2, rw_g2_2,
        rw_k_k_2, rw_k_a_2, rw_r_k_2, rw_ln_w_2, rw_ln_b_2, rw_v0_2, rw_v1_2, rw_v2_2,
        mb_w_in_2, mb_conv_w_2, mb_conv_b_2, mb_dt_bias_2, mb_A_log_2, mb_D_2, mb_norm_g_2,
        mb_w_out_2, sw_w_qkv_2, sw_q_norm_2, sw_k_norm_2, sw_sinks_2, sw_w_o_2,
    )


_drawn_inputs = setup_inputs


def setup_inputs(seed=0):
    import zlib

    import numpy as np

    out = dict(_drawn_inputs(seed))
    spreads = {}
    factors = {'b_ada': 3.141,
     'conv_b': 7.651,
     'w_gate_a': 2.778,
     'b_gate_a': 8.0,
     'b_gate_x': 8.0,
     'norm_lru_g': 8.0,
     'norm_attn_g': 8.0,
     'b_router_group': 8.0,
     'b_router_expert': 26.595,
     'rw_w1_2': 8.0,
     'rw_w2_2': 8.0,
     'rw_a0_2': 6.151,
     'rw_k_k_2': 3.685,
     'rw_k_a_2': 3.339,
     'rw_ln_w_2': 5.434,
     'rw_ln_b_2': 8.0,
     'rw_v0_2': 64.0,
     'rw_v1_2': 21.52,
     'mb_conv_b_2': 7.457,
     'mb_D_2': 3.614,
     'mb_norm_g_2': 4.056,
     'sw_q_norm_2': 8.0,
     'sw_k_norm_2': 8.0,
     'sw_sinks_2': 64.0,
     'rw_v2_2': 8.0}
    for name, (base, spread) in spreads.items():
        noise = np.random.default_rng([zlib.crc32(name.encode()), seed]).standard_normal(out[name].shape)
        drawn = base * np.exp(spread * noise) if base else spread * noise
        out[name] = jnp.asarray(drawn.astype(out[name].dtype))
    for name, factor in factors.items():
        out[name] = (out[name] * factor).astype(out[name].dtype)
    return out
```

```python
from contextlib import ExitStack

import numpy as np

import concourse.bass as bass
from concourse import mybir

P = 128
SEQ = 256
D = 1024
KC = D // P
D_LRU, D_ATTN = 512, 512
HEADS_A, HEAD = 8, 64
REL_BUCKETS, REL_MAX_DIST = 32, 128
N_GROUPS, PER_GROUP = 4, 8
N_EXPERTS = N_GROUPS * PER_GROUP
D_EXPERT = 256
DEPTH_2, N_SUB = 4, 3
D_FF = 2816
GLU = 256
LN_EPS, NORM_EPS, GN_EPS = 1e-5, 1e-6, 64e-5
ALPHA = 2.0 ** 0.25
RW_HEADS = D // HEAD
MB_INNER, MB_GROUPS, MB_STATE, MB_HEADS = 2 * D, 8, 128, 32
MB_CONV_DIM = MB_INNER + 2 * MB_GROUPS * MB_STATE
SW_Q, SW_KV = 16, 4
NEG = -1e30
SLOTS, UNIT = 4, 6144
LEVELS = 7

F32 = mybir.dt.float32
ALU = mybir.AluOpType
ACT = mybir.ActivationFunctionType
AX = mybir.AxisListType.X



def columns_of_blocks(w, n=P):
    k, cols = w.shape
    kc = k // P
    out = []
    for c in range(0, cols, n):
        m = min(n, cols - c)
        out.append(w[:, c:c + m].reshape(kc, P, m).transpose(1, 0, 2).reshape(P, kc * m))
    return out


def rows_padded(w):
    out = np.zeros((P, w.shape[1]), w.dtype)
    out[:w.shape[0]] = w
    return out


def glu_unit(wa, wb, wo):
    down = wo.reshape(2, P, D).transpose(1, 0, 2).reshape(P, 2 * D)
    return np.concatenate(columns_of_blocks(wa) + columns_of_blocks(wb) + [down], axis=1)


def weight_plan():
    plan = []

    def blocks(name, k, cols):
        for j in range(0, cols, P):
            plan.append(((name, j // P), k // P * min(P, cols - j)))

    blocks("w_in", D, 2 * D_LRU + 3 * D_ATTN)
    plan += [(("gate_a", 0), D_LRU), (("gate_x", 0), D_LRU)]
    blocks("w_out", D, D)
    plan.append((("router", 0), KC * (N_GROUPS + N_EXPERTS)))
    plan.append(("unit", 0))
    for e in range(N_EXPERTS):
        plan.append((("moe", e), UNIT))
    for i in range(DEPTH_2):
        for j in range(D_FF // GLU):
            plan.append(((f"ffn{i}0", j), UNIT))
        if i % 3 == 0:
            n = i // 3
            blocks(f"r{n}", D, D)
            blocks(f"k{n}", D, D)
            blocks(f"v{n}", D, D)
            if n:
                blocks(f"v1{n}", D, 32)
                plan.append(((f"v2{n}", 0), D))
            blocks(f"w1{n}", D, 64)
            plan.append(((f"w2{n}", 0), D))
            blocks(f"a1{n}", D, 64)
            plan.append(((f"a2{n}", 0), D))
            blocks(f"g1{n}", D, 160)
            plan.append(((f"g2{n}", 0), D))
            plan.append(((f"g2{n}", 1), D))
            blocks(f"o{n}", D, D)
        elif i % 3 == 1:
            blocks("mb_in", D, 2 * MB_INNER + 2 * MB_GROUPS * MB_STATE + MB_HEADS)
            blocks("mb_out", MB_INNER, D)
        else:
            blocks("sw_qkv", D, (SW_Q + 2 * SW_KV) * HEAD)
            blocks("sw_o", D, D)
        plan.append(("unit", 0))
        for j in range(D_FF // GLU):
            plan.append(((f"ffn{i}1", j), UNIT))
    return plan


def place_weights(plan=None):
    place, fill, last = {}, [], {}
    full = True
    for key, n in plan or weight_plan():
        if key == "unit":
            full = True
            continue
        if full or fill[-1] + n > UNIT:
            fill.append(0)
            full = False
        place[key] = (len(fill) - 1, fill[-1], n)
        last[len(fill) - 1] = key
        fill[-1] += n
    return {k: (*v, last[v[0]] == k) for k, v in place.items()}, fill


def weight_arrays(inp):
    out = {}

    def blocks(name, w):
        for j, a in enumerate(columns_of_blocks(w)):
            out[(name, j)] = a

    blocks("w_in", inp["w_in"][0])
    blocks("w_out", inp["w_out"][0])
    for key in ("gate_a", "gate_x"):
        w = np.zeros((P, D_LRU // P, P), np.float32)
        for b in range(D_LRU // HEAD):
            rows = slice(HEAD * (b % 2), HEAD * (b % 2) + HEAD)
            w[rows, b // 2, rows] = inp["w_" + key][0, b]
        out[(key, 0)] = w.reshape(P, -1)
    router = np.concatenate([inp["w_router_group"][0], inp["w_router_expert"][0]], axis=1)
    out[("router", 0)] = columns_of_blocks(router)[0]
    for e in range(N_EXPERTS):
        out[("moe", e)] = glu_unit(inp["w1"][0, e], inp["w3"][0, e], inp["w2"][0, e])
    for i in range(DEPTH_2):
        for s in range(2):
            wi, wo = inp["ffn_w_in_2"][i, s], inp["ffn_w_out_2"][i, s]
            for j in range(D_FF // GLU):
                a = slice(j * GLU, (j + 1) * GLU)
                b = slice(D_FF + j * GLU, D_FF + (j + 1) * GLU)
                out[(f"ffn{i}{s}", j)] = glu_unit(wi[:, a], wi[:, b], wo[a])
    for n in range(2):
        for j, name in enumerate("rkv"):
            blocks(f"{name}{n}", inp["rw_w_rkv_2"][n, j])
        blocks(f"o{n}", inp["rw_w_o_2"][n])
        for name, up, down in (("w", "rw_w1_2", "rw_w2_2"), ("a", "rw_a1_2", "rw_a2_2"), ("g", "rw_g1_2", "rw_g2_2")):
            blocks(f"{name}1{n}", inp[up][n])
            for j in range(0, inp[down].shape[1], P):
                out[(f"{name}2{n}", j // P)] = rows_padded(inp[down][n, j:j + P])
    blocks("v11", inp["rw_v1_2"][0])
    out[("v21", 0)] = rows_padded(inp["rw_v2_2"][0])
    blocks("mb_in", inp["mb_w_in_2"][0])
    blocks("mb_out", inp["mb_w_out_2"][0])
    blocks("sw_qkv", inp["sw_w_qkv_2"][0])
    blocks("sw_o", inp["sw_w_o_2"][0])
    return out


def ada_array(inp):
    out = [inp["w_ada"][0]] + [inp["ada_w_2"][i] for i in range(DEPTH_2)]
    return np.concatenate([w.reshape(2, 4, P, -1, D).transpose(3, 0, 2, 1, 4).reshape(-1, P, 4 * D) for w in out])


def column_plan():
    sizes = [("c", KC), ("b_ada", 48), ("conv_w", 16), ("conv_b", 4), ("b_gate_a", 4), ("b_gate_x", 4), ("lam", 4),
             ("norm_lru_g", 4), ("norm_attn_g", 4), ("ln1_g", KC), ("ln1_b", KC), ("ln2_g", KC), ("ln2_b", KC),
             ("c_2", KC)]
    for i in range(DEPTH_2):
        sizes += [(f"ada_b{i}", 9 * KC), (f"norm_g{i}", N_SUB * KC)]
    for n in range(2):
        sizes += [(f"mu{n}", 6 * KC)] + [(f"{v}{n}", KC) for v in ("w0", "a0", "v0", "k_k", "k_a", "r_k", "ln_w", "ln_b")]
    sizes += [("mb_conv_w", 4 * 32), ("mb_conv_b", 32), ("mb_dt_bias", 1), ("mb_A_log", 1), ("mb_D", 16),
              ("mb_norm_g", 16), ("q_norm", 1), ("k_norm", 1), ("sinks", SW_Q),
              ("router_b", N_GROUPS + N_EXPERTS)]
    place, at = {}, 0
    for name, n in sizes:
        place[name] = (at, n)
        at += n
    return place, at


def column_array(inp):
    place, total = column_plan()
    out = np.zeros((P, total), np.float32)

    def put(name, v):
        at, n = place[name]
        v = np.asarray(v)
        if v.size == n * P:
            out[:, at:at + n] = v.reshape(n, P).T
        else:
            out[:v.size, at] = v.reshape(-1)

    for name in ("c", "c_2"):
        put(name, inp[name])
    for name in ("b_ada", "conv_w", "conv_b", "b_gate_a", "b_gate_x", "norm_lru_g", "norm_attn_g", "ln1_g", "ln1_b",
                 "ln2_g", "ln2_b"):
        put(name, inp[name][0])
    put("lam", inp["lru_lambda"][0])
    for i in range(DEPTH_2):
        put(f"ada_b{i}", inp["ada_b_2"][i])
        put(f"norm_g{i}", inp["norm_g_2"][i])
    for n in range(2):
        put(f"mu{n}", inp["rw_mu_2"][n])
        for v in ("w0", "a0", "k_k", "k_a", "r_k", "ln_w", "ln_b"):
            put(f"{v}{n}", inp[f"rw_{v}_2"][n])
    put("v01", inp["rw_v0_2"][0])
    put("mb_conv_w", inp["mb_conv_w_2"][0])
    put("mb_conv_b", inp["mb_conv_b_2"][0])
    put("mb_dt_bias", inp["mb_dt_bias_2"][0])
    put("mb_A_log", inp["mb_A_log_2"][0])
    put("mb_D", np.repeat(inp["mb_D_2"][0], HEAD))
    put("mb_norm_g", inp["mb_norm_g_2"][0])
    put("q_norm", np.tile(inp["sw_q_norm_2"][0], 2))
    put("k_norm", np.tile(inp["sw_k_norm_2"][0], 2))
    at, n = place["router_b"]
    out[0, at:at + n] = np.concatenate([inp["b_router_group"][0], inp["b_router_expert"][0]])
    put("sinks", np.repeat(inp["sw_sinks_2"][0], P))
    return out


def const_plan():
    sizes = [("ident", P), ("ones", P), ("heads", P), ("below", LEVELS * P), ("above", LEVELS * P),
             ("causal", 2 * P), ("lower", P), ("zeros", P),
             ("band", 2 * SEQ), ("buckets", 2 * SEQ)]
    place, at = {}, 0
    for name, n in sizes:
        place[name] = (at, n)
        at += n
    return place, at


def const_array():
    place, total = const_plan()
    out = np.zeros((P, total), np.float32)

    def put(name, v):
        at, n = place[name]
        out[:v.shape[0], at:at + v.shape[1]] = v

    i = np.arange(P)
    put("ident", np.eye(P))
    put("ones", np.ones((P, P)))
    put("heads", (i[:, None] // HEAD == i[None, :] // HEAD).astype(np.float32))
    below = []
    for level in range(LEVELS):
        half = 1 << level
        row, col = i[:, None], i[None, :]
        below.append((row // (2 * half) == col // (2 * half)) & (row % (2 * half) >= half) & (col % (2 * half) < half))
    put("below", np.concatenate(below, axis=1).astype(np.float32))
    put("above", np.concatenate([b.T for b in below], axis=1).astype(np.float32))
    put("causal", np.concatenate([i[:, None] < i[None, :], i[:, None] <= i[None, :]], axis=1).astype(np.float32))
    put("lower", (i[:, None] > i[None, :]).astype(np.float32))
    band = np.zeros((P, 2, SEQ), np.float32)
    for t in range(2):
        rel = (t * P + i)[:, None] - np.arange(SEQ)[None, :]
        band[:, t] = np.where((rel >= 0) & (rel < P), 0.0, NEG)
    put("band", band.reshape(P, -1))
    dist = (SEQ - 1) - np.arange(2 * SEQ)
    n = np.maximum(dist, 0)
    exact = REL_BUCKETS // 2
    far = np.log(np.maximum(n, 1).astype(np.float32) / np.float32(exact)).astype(np.float32)
    far = (far / np.float32(np.log(REL_MAX_DIST / exact)) * np.float32(REL_BUCKETS - exact)).astype(np.int32)
    bucket = np.where(n < exact, n, np.minimum(exact + far, REL_BUCKETS - 1))
    hot = np.zeros((REL_BUCKETS + 1, 2 * SEQ), np.float32)
    hot[bucket, np.arange(2 * SEQ)] = (dist >= 0)
    hot[REL_BUCKETS] = np.where(dist < 0, NEG, 0.0)
    put("buckets", hot)
    return out



class Event:

    def __init__(self, nc, name):
        self.sem = nc.semaphore(name).__enter__()
        self.before = 0
        self.made = 0

    def count(self, n):
        self.made += n
        return n

    def at(self, k):
        return self.before + k


class Core:

    def __init__(self, nc, stream, cols_dram, consts_dram, place, fill):
        self.nc, self.stream, self.place, self.fill = nc, stream, place, fill
        self.cols_dram, self.consts_dram = cols_dram, consts_dram
        sb = lambda name, shape: nc.alloc_sbuf_tensor(name, shape, F32)
        self.ring = sb("ring", [P, SLOTS, UNIT])
        self.x = sb("x_sb", [P, KC, SEQ])
        at = nc.sbuf_base
        self.bufs = sb("bufs", [P, 10, 2048])
        split = lambda name, buffer, shape: nc.alloc_sbuf_tensor_at(name, shape, mybir.dt.float32r, offset=at + 8192 * buffer)
        self.h_split = split("h_split", 0, [P, 2, 2, 2, SEQ])
        self.u_split = split("u_split", 1, [P, 2, KC, SEQ])
        self.w_split = split("w_split", 3, [P, 3, 2, D])
        self.consts = sb("consts_sb", [P, const_plan()[0]["band"][0]])
        self.cols = sb("cols_sb", [P, column_plan()[1]])
        self.mod = sb("mod", [P, 9 * KC])
        self.c_act = sb("c_act", [P, 2 * KC])
        self.gain = sb("gain", [P, KC])
        self.rstd = sb("rstd", [P, SEQ])
        self.small = sb("small", [P, 704])
        self.state = sb("state", [P, 2, 512])
        self.narrow = self.state[:, 0, :].rearrange("p (b t) -> p b t", b=2)
        self.psum = nc.alloc_psum_tensor("banks", [P, 8, 512], F32)
        self.names = {}
        self.loaded_units = 0
        self.loaded = [Event(nc, f"unit_loaded{s}") for s in range(SLOTS)]
        self.freed = Event(nc, "unit_freed")

    def buf(self, i, n=1):
        return self.bufs[:, i:i + n, :].rearrange("p b (c t) -> p (b c) t", t=SEQ)

    def const(self, name):
        at, n = const_plan()[0][name]
        return self.consts[:, at:at + n]

    def load_const(self, sync, name, dst):
        at, n = const_plan()[0][name]
        s = self.event("constant_loaded")
        sync.dma_start(dst, self.consts_dram[:, at:at + n]).then_inc(s.sem, s.count(16))
        sync.wait_ge(s.sem, s.made)

    def col(self, name):
        at, n = column_plan()[0][name]
        return self.cols[:, at:at + n]

    def event(self, name):
        if name not in self.names:
            self.names[name] = Event(self.nc, name)
        return self.names[name]

    def end_stage(self):
        for s in self.names.values():
            s.before = s.made


    def load_ahead(self, sync, upto_key, upto=0, after=None):
        if upto_key:
            upto = min(len(self.fill), self.place[upto_key][0] + SLOTS)
        for u in range(self.loaded_units, upto):
            if u >= SLOTS:
                sync.wait_ge(self.freed.sem, u - SLOTS + 1)
            n = self.fill[u]
            sync.dma_start(self.ring[:, u % SLOTS, 0:n], self.stream[u, :, 0:n])\
                .then_inc(self.loaded[u % SLOTS].sem, self.loaded[u % SLOTS].count(16))
            if after:
                after(u - SLOTS)
        self.loaded_units = max(self.loaded_units, upto)

    def weights(self, pe, key):
        unit, at, n, _ = self.place[key]
        pe.wait_ge(self.loaded[unit % SLOTS].sem, 16 * (unit // SLOTS + 1))
        return self.ring[:, unit % SLOTS, at:at + n]

    def used(self, pe, key, instruction, done=None):
        last_of_unit = self.place[key][3]
        if done:
            instruction.then_inc(done.sem, done.count(1))
            if last_of_unit:
                pe.wait_ge(done.sem, done.made)
                pe.nop().then_inc(self.freed.sem, self.freed.count(1))
        elif last_of_unit:
            instruction.then_inc(self.freed.sem, self.freed.count(1))

    def project(self, pe, key, rhs, out, done=None, kcs=KC, m=P):
        w = self.weights(pe, key).rearrange("p (k m) -> p k m", k=kcs)
        for k in range(kcs):
            last = pe.matmul(out, w[:, k, :], rhs(k), start=(k == 0), stop=(k == kcs - 1))
        self.used(pe, key, last, done)


def chain(core, eng, name):
    s = core.event(f"{name}_step")

    def link(instruction):
        instruction.then_inc(s.sem, s.count(1))
        eng.wait_ge(s.sem, s.made)
        return instruction
    return link


def setup_stage(core, x_in):
    with core.nc.Block() as block:
        @block.sync
        def _(sync):
            s = core.event("setup_loaded")
            sync.dma_start(core.consts[:], core.consts_dram[:, 0:const_plan()[0]["band"][0]]).then_inc(s.sem, s.count(16))
            sync.dma_start(core.cols[:], core.cols_dram).then_inc(s.sem, s.count(16))
            sync.dma_start(core.x[:], x_in.rearrange("(c p) t -> p c t", p=P)).then_inc(s.sem, s.count(16))
            sync.wait_ge(s.sem, s.at(48))
    core.end_stage()


def store_stage(core, out):
    with core.nc.Block() as block:
        @block.sync
        def _(sync):
            s = core.event("stored")
            sync.dma_start(out.rearrange("(c p) t -> p c t", p=P), core.x[:]).then_inc(s.sem, s.count(16))
            sync.wait_ge(s.sem, s.at(16))
    core.end_stage()


def ada_columns(core, pe, sums, n):
    for j in range(n):
        for half in range(2):
            at = j * P + half * HEAD
            last = pe.matmul(core.psum[half * HEAD:(half + 1) * HEAD, 0, j:j + 1], sums[:, at:at + HEAD],
                             core.const("ones")[:, 0:1], start=True, stop=True)
    return last


def ada_accumulate(core, dve, half, slot, sums, c_act, step):
    done = core.event("ada_step")
    for q in range(4):
        k, w = 4 * half + q, slot[:, q * D:(q + 1) * D]
        if k == 0:
            e = dve.tensor_scalar(sums, w, c_act[:, 0:1], None, ALU.mult)
        else:
            dve.wait_ge(done.sem, done.at(step + q))
            e = dve.scalar_tensor_tensor(sums, w, c_act[:, k:k + 1], sums, ALU.mult, ALU.add)
        e.then_inc(done.sem, 1)


def first_ada_stage(core):
    ranges = 6
    slots = [core.bufs[:, 2 * q:2 * q + 2, :].rearrange("p b n -> p (b n)") for q in range(3)]
    sums = core.bufs[:, 6:9, :].rearrange("p b n -> p (b n)")
    with core.nc.Block() as block:
        silu_ready, products, step = core.event("c_silu"), core.event("ada_products"), core.event("ada_step")
        loaded = [core.event(f"ada_first_loaded{q}") for q in range(3)]

        @block.sync
        def _(sync):
            for k in range(2 * ranges):
                if k >= 3:
                    sync.wait_ge(step.sem, step.at(4 * (k - 2)))
                sync.dma_start(slots[k % 3], core.ada[k, :, :]).then_inc(loaded[k % 3].sem, loaded[k % 3].count(16))
            core.load_ahead(sync, None, SLOTS)

        @block.scalar
        def _(act):
            act.activation(core.c_act[:, 0:KC], core.col("c"), ACT.Silu).then_inc(silu_ready.sem, silu_ready.count(1))
            act.activation(core.c_act[:, KC:], core.col("c_2"), ACT.Silu).then_inc(silu_ready.sem, silu_ready.count(1))

        @block.vector
        def _(dve):
            dve.wait_ge(silu_ready.sem, silu_ready.at(2))
            for k in range(2 * ranges):
                dve.wait_ge(loaded[k % 3].sem, loaded[k % 3].at(16 * (k // 3 + 1)))
                ada_accumulate(core, dve, k % 2, slots[k % 3], sums[:, (k // 2) * D:(k // 2 + 1) * D], core.c_act[:, 0:KC], 4 * k)
            dve.wait_ge(products.sem, products.at(1))
            dve.tensor_tensor(core.mod[:, 0:6 * KC], core.psum[:, 0, 0:6 * KC], core.col("b_ada"), ALU.add)

        @block.tensor
        def _(pe):
            pe.wait_ge(step.sem, step.at(8 * ranges))
            ada_columns(core, pe, sums, 6 * KC).then_inc(products.sem, products.count(1))

        step.made += 8 * ranges
    core.end_stage()


def ada_stage(core, i):
    n = 9
    sums = core.bufs[:, 0:5, :].rearrange("p b n -> p (b n)")[:, 0:n * D]
    with core.nc.Block() as block:
        products, read = core.event("ada_products"), core.event("ada_sums_read")

        @block.sync
        def _(sync):
            sync.dma_start(sums.rearrange("p (r n) -> p r n", r=n), core.ada_sums.rearrange("r p n -> p r n"))\
                .then_inc(read.sem, read.count(16))

        @block.tensor
        def _(pe):
            pe.wait_ge(read.sem, read.at(16))
            ada_columns(core, pe, sums, n * KC).then_inc(products.sem, products.count(1))

        @block.vector
        def _(dve):
            dve.wait_ge(products.sem, products.at(1))
            dve.tensor_tensor(core.mod[:, 0:n * KC], core.psum[:, 0, 0:n * KC], core.col(f"ada_b{i}"), ALU.add)
    core.end_stage()


def norm_stage(core, src, out, eps, gain, shift=None, center=False, n=KC, ones="ones", sub_g=1.0, pre=None, next_key=None):
    count = float(n * P)
    ones = core.const(ones)
    with core.nc.Block() as block:
        centered, squared, summed, meaned = (core.event(s) for s in ("centered", "squared", "square_sum", "mean_sum"))
        root, scaled = core.event("root"), core.event("scaled")
        squares = core.buf(9)

        @block.tensor
        def _(pe):
            if center:
                for c in range(n):
                    last = pe.matmul(core.psum[:, 0, 0:SEQ], ones, src[:, c, :], start=(c == 0), stop=(c == n - 1))
                last.then_inc(meaned.sem, meaned.count(1))
            for c in range(n):
                pe.wait_ge(squared.sem, squared.at(c + 1))
                last = pe.matmul(core.psum[:, 1, 0:SEQ], ones, squares[:, c, :], start=(c == 0), stop=(c == n - 1))
            last.then_inc(summed.sem, summed.count(1))

        @block.scalar
        def _(act):
            for c in range(n):
                if center:
                    act.wait_ge(centered.sem, centered.at(c + 1))
                act.activation(squares[:, c, :], (out if center else src)[:, c, :], ACT.Square)\
                    .then_inc(squared.sem, squared.count(1))
            act.wait_ge(scaled.sem, scaled.at(1))
            act.activation(core.rstd[:], core.rstd[:], ACT.Sqrt).then_inc(root.sem, root.count(1))
            if shift is not None:
                for c in range(n):
                    act.wait_ge(scaled.sem, scaled.at(2 + c))
                    act.activation(out[:, c, :], out[:, c, :], ACT.Identity, bias=shift[:, c:c + 1])

        @block.vector
        def _(dve):
            link = chain(core, dve, "dve")
            if pre:
                pre(dve, link)
            if center:
                dve.wait_ge(meaned.sem, meaned.at(1))
                for c in range(n):
                    dve.scalar_tensor_tensor(out[:, c, :], core.psum[:, 0, 0:SEQ], -1.0 / count, src[:, c, :],
                                                         ALU.mult, ALU.add)\
                        .then_inc(centered.sem, centered.count(1))
            dve.wait_ge(summed.sem, summed.at(1))
            dve.tensor_scalar(core.rstd[:], core.psum[:, 1, 0:SEQ], 1.0 / count, eps, ALU.mult, ALU.add)\
                .then_inc(scaled.sem, scaled.count(1))
            dve.wait_ge(root.sem, root.at(1))
            link(dve.reciprocal(core.rstd[:], core.rstd[:]))
            for c in range(n):
                if center:
                    dve.wait_ge(centered.sem, centered.at(c + 1))
                dve.scalar_tensor_tensor(out[:, c, :], (out if center else src)[:, c, :], gain[:, c:c + 1],
                                                   core.rstd[:], ALU.mult, ALU.mult)\
                    .then_inc(scaled.sem, scaled.count(1))
    core.end_stage()


def glu_stage(core, key, n, src, residual, gates=None, ada=None):
    nc = core.nc
    unit0 = core.place[(key, 0)][0]
    zeros, anything = core.const("zeros"), core.const("below")[:, 0:512]
    work = core.bufs[:, 8, :]
    silu_a = [work[:, q * 512:(q + 1) * 512].rearrange("p (f t) -> p f t", t=SEQ) for q in range(2)]
    h_full = work[:, 1024:1536].rearrange("p (f t) -> p f t", t=SEQ)
    gate_rows = [work[:, 1536 + q * SEQ:1536 + (q + 1) * SEQ] for q in range(2)]
    y = core.psum[:, 4:8, :].rearrange("p b (c t) -> p (b c) t", t=SEQ)
    u_split, w_split, h_split = core.u_split, core.w_split, core.h_split
    with nc.Block() as block:
        u_high, u_low, high, low, piece_used, act_done, gated, h_ready, h_high, h_low = (core.event(s) for s in (
            "u_high", "u_low", "w_high", "w_low", "piece_used", "glu_silu", "glu_gated", "glu_hidden", "h_high", "h_low"))
        gate_loaded = [core.event(f"gate_loaded{q}") for q in range(2)]
        step, ada_loaded = (core.event(s) for s in ("ada_step", "ada_loaded"))
        sums_free = [core.event(f"ada_sums_free{q}") for q in range(2)]
        layer, range0, ranges = ada or (0, 0, 0)
        half0 = 2 * (6 + 9 * layer + range0)
        ada_slot = core.bufs[:, 6:8, :].rearrange("p b n -> p (b n)")
        ada_sums = [core.bufs[:, 9, q * D:(q + 1) * D] for q in range(2)]
        turns = (n - 2) // 4
        ada_turns = min(turns, ranges // 2)
        rest = n - 2 - 4 * turns
        assert ranges - 2 * ada_turns in (0, 1) and (ranges == 2 * ada_turns or rest)

        def half(j, which):
            return core.psum[:, 2 * (j % 2) + which, :].rearrange("p (f t) -> p f t", t=SEQ)

        def in_turns(eng, unit):
            for first, last, with_ada in ((0, ada_turns, True), (ada_turns, turns, False)):
                if first < last:
                    with eng.Fori(first, last) as turn:
                        for j in range(4):
                            unit(2 + j, turn * 4 + (2 + j), (turn * 4 + j) if with_ada else None)
            for j in range(n - rest, n):
                unit(j, j, None)

        def up_piece(at, b):
            return at * 6 + (b - 2)

        def down_piece(at, f):
            return at * 6 + (f + 2)

        def piece(j, b):
            return core.ring[:, (unit0 + j) % SLOTS, b * D:(b + 1) * D]

        @block.sync
        def _(sync):
            stored = [0]

            def store(unit, upto=2 * ada_turns):
                while stored[0] < upto and unit >= unit0 + 3 + 2 * stored[0]:
                    q = stored[0]
                    sync.wait_ge(step.sem, step.at(8 * (q + 1)))
                    sync.dma_start(core.ada_sums[range0 + q, :, :], ada_sums[q % 2])\
                        .then_inc(sums_free[q % 2].sem, sums_free[q % 2].count(16))
                    stored[0] += 1

            if ranges:
                for free in sums_free:
                    sync.nop().then_inc(free.sem, free.count(16))
            core.load_ahead(sync, (key, n - 1), after=store)
            store(unit0 + 2 * ranges + 4, ranges)
            if ranges:
                for free in sums_free:
                    sync.wait_ge(free.sem, free.made)

        @block.tensor
        def _(pe):
            def three(out, w, x, start, stop):
                pe.matmul(out, w(0), x(0), start=start, stop=False, skip_group_check=True)
                pe.matmul(out, w(0), x(1), start=False, stop=False, skip_group_check=True)
                return pe.matmul(out, w(1), x(0), start=False, stop=stop, skip_group_check=True)

            def up_products(j, at, ada_half=None):
                if j >= 2:
                    pe.wait_ge(h_ready.sem, h_ready.at(at - 1))
                for b in range(4):
                    number = b if j == 0 else up_piece(at, b)
                    slot = b % 3 if j == 0 else (b + 1) % 3
                    pe.wait_ge(low.sem, low.at(number + 1))
                    for k in range(KC):
                        last = three(half(j, b // 2)[:, b % 2, :], lambda part: w_split[:, slot, part, k * P:(k + 1) * P],
                                     lambda part: u_split[:, part, k, :], start=(k == 0), stop=(k == KC - 1))
                    last.then_inc(piece_used.sem, 1)

            def down_products(j, at, last_unit=False):
                pe.wait_ge(h_low.sem, h_low.at(at))
                for f in range(2):
                    slot = (f + 1) % 3 if last_unit else (f + 2) % 3
                    number = 6 * n - 2 + f if last_unit else down_piece(at, f)
                    pe.wait_ge(low.sem, low.at(number + 1))
                    for c in range(KC):
                        last = three(y[:, c, :], lambda part: w_split[:, slot, part, c * P:(c + 1) * P],
                                     lambda part: h_split[:, j % 2, part, f, :], start=False, stop=(f == 1))
                    last.then_inc(piece_used.sem, 1)

            for b in range(4):
                pe.matmul(core.psum[:, 4 + b, :], zeros, anything, start=True, stop=True)
            pe.wait_ge(u_low.sem, u_low.at(1))
            up_products(0, 0)
            up_products(1, 1)
            down_products(0, 1)

            def turn(j, at, ada_half):
                up_products(j, at)
                down_products(j - 1, at)

            in_turns(pe, turn)
            down_products(n - 1, n, last_unit=True)
            piece_used.made += 6 * n

        @block.scalar
        def _(act):
            def high_part(j, b, number, slot):
                if isinstance(number, int) and number < 3:
                    pass
                else:
                    act.wait_ge(piece_used.sem, piece_used.at(number - 2))
                nc.scalar.activation(w_split[:, slot, 0, :], piece(j, b), ACT.Copy).then_inc(high.sem, 1)

            def loaded(j, at):
                act.wait_ge(core.loaded[(unit0 + j) % SLOTS].sem, 16 * ((unit0 + j) // SLOTS + 1) + (at - j) * (16 // SLOTS))

            def silu(j, at):
                act.wait_ge(piece_used.sem, piece_used.at(at * 6 - 4) if j else piece_used.at(4))
                nc.scalar.activation(silu_a[j % 2], half(j, 0), ACT.Silu).then_inc(act_done.sem, 1)

            def h_high_part(j, at):
                act.wait_ge(h_ready.sem, h_ready.at(at))
                if j >= 2:
                    act.wait_ge(piece_used.sem, piece_used.at(at * 6 - 8))
                nc.scalar.activation(h_split[:, j % 2, 0, :, :], h_full, ACT.Copy).then_inc(h_high.sem, 1)

            def unit(j, at, ada_half):
                loaded(j, at)
                high_part(j, 0, up_piece(at, 0), 1)
                silu(j - 1, at)
                high_part(j, 1, up_piece(at, 1), 2)
                h_high_part(j - 1, at)
                if ada_half is not None:
                    load_half(ada_half)
                high_part(j, 2, up_piece(at, 2), 0)
                high_part(j, 3, up_piece(at, 3), 1)
                high_part(j - 1, 4, down_piece(at, 0), 2)
                high_part(j - 1, 5, down_piece(at, 1), 0)

            def load_half(k):
                act.wait_ge(step.sem, step.at(k * 4))
                act.dma_start(ada_slot, core.ada[bass.ds(k + half0, 1), :, :].rearrange("a p n -> p (a n)"))\
                    .then_inc(ada_loaded.sem, 16)

            act.activation(u_split[:, 0, :, :], src, ACT.Copy).then_inc(u_high.sem, u_high.count(1))
            loaded(0, 0)
            for b in range(4):
                high_part(0, b, b, b % 3)
            unit(1, 1, None)
            in_turns(act, unit)
            silu(n - 1, n)
            h_high_part(n - 1, n)
            for f in range(2):
                high_part(n - 1, 4 + f, 6 * n - 2 + f, f + 1)
            if ranges % 2:
                load_half(2 * ranges - 2)
                load_half(2 * ranges - 1)
            high.made += 6 * n
            act_done.made += n
            h_high.made += n
            ada_loaded.made += 32 * ranges

        if gates is not None:
            @block.gpsimd
            def _(pool):
                def load(q, index):
                    row = gates[bass.ds(index, 1), :] if not isinstance(index, int) else gates[index:index + 1, :]
                    pool.dma_start(gate_rows[q], row.to_broadcast([P, SEQ])).then_inc(gate_loaded[q].sem, 16)

                def gate(q, pair):
                    pool.wait_ge(act_done.sem, act_done.at(pair * 2 + (q + 1)))
                    pool.wait_ge(gate_loaded[q].sem, gate_loaded[q].at(pair * 16 + 16))
                    nc.gpsimd.tensor_tensor(silu_a[q], silu_a[q], gate_rows[q].unsqueeze(1).to_broadcast([P, 2, SEQ]), ALU.mult)\
                        .then_inc(gated.sem, 1)

                load(0, 0)
                load(1, 1)
                with pool.Fori(0, n // 2 - 1) as pair:
                    for q in range(2):
                        gate(q, pair)
                        pool.wait_ge(gated.sem, gated.at(pair * 2 + (q + 1)))
                        load(q, pair * 2 + (q + 2))
                for q in range(2):
                    gate(q, n // 2 - 1)
                    gate_loaded[q].made += 8 * n
                gated.made += n

        @block.vector
        def _(dve):
            ready = act_done if gates is None else gated

            def low_part(j, b, number, slot):
                dve.wait_ge(high.sem, high.at(number + 1))
                e = nc.vector.tensor_tensor(w_split[:, slot, 1, :], piece(j, b), w_split[:, slot, 0, :].bitcast(F32), ALU.subtract)
                e.then_inc(low.sem, 1)

            def product(j, at):
                dve.wait_ge(ready.sem, ready.at(at))
                nc.vector.tensor_tensor(h_full, silu_a[j % 2], half(j, 1), ALU.mult).then_inc(h_ready.sem, 1)

            def h_low_part(j, at):
                dve.wait_ge(h_high.sem, h_high.at(at))
                nc.vector.tensor_tensor(h_split[:, j % 2, 1, :, :], h_full, h_split[:, j % 2, 0, :, :].bitcast(F32), ALU.subtract)\
                    .then_inc(h_low.sem, 1)

            def freed(at):
                dve.wait_ge(low.sem, low.at(at))
                dve.nop().then_inc(core.freed.sem, 1)

            def sum_half(j, k):
                dve.wait_ge(ada_loaded.sem, ada_loaded.at(k * 16 + 16))
                if j % 2 == 0:
                    free = sums_free[(j // 2) % 2]
                    dve.wait_ge(free.sem, free.at(k * 4 + (16 - 4 * j)))
                ada_accumulate(core, dve, j % 2, ada_slot, ada_sums[(j // 2) % 2], core.c_act[:, KC:], k * 4)

            def unit(j, at, ada_half):
                low_part(j, 0, up_piece(at, 0), 1)
                product(j - 1, at)
                low_part(j, 1, up_piece(at, 1), 2)
                h_low_part(j - 1, at)
                low_part(j, 2, up_piece(at, 2), 0)
                low_part(j, 3, up_piece(at, 3), 1)
                low_part(j - 1, 4, down_piece(at, 0), 2)
                low_part(j - 1, 5, down_piece(at, 1), 0)
                freed(down_piece(at, 1) + 1)
                if ada_half is not None:
                    sum_half(j - 2, ada_half)

            dve.wait_ge(u_high.sem, u_high.at(1))
            dve.tensor_tensor(u_split[:, 1, :, :], src, u_split[:, 0, :, :].bitcast(F32), ALU.subtract)\
                .then_inc(u_low.sem, u_low.count(1))
            dve.wait_ge(u_low.sem, u_low.at(1))
            for b in range(4):
                low_part(0, b, b, b % 3)
            unit(1, 1, None)
            in_turns(dve, unit)
            product(n - 1, n)
            h_low_part(n - 1, n)
            for f in range(2):
                low_part(n - 1, 4 + f, 6 * n - 2 + f, f + 1)
            freed(6 * n)
            if ranges % 2:
                sum_half(0, 2 * ranges - 2)
                sum_half(1, 2 * ranges - 1)
            low.made += 6 * n
            h_ready.made += n
            h_low.made += n
            step.made += 8 * ranges
            core.freed.made += n
            dve.wait_ge(piece_used.sem, piece_used.at(6 * n))
            residual(dve, chain(core, dve, "dve"), y)
    core.end_stage()


def log1p_series(dve, link, out, e, t, z):
    link(dve.tensor_scalar(t, e, 2.0, None, ALU.add))
    link(dve.reciprocal(t, t))
    link(dve.tensor_tensor(z, e, t, ALU.mult))
    link(dve.tensor_tensor(t, z, z, ALU.mult))
    link(dve.tensor_scalar(out, t, 1.0 / 17, None, ALU.mult))
    for n in (15, 13, 11, 9, 7, 5, 3):
        link(dve.scalar_tensor_tensor(out, out, 1.0 / n, t, ALU.add, ALU.mult))
    link(dve.scalar_tensor_tensor(out, out, 1.0, z, ALU.add, ALU.mult))
    link(dve.tensor_scalar(out, out, 2.0, None, ALU.mult))


def first_projection_stage(core, u, raw, xc, y_act, qk, v_tok):
    raw_rows = raw[:, 0:4 * (SEQ + 3)].rearrange("p (c t) -> p c t", c=4)
    with core.nc.Block() as block:
        projected, raw_copied = (core.event(s) for s in ("projected", "raw_copied"))

        def pair(g):
            return core.psum[:, g % 8, :].rearrange("p (c t) -> p c t", t=SEQ)

        @block.sync
        def _(sync):
            core.load_ahead(sync, ("gate_x", 0))

        @block.tensor
        def _(pe):
            for j in range(16):
                core.project(pe, ("w_in", j), lambda k: u[:, k, :], pair(j // 2)[:, j % 2, :], projected)
            for j in range(16, 20):
                w = core.weights(pe, ("w_in", j)).rearrange("p (k m) -> p k m", k=KC)
                if j == 16:
                    pe.wait_ge(raw_copied.sem, raw_copied.at(2))
                for t in range(2):
                    for k in range(KC):
                        last = pe.matmul(core.psum[:, t, (j - 16) * P:(j - 15) * P], u[:, k, t * P:(t + 1) * P], w[:, k, :],
                                         start=(k == 0), stop=(k == KC - 1))
                core.used(pe, ("w_in", j), last, projected)

        @block.vector
        def _(dve):
            link = chain(core, dve, "dve")
            link(dve.memset(raw_rows[:, :, 0:3], 0.0))
            for g in range(2):
                dve.wait_ge(projected.sem, projected.at(2 * g + 2))
                dve.tensor_copy(raw_rows[:, 2 * g:2 * g + 2, 3:], pair(g)).then_inc(raw_copied.sem, raw_copied.count(1))
            dve.wait_ge(raw_copied.sem, raw_copied.at(2))
            w = core.col("conv_w")
            for c in range(4):
                link(dve.tensor_scalar(xc[:, c, :], raw_rows[:, c, 0:SEQ], w[:, c:c + 1], core.col("conv_b")[:, c:c + 1],
                                       ALU.mult, ALU.add))
                for k in range(1, 4):
                    link(dve.scalar_tensor_tensor(xc[:, c, :], raw_rows[:, c, k:k + SEQ], w[:, 4 * k + c:4 * k + c + 1],
                                                  xc[:, c, :], ALU.mult, ALU.add))
            dve.wait_ge(projected.sem, projected.at(20))
            for t in range(2):
                dve.tensor_copy(v_tok[:, t, :], core.psum[:, t, :])

        @block.scalar
        def _(act):
            for g in range(2, 4):
                act.wait_ge(projected.sem, projected.at(2 * g + 2))
                act.activation(y_act[:, 2 * g - 4:2 * g - 2, :], pair(g), ACT.Gelu_apprx_tanh)
            for g in range(4, 8):
                act.wait_ge(projected.sem, projected.at(2 * g + 2))
                act.activation(qk[:, 2 * g - 8:2 * g - 6, :], pair(g), ACT.Copy)
    core.end_stage()


def lru_stage(core, xc, y_act, out, r, i, a, th, u):
    lam, s = core.col("lam"), core.small
    neg, pos, e, t, z, sp, c8, nc8 = (s[:, 4 * k:4 * k + 4] for k in range(8))
    with core.nc.Block() as block:
        gate_sums, sigmoids, small_exp, small_in, rates, decays, roots, root_in = (
            core.event(n) for n in ("gate_sums", "sigmoids", "small_exp", "small_in", "rates", "decays", "roots", "root_in"))
        bank = lambda g: core.psum[:, 2 * g:2 * g + 2, :].rearrange("p b (c t) -> p (b c) t", t=SEQ)

        @block.tensor
        def _(pe):
            for g, key in enumerate(("gate_a", "gate_x")):
                w = core.weights(pe, (key, 0)).rearrange("p (c m) -> p c m", c=4)
                for c in range(4):
                    last = pe.matmul(bank(g)[:, c, :], w[:, c, :], xc[:, c, :], start=True, stop=True)
                core.used(pe, (key, 0), last, gate_sums)

        @block.scalar
        def _(act):
            act.wait_ge(small_in.sem, small_in.at(1))
            act.activation(e, neg, ACT.Exp).then_inc(small_exp.sem, small_exp.count(1))
            for g, (dst, bias) in enumerate(((r, "b_gate_a"), (i, "b_gate_x"))):
                act.wait_ge(gate_sums.sem, gate_sums.at(g + 1))
                for c in range(4):
                    act.activation(dst[:, c, :], bank(g)[:, c, :], ACT.Sigmoid, bias=core.col(bias)[:, c:c + 1])\
                        .then_inc(sigmoids.sem, sigmoids.count(1))
            act.wait_ge(rates.sem, rates.at(1))
            act.wait_ge(sigmoids.sem, sigmoids.at(8))
            for c in range(4):
                act.activation(a[:, c, :], r[:, c, :], ACT.Exp, scale=c8[:, c:c + 1])
                act.activation(th[:, c, :], r[:, c, :], ACT.Tanh, scale=nc8[:, c:c + 1]).then_inc(decays.sem, decays.count(1))
            act.wait_ge(root_in.sem, root_in.at(1))
            act.activation(th, th, ACT.Sqrt).then_inc(roots.sem, roots.count(1))

        @block.vector
        def _(dve):
            link = chain(core, dve, "dve")
            dve.scalar_tensor_tensor(neg, lam, -1.0, lam, ALU.mult, ALU.min).then_inc(small_in.sem, small_in.count(1))
            link(dve.tensor_scalar(pos, lam, -1.0, 0.0, ALU.mult, ALU.max))
            dve.wait_ge(small_exp.sem, small_exp.at(1))
            log1p_series(dve, link, sp, e, t, z)
            link(dve.tensor_tensor(sp, sp, pos, ALU.add))
            link(dve.tensor_scalar(c8, sp, -8.0, None, ALU.mult))
            dve.tensor_scalar(nc8, sp, 8.0, None, ALU.mult).then_inc(rates.sem, rates.count(1))
            dve.wait_ge(sigmoids.sem, sigmoids.at(8))
            dve.wait_ge(decays.sem, decays.at(4))
            link(dve.tensor_tensor(u, a, a, ALU.mult))
            dve.scalar_tensor_tensor(th, u, 1.0, th, ALU.add, ALU.mult).then_inc(root_in.sem, root_in.count(1))
            link(dve.tensor_tensor(i, i, xc, ALU.mult))
            dve.wait_ge(roots.sem, roots.at(1))
            link(dve.tensor_tensor(u, i, th, ALU.mult))
            for c in range(4):
                link(dve.tensor_tensor_scan(th[:, c, :], a[:, c, :], u[:, c, :], 0.0, ALU.mult, ALU.add))
            link(dve.tensor_tensor(out, th, y_act, ALU.mult))
    core.end_stage()


def bias_stage(core, rel_bias, scratch, bias):
    table = core.small[:, 0:HEADS_A]
    rows = core.buf(9).rearrange("p c t -> p (c t)")
    buckets = core.bufs[:, 7, 0:2 * SEQ]
    rows2 = core.buf(8).rearrange("p c t -> p (c t)")
    with core.nc.Block() as block:
        table_ready, distances, stored, read = (core.event(n) for n in ("table", "distances", "rows_stored", "rows_read"))
        copied = core.event("rows_copied")

        @block.sync
        def _(sync):
            core.load_const(sync, "buckets", buckets)
            sync.wait_ge(table_ready.sem, table_ready.at(1))
            sync.dma_start(table[0:REL_BUCKETS, :], rel_bias).then_inc(table_ready.sem, table_ready.count(16))
            sync.wait_ge(copied.sem, copied.at(8))
            for n, part in enumerate((rows, rows2)):
                sync.dma_start(scratch[:, 4 * n:4 * n + 4, :], part.rearrange("p (h j) -> p h j", h=4))\
                    .then_inc(stored.sem, stored.count(16))
            sync.wait_ge(stored.sem, stored.at(32))
            for t in range(2):
                for h in range(HEADS_A):
                    src = bass.AP(scratch.tensor, h * 2 * SEQ + (SEQ - 1) - t * P, [[HEADS_A * 2 * SEQ - 1, P], [1, SEQ]])
                    sync.dma_start(bias[:, h, t, :], src).then_inc(read.sem, read.count(16))
            sync.wait_ge(read.sem, read.at(16 * 16))

        @block.vector
        def _(dve):
            dve.memset(table[0:REL_BUCKETS + 1, :], 1.0).then_inc(table_ready.sem, table_ready.count(1))
            for h in range(HEADS_A):
                dve.wait_ge(distances.sem, distances.at(h + 1))
                dst = (rows if h < 4 else rows2)[:, (h % 4) * 512:(h % 4 + 1) * 512]
                dve.tensor_copy(dst, core.psum[:, h, :]).then_inc(copied.sem, copied.count(1))

        @block.tensor
        def _(pe):
            pe.wait_ge(table_ready.sem, table_ready.at(17))
            for h in range(HEADS_A):
                pe.matmul(core.psum[:, h, :], table[0:REL_BUCKETS + 1, h:h + 1].to_broadcast([REL_BUCKETS + 1, P]),
                                       buckets[0:REL_BUCKETS + 1, :], start=True, stop=True)\
                    .then_inc(distances.sem, distances.count(1))
    core.end_stage()


def attention_stage(core, heads, q, k, v, bias, out, s_buf, p_buf, pt_buf, sinks=None):
    scale = HEAD ** -0.5
    ident = core.const("ident")
    stat = lambda h, n: core.small[:, 64 + 16 * (h % 2) + 2 * n:64 + 16 * (h % 2) + 2 * n + 2]
    bank = lambda n, h: core.psum[:, 2 * n + h % 2, :].rearrange("p (a t) -> p a t", a=2)
    with core.nc.Block() as block:
        scored, maxed, exped, normed, turned, turned_sb, attended, stored = (
            core.event(n) for n in ("scored", "row_max", "exped", "normed", "turned", "turned_sb", "attended", "head_out"))

        @block.tensor
        def _(pe):
            def scores(h):
                if h >= 2:
                    pe.wait_ge(maxed.sem, maxed.at(h - 1))
                for t in range(2):
                    last = pe.matmul(bank(0, h)[:, t, :], q(h)[:, t * P:(t + 1) * P], k(h), start=True, stop=True)
                last.then_inc(scored.sem, scored.count(1))

            def turn(h):
                pe.wait_ge(normed.sem, normed.at(h + 1))
                if h >= 2:
                    pe.wait_ge(turned_sb.sem, turned_sb.at(h - 1))
                for kt in range(2):
                    for t in range(2):
                        last = pe.transpose(bank(1, h)[:, kt, t * P:(t + 1) * P], p_buf(h)[:, t, kt * P:(kt + 1) * P], ident)
                last.then_inc(turned.sem, turned.count(1))

            def attend(h):
                pe.wait_ge(turned_sb.sem, turned_sb.at(h + 1))
                if h >= 2:
                    pe.wait_ge(stored.sem, stored.at(h - 1))
                base = HEAD * (h % 2)
                for kt in range(2):
                    last = pe.matmul(bank(2, h)[base:base + HEAD, 0, :], v(h, kt), pt_buf(h)[:, kt, :],
                                     start=(kt == 0), stop=(kt == 1))
                last.then_inc(attended.sem, attended.count(1))

            scores(0)
            scores(1)
            for h in range(heads):
                turn(h)
                if h + 2 < heads:
                    scores(h + 2)
                attend(h)

        @block.vector
        def _(dve):
            link = chain(core, dve, "dve")

            def softmax_in(h):
                dve.wait_ge(scored.sem, scored.at(h + 1))
                link(dve.scalar_tensor_tensor(s_buf(h), bank(0, h), scale, bias(h), ALU.mult, ALU.add))
                link(dve.tensor_reduce(stat(h, 0), s_buf(h), AX, ALU.max))
                if sinks is not None:
                    link(dve.tensor_scalar(stat(h, 0), stat(h, 0), sinks[:, h:h + 1], None, ALU.max))
                dve.tensor_scalar(stat(h, 1), stat(h, 0), -1.0, None, ALU.mult).then_inc(maxed.sem, maxed.count(1))

            def softmax_out(h):
                dve.wait_ge(exped.sem, exped.at(h + 1))
                if sinks is not None:
                    link(dve.tensor_tensor(stat(h, 2), stat(h, 2), stat(h, 3), ALU.add))
                link(dve.reciprocal(stat(h, 4), stat(h, 2)))
                link(dve.tensor_scalar(p_buf(h)[:, 0, :], p_buf(h)[:, 0, :], stat(h, 4)[:, 0:1], None, ALU.mult))
                dve.tensor_scalar(p_buf(h)[:, 1, :], p_buf(h)[:, 1, :], stat(h, 4)[:, 1:2], None, ALU.mult)\
                    .then_inc(normed.sem, normed.count(1))

            def head_out(h):
                dve.wait_ge(attended.sem, attended.at(h + 1))
                base = HEAD * (h % 2)
                dve.tensor_copy(out(h), bank(2, h)[base:base + HEAD, 0, :]).then_inc(stored.sem, stored.count(1))

            softmax_in(0)
            for h in range(heads):
                if h + 1 < heads:
                    softmax_in(h + 1)
                softmax_out(h)
                if h >= 1:
                    head_out(h - 1)
            head_out(heads - 1)

        @block.scalar
        def _(act):
            link = chain(core, act, "act")

            def exps(h):
                act.wait_ge(maxed.sem, maxed.at(h + 1))
                if h >= 2:
                    act.wait_ge(turned.sem, turned.at(h - 1))
                for t in range(2):
                    if sinks is not None:
                        link(act.activation(stat(h, 3)[:, t:t + 1], sinks[:, h:h + 1], ACT.Exp, bias=stat(h, 1)[:, t:t + 1]))
                    e = act.activation(p_buf(h)[:, t, :], s_buf(h)[:, t, :], ACT.Exp, bias=stat(h, 1)[:, t:t + 1],
                                       accum_out=stat(h, 2)[:, t:t + 1])
                    if t == 0:
                        link(e)
                e.then_inc(exped.sem, exped.count(1))

            def turned_copy(h):
                act.wait_ge(turned.sem, turned.at(h + 1))
                if h >= 2:
                    act.wait_ge(attended.sem, attended.at(h - 1))
                act.activation(pt_buf(h), bank(1, h), ACT.Copy).then_inc(turned_sb.sem, turned_sb.count(1))

            exps(0)
            for h in range(heads):
                if h + 1 < heads:
                    exps(h + 1)
                turned_copy(h)
    core.end_stage()


def output_stage(core, key, merged, n, residual):
    y = core.psum[:, 0:4, :].rearrange("p b (c t) -> p (b c) t", t=SEQ)
    with core.nc.Block() as block:
        projected = core.event("projected")

        @block.sync
        def _(sync):
            core.load_ahead(sync, (key, KC - 1))

        @block.tensor
        def _(pe):
            for j in range(KC):
                core.project(pe, (key, j), lambda k: merged(k), y[:, j, :], projected, kcs=n)

        @block.vector
        def _(dve):
            dve.wait_ge(projected.sem, projected.at(KC))
            residual(dve, chain(core, dve, "dve"), y)
    core.end_stage()


def router_stage(core, u, gate_t, gates):
    G, E = N_GROUPS, PER_GROUP
    n = G + N_EXPERTS
    s = core.small
    logits = s[:, 0:2 * n].rearrange("p (t n) -> p t n", t=2)
    at = 2 * n

    def tile(*shape):
        nonlocal at
        size = int(np.prod(shape))
        v = s[:, at:at + size]
        at += size
        names = "abc"[:len(shape)]
        return v.rearrange(f"p ({' '.join(names)}) -> p {' '.join(names)}", **dict(zip(names, shape)))

    rank, rank_g = tile(E), tile(G)
    m, gsum, gtop = tile(2, 1), tile(2, 1), tile(2, 1)
    ge, hot_g, e_in, hot1, hot2, left = tile(2, G), tile(2, G), tile(2, E), tile(2, E), tile(2, E), tile(2, E)
    m1, m2, ed, w1, w2 = (tile(2, 1) for _ in range(5))
    picked, weight_e, gate = tile(2, G, E), tile(2, E), tile(2, G, E)
    bc = lambda a, w: a.to_broadcast([P, 2, w])
    with core.nc.Block() as block:
        routed, softened, soft_in, gate_ready, gate_turned, gate_sb, gate_stored = (
            core.event(x) for x in ("routed", "softened", "soft_in", "gate_ready", "gate_turned", "gate_sb", "gate_stored"))

        @block.sync
        def _(sync):
            core.load_ahead(sync, ("router", 0))
            sync.wait_ge(gate_sb.sem, gate_sb.at(1))
            sync.dma_start(gates, gate_t[0:N_EXPERTS, :]).then_inc(gate_stored.sem, gate_stored.count(16))
            sync.wait_ge(gate_stored.sem, gate_stored.made)

        @block.tensor
        def _(pe):
            w = core.weights(pe, ("router", 0)).rearrange("p (k m) -> p k m", k=KC)
            for t in range(2):
                pe.matmul(core.psum[:, 0, t * n:(t + 1) * n], core.const("ones")[0:1, :], core.col("router_b")[0:1, :],
                          start=True, stop=False)
                for k in range(KC):
                    last = pe.matmul(core.psum[:, 0, t * n:(t + 1) * n], u[:, k, t * P:(t + 1) * P], w[:, k, :],
                                     start=False, stop=(k == KC - 1))
            core.used(pe, ("router", 0), last, routed)
            pe.wait_ge(gate_ready.sem, gate_ready.at(1))
            for t in range(2):
                last = pe.transpose(core.psum[0:N_EXPERTS, 1, t * P:(t + 1) * P], gate[:, t, :, :].rearrange("p g e -> p (g e)"),
                                    core.const("ident"))
            last.then_inc(gate_turned.sem, gate_turned.count(1))

        @block.scalar
        def _(act):
            act.wait_ge(soft_in.sem, soft_in.at(1))
            act.activation(ge, ge, ACT.Exp).then_inc(softened.sem, softened.count(1))
            act.wait_ge(soft_in.sem, soft_in.at(2))
            act.activation(ed, ed, ACT.Exp).then_inc(softened.sem, softened.count(1))

        @block.vector
        def _(dve):
            link = chain(core, dve, "dve")

            def first_hot(hot, x, top, rank_, width):
                link(dve.tensor_tensor(hot, x, bc(top, width), ALU.is_equal))
                link(dve.tensor_tensor(hot, hot, rank_.unsqueeze(1).to_broadcast([P, 2, width]), ALU.mult))
                link(dve.tensor_reduce(m, hot, AX, ALU.max))
                link(dve.tensor_tensor(hot, hot, bc(m, width), ALU.is_equal))

            for k in range(E):
                link(dve.memset(rank[:, k:k + 1], float(E - k)))
            for k in range(G):
                link(dve.memset(rank_g[:, k:k + 1], float(G - k)))
            dve.wait_ge(routed.sem, routed.at(1))
            link(dve.tensor_copy(logits, core.psum[:, 0, 0:2 * n].rearrange("p (t n) -> p t n", t=2)))
            lg = logits[:, :, 0:G]
            le = logits[:, :, G:n].rearrange("p t (g e) -> p t g e", g=G)
            link(dve.tensor_reduce(gtop, lg, AX, ALU.max))
            first_hot(hot_g, lg, gtop, rank_g, G)
            dve.tensor_tensor(ge, lg, bc(gtop, G), ALU.subtract).then_inc(soft_in.sem, soft_in.count(1))
            for t in range(2):
                link(dve.tensor_tensor(picked[:, t, :, :], le[:, t, :, :], hot_g[:, t, :].unsqueeze(2).to_broadcast([P, G, E]), ALU.mult))
                link(dve.tensor_reduce(e_in[:, t, :], picked[:, t, :, :].rearrange("p g e -> p e g"), AX, ALU.add))
            link(dve.tensor_reduce(m1, e_in, AX, ALU.max))
            first_hot(hot1, e_in, m1, rank, E)
            link(dve.scalar_tensor_tensor(left, hot1, NEG, e_in, ALU.mult, ALU.add))
            link(dve.tensor_reduce(m2, left, AX, ALU.max))
            first_hot(hot2, left, m2, rank, E)
            dve.wait_ge(softened.sem, softened.at(1))
            dve.tensor_tensor(ed, m2, m1, ALU.subtract).then_inc(soft_in.sem, soft_in.count(1))
            link(dve.tensor_reduce(gsum, ge, AX, ALU.add))
            link(dve.reciprocal(gtop, gsum))
            dve.wait_ge(softened.sem, softened.at(2))
            link(dve.tensor_scalar(w1, ed, 1.0, None, ALU.add))
            link(dve.reciprocal(w1, w1))
            link(dve.tensor_tensor(w1, w1, gtop, ALU.mult))
            link(dve.tensor_tensor(w2, w1, ed, ALU.mult))
            link(dve.tensor_tensor(hot1, hot1, bc(w1, E), ALU.mult))
            link(dve.tensor_tensor(hot2, hot2, bc(w2, E), ALU.mult))
            link(dve.tensor_tensor(weight_e, hot1, hot2, ALU.add))
            for t in range(2):
                last = dve.tensor_tensor(gate[:, t, :, :], hot_g[:, t, :].unsqueeze(2).to_broadcast([P, G, E]),
                                         weight_e[:, t, :].unsqueeze(1).to_broadcast([P, G, E]), ALU.mult)
                if t == 0:
                    link(last)
            last.then_inc(gate_ready.sem, gate_ready.count(1))
            dve.wait_ge(gate_turned.sem, gate_turned.at(1))
            dve.tensor_copy(gate_t[0:N_EXPERTS, :], core.psum[0:N_EXPERTS, 1, 0:SEQ]).then_inc(gate_sb.sem, gate_sb.count(1))
    core.end_stage()


def first_block(core):
    first_ada_stage(core)
    sh1, sc1, g1, sh2, sc2, g2 = (core.mod[:, v * KC:(v + 1) * KC] for v in range(6))
    one_plus = lambda scale: (lambda dve, link: link(dve.tensor_scalar(core.gain[:], scale, 1.0, None, ALU.add)))
    u = core.buf(0)
    norm_stage(core, core.x, u, LN_EPS, core.gain, sh1, center=True, pre=one_plus(sc1))
    y_act, qk, v_tok = core.buf(1)[:, 0:4, :], core.buf(2), core.buf(3)[:, 0:4, :].rearrange("p c t -> p (c t)").rearrange("p (t n) -> p t n", t=2)
    xc = core.buf(5)[:, 0:4, :]
    first_projection_stage(core, u, core.bufs[:, 4, :], xc, y_act, qk, v_tok)
    lru_out, attn_out = core.buf(0)[:, 0:4, :], core.buf(0)[:, 4:8, :]
    lru_stage(core, xc, y_act, lru_out, core.buf(5)[:, 4:8, :], core.buf(6)[:, 0:4, :], core.buf(6)[:, 4:8, :],
              core.buf(7)[:, 0:4, :], core.buf(7)[:, 4:8, :])
    bias = core.buf(4, 2).rearrange("p (h a) t -> p h a t", h=HEADS_A)
    bias_stage(core, core.rel_bias, core.scratch, bias)
    rows = lambda x, h: x[HEAD * (h % 2):HEAD * (h % 2) + HEAD, h // 2, :]
    attention_stage(core, HEADS_A, lambda h: rows(qk[:, 0:4, :], h), lambda h: rows(qk[:, 4:8, :], h),
                    lambda h, kt: v_tok[:, kt, HEAD * h:HEAD * h + HEAD], lambda h: bias[:, h, :, :],
                    lambda h: rows(attn_out, h), lambda h: core.buf(6)[:, 2 * (h % 2):2 * (h % 2) + 2, :],
                    lambda h: core.buf(6)[:, 4 + 2 * (h % 2):6 + 2 * (h % 2), :],
                    lambda h: core.buf(7)[:, 2 * (h % 2):2 * (h % 2) + 2, :])
    norm_stage(core, lru_out, lru_out, LN_EPS, core.col("norm_lru_g"), n=4)
    norm_stage(core, attn_out, attn_out, LN_EPS, core.col("norm_attn_g"), n=4)

    def residual(gate):
        def run(dve, link, y):
            for c in range(KC):
                link(dve.tensor_scalar(core.x[:, c, :], core.x[:, c, :], ALPHA, None, ALU.mult))
                dve.scalar_tensor_tensor(core.x[:, c, :], y[:, c, :], gate[:, c:c + 1], core.x[:, c, :], ALU.mult, ALU.add)
        return run

    output_stage(core, "w_out", lambda k: core.buf(0)[:, k, :], KC, residual(g1))
    norm_stage(core, core.x, core.x, LN_EPS, core.col("ln1_g"), core.col("ln1_b"), center=True)
    norm_stage(core, core.x, u, LN_EPS, core.gain, sh2, center=True, pre=one_plus(sc2))
    router_stage(core, u, core.buf(1)[:, 0, :], core.gates)
    glu_stage(core, "moe", N_EXPERTS, u, residual(g2), gates=core.gates, ada=(0, 0, 9))
    norm_stage(core, core.x, core.x, LN_EPS, core.col("ln2_g"), core.col("ln2_b"), center=True)


def head_rms_stage(core, x, n, gains, squares, roots):
    banks = core.psum[:, 0:8, :].rearrange("p b (c t) -> p (b c) t", t=SEQ)
    with core.nc.Block() as block:
        squared, summed, scaled, rooted = (core.event(s) for s in ("squared", "square_sum", "scaled", "rooted"))

        @block.scalar
        def _(act):
            for c in range(n):
                act.activation(squares[:, c, :], x[:, c, :], ACT.Square).then_inc(squared.sem, squared.count(1))
            act.wait_ge(scaled.sem, scaled.at(1))
            act.activation(roots[:, 0:n, :], roots[:, 0:n, :], ACT.Sqrt).then_inc(rooted.sem, rooted.count(1))

        @block.tensor
        def _(pe):
            for c in range(n):
                pe.wait_ge(squared.sem, squared.at(c + 1))
                last = pe.matmul(banks[:, c, :], core.const("heads"), squares[:, c, :], start=True, stop=True)
            last.then_inc(summed.sem, summed.count(1))

        @block.vector
        def _(dve):
            link = chain(core, dve, "dve")
            dve.wait_ge(summed.sem, summed.at(1))
            dve.tensor_scalar(roots[:, 0:n, :], banks[:, 0:n, :], 1.0 / HEAD, NORM_EPS, ALU.mult, ALU.add)\
                .then_inc(scaled.sem, scaled.count(1))
            dve.wait_ge(rooted.sem, rooted.at(1))
            link(dve.reciprocal(roots[:, 0:n, :], roots[:, 0:n, :]))
            for c in range(n):
                dve.scalar_tensor_tensor(x[:, c, :], x[:, c, :], gains(c), roots[:, c, :], ALU.mult, ALU.mult)
    core.end_stage()


def window_projection_stage(core, u, qk, v_tok):
    with core.nc.Block() as block:
        projected = core.event("projected")

        def slot(c):
            return core.psum[:, c // 2, (c % 2) * SEQ:(c % 2 + 1) * SEQ]

        @block.sync
        def _(sync):
            core.load_ahead(sync, ("sw_qkv", 11))
            core.load_const(sync, "band", core.bufs[:, 8, 0:2 * SEQ])

        @block.tensor
        def _(pe):
            for j in range(10):
                if j < 8:
                    core.project(pe, ("sw_qkv", j), lambda k: u[:, k, :], slot(j), projected)
                    continue
                w = core.weights(pe, ("sw_qkv", j)).rearrange("p (k m) -> p k m", k=KC)
                for half in range(2):
                    for k in range(KC):
                        pe.matmul(slot(j + 2)[HEAD * half:HEAD * (half + 1), :], w[:, k, HEAD * (1 - half):HEAD * (2 - half)],
                                  u[:, k, :], start=(k == 0), stop=(k == KC - 1))
                core.project(pe, ("sw_qkv", j), lambda k: u[:, k, :], slot(j), projected)
            for j in range(10, 12):
                w = core.weights(pe, ("sw_qkv", j)).rearrange("p (k m) -> p k m", k=KC)
                for t in range(2):
                    for k in range(KC):
                        last = pe.matmul(core.psum[:, 6 + t, (j - 10) * P:(j - 9) * P], u[:, k, t * P:(t + 1) * P], w[:, k, :],
                                         start=(k == 0), stop=(k == KC - 1))
                core.used(pe, ("sw_qkv", j), last, projected)

        @block.scalar
        def _(act):
            for g in range(4):
                act.wait_ge(projected.sem, projected.at(2 * g + 2))
                act.activation(qk[:, 2 * g:2 * g + 2, :], core.psum[:, g, :].rearrange("p (c t) -> p c t", t=SEQ), ACT.Copy)
            for g in (4, 5):
                act.wait_ge(projected.sem, projected.at(10))
                act.activation(qk[:, 2 * g:2 * g + 2, :], core.psum[:, g, :].rearrange("p (c t) -> p c t", t=SEQ), ACT.Copy)

        @block.vector
        def _(dve):
            dve.wait_ge(projected.sem, projected.at(12))
            for t in range(2):
                dve.tensor_copy(v_tok[:, t, :], core.psum[:, 6 + t, 0:SEQ])
    core.end_stage()


def gated_residual(core):
    gate = core.mod[:, 5 * KC:6 * KC]

    def run(dve, link, y):
        for c in range(KC):
            dve.scalar_tensor_tensor(core.x[:, c, :], y[:, c, :], gate[:, c:c + 1], core.x[:, c, :], ALU.mult, ALU.add)
    return run


def window_attention(core):
    u = core.buf(0)
    qk = core.buf(1, 2)
    v_tok = core.buf(2)[:, 4:6, :]
    window_projection_stage(core, u, qk, v_tok)
    head_rms_stage(core, qk, 12, lambda c: core.col("q_norm" if c < 8 else "k_norm"), core.buf(3, 2), core.buf(5, 2))
    band = core.bufs[:, 8, 0:2 * SEQ].rearrange("p (a t) -> p a t", a=2)
    rows = lambda x, c, h: x[HEAD * (h % 2):HEAD * (h % 2) + HEAD, c, :]

    def k_rows(h):
        kv = h // (SW_Q // SW_KV)
        return rows(qk, (8 if kv % 2 == h % 2 else 10) + kv // 2, h)

    attention_stage(core, SW_Q, lambda h: rows(qk, h // 2, h), k_rows,
                    lambda h, kt: v_tok[:, kt, HEAD * (h // 4):HEAD * (h // 4) + HEAD], lambda h: band,
                    lambda h: rows(u, h // 2, h), lambda h: core.buf(6)[:, 2 * (h % 2):2 * (h % 2) + 2, :],
                    lambda h: core.buf(6)[:, 4 + 2 * (h % 2):6 + 2 * (h % 2), :],
                    lambda h: core.buf(7)[:, 2 * (h % 2):2 * (h % 2) + 2, :], sinks=core.col("sinks"))
    output_stage(core, "sw_o", lambda k: u[:, k, :], KC, gated_residual(core))


def rwkv_projection_stage(core, jobs, h, dx, xs, after=None):
    with core.nc.Block() as block:
        mixed, projected, evacuated, up_done, narrow_ready = (
            core.event(s) for s in ("mixed", "projected", "evacuated", "narrow_sums", "narrow_ready"))
        inputs = [j for j in jobs if j[0] is not None]
        narrow = core.narrow
        last_use, products, ups = [], 0, 0
        for mu, up, _, down, *_ in jobs:
            if mu is None:
                last_use.pop()
            ups += len(up) if down else 0
            products += KC
            last_use.append((up_done, ups) if down else (projected, products))

        def pair(g):
            return core.psum[:, g % 6, :].rearrange("p (c t) -> p c t", t=SEQ)

        @block.sync
        def _(sync):
            core.load_ahead(sync, (jobs[-1][3] or jobs[-1][1])[-1])
            if after:
                after(sync)

        @block.vector
        def _(dve):
            link = chain(core, dve, "dve")
            if isinstance(jobs[0][6], str):
                link(dve.tensor_tensor(dx[:, :, 1:], h[:, :, :SEQ - 1], h[:, :, 1:], ALU.subtract))
                link(dve.tensor_scalar(dx[:, :, 0:1], h[:, :, 0:1], -1.0, None, ALU.mult))
            for n, job in enumerate(inputs):
                if n >= 2:
                    used, count = last_use[n - 2]
                    dve.wait_ge(used.sem, used.at(count))
                for c in range(KC):
                    last = dve.scalar_tensor_tensor(xs(n)[:, c, :], dx[:, c, :], job[0][:, c:c + 1], h[:, c, :], ALU.mult, ALU.add)
                last.then_inc(mixed.sem, mixed.count(1))

        @block.tensor
        def _(pe):
            n, g, ups = -1, 0, 0
            for mu, up, up_func, down, out, func, bias in jobs:
                if mu is not None:
                    n += 1
                    pe.wait_ge(mixed.sem, mixed.at(n + 1))
                source = xs(n)
                if not down:
                    for j, key in enumerate(up):
                        if j % 2 == 0 and g >= 6:
                            pe.wait_ge(evacuated.sem, evacuated.at(g - 5))
                        core.project(pe, key, lambda k: source[:, k, :], pair(g)[:, j % 2, :], projected)
                        g += j % 2
                else:
                    for b, key in enumerate(up):
                        m = core.place[key][2] // KC
                        core.project(pe, key, lambda k: source[:, k, :], core.psum[0:m, 6 + b, 0:SEQ], up_done, m=m)
                if down:
                    ups += len(up)
                    pe.wait_ge(narrow_ready.sem, narrow_ready.at(ups))
                    for c in range(KC):
                        if c % 2 == 0 and g >= 6:
                            pe.wait_ge(evacuated.sem, evacuated.at(g - 5))
                        for b, key in enumerate(down):
                            rows = core.place[up[b]][2] // KC
                            w = core.weights(pe, key)
                            last = pe.matmul(pair(g)[:, c % 2, :], w[0:rows, c * P:(c + 1) * P], narrow[0:rows, b, :],
                                             start=(b == 0), stop=(b == len(down) - 1))
                            if c == KC - 1 and b < len(down) - 1:
                                core.used(pe, key, last)
                        if c == KC - 1:
                            core.used(pe, down[-1], last, projected)
                        else:
                            last.then_inc(projected.sem, projected.count(1))
                        g += c % 2

        @block.scalar
        def _(act):
            g, products, ups = 0, 0, 0
            for mu, up, up_func, down, out, func, bias in jobs:
                for b, key in enumerate(up if down else ()):
                    ups += 1
                    act.wait_ge(up_done.sem, up_done.at(ups))
                    m = core.place[key][2] // KC
                    act.activation(narrow[0:m, b, :], core.psum[0:m, 6 + b, 0:SEQ], up_func)\
                        .then_inc(narrow_ready.sem, narrow_ready.count(1))
                for c in range(0, KC, 2):
                    products += 2
                    act.wait_ge(projected.sem, projected.at(products))
                    if bias is None or isinstance(bias, str):
                        e = act.activation(out[:, c:c + 2, :], pair(g), func)
                    else:
                        act.activation(out[:, c, :], pair(g)[:, 0, :], func, bias=bias[:, c:c + 1])
                        e = act.activation(out[:, c + 1, :], pair(g)[:, 1, :], func, bias=bias[:, c + 1:c + 2])
                    e.then_inc(evacuated.sem, evacuated.count(1))
                    g += 1
    core.end_stage()


def value_mix_stage(core, v, gate, first, v_first):
    with core.nc.Block() as block:
        read = core.event("v_first_read")

        @block.sync
        def _(sync):
            sync.dma_start(first, v_first).then_inc(read.sem, read.count(16))

        @block.vector
        def _(dve):
            link = chain(core, dve, "dve")
            dve.wait_ge(read.sem, read.at(16))
            link(dve.tensor_tensor(first, first, v, ALU.subtract))
            link(dve.tensor_tensor(first, first, gate, ALU.mult))
            link(dve.tensor_tensor(v, v, first, ALU.add))
    core.end_stage()


def rwkv_scale_stage(core, n, kk, w, tmp, bonus, r, k, v, lw, a):
    s = core.small
    mid, end, e_mid, e_end = (s[:, 16 * q:16 * q + 16] for q in range(4))
    flat = lambda x: x.rearrange("p c t -> p (c t)")
    by_chunk = lambda x: flat(x).rearrange("p (q t) -> p q t", t=P)
    sums = lambda g: core.psum[:, 4 * g:4 * g + 4, :].rearrange("p b t -> p (b t)")
    with core.nc.Block() as block:
        names = ("kk_raw", "kk_squared", "kk_sums", "kk_bounded", "kk_rooted", "bonus_in", "bonus_sums",
                 "w_ready", "w_centered", "prev_ready", "mid_exp", "r_exp", "prev_exp", "r_scaled", "k_exp")
        sig = {x: core.event(x) for x in names}

        @block.vector
        def _(dve):
            link = chain(core, dve, "dve")
            kc = lambda x: core.col(f"{x}{n}")
            for c in range(KC):
                last = dve.tensor_scalar(kk[:, c, :], k[:, c, :], kc("k_k")[:, c:c + 1], None, ALU.mult)
            last.then_inc(sig["kk_raw"].sem, sig["kk_raw"].count(1))
            link(dve.tensor_scalar(flat(lw), flat(lw), -float(np.exp(-0.5)), None, ALU.mult))
            for q in range(16):
                last = dve.tensor_tensor_scan(by_chunk(w)[:, q, :], core.const("ones"), by_chunk(lw)[:, q, :], 0.0, ALU.mult, ALU.add)
            link(last)
            link(dve.tensor_copy(mid, by_chunk(w)[:, :, P // 2 - 1]))
            link(dve.tensor_tensor(end, by_chunk(w)[:, :, P - 1], mid, ALU.subtract))
            dve.tensor_tensor(by_chunk(w), by_chunk(w), mid.unsqueeze(2).to_broadcast([P, 16, P]), ALU.subtract)\
                .then_inc(sig["w_centered"].sem, sig["w_centered"].count(1))
            dve.wait_ge(sig["w_centered"].sem, sig["w_centered"].at(1))
            dve.tensor_tensor(flat(lw), flat(w), flat(lw), ALU.subtract)\
                .then_inc(sig["prev_ready"].sem, sig["prev_ready"].count(1))
            dve.wait_ge(sig["kk_sums"].sem, sig["kk_sums"].at(1))
            dve.wait_ge(sig["kk_squared"].sem, sig["kk_squared"].at(1))
            dve.tensor_scalar(flat(bonus), sums(0), 1e-24, None, ALU.max)\
                .then_inc(sig["kk_bounded"].sem, sig["kk_bounded"].count(1))
            dve.wait_ge(sig["kk_rooted"].sem, sig["kk_rooted"].at(1))
            link(dve.reciprocal(flat(bonus), flat(bonus)))
            link(dve.tensor_tensor(flat(kk), flat(kk), flat(bonus), ALU.mult))
            for c in range(KC):
                last = dve.tensor_scalar(bonus[:, c, :], a[:, c, :], -1.0, kc("k_a")[:, c:c + 1], ALU.add, ALU.mult)
            link(last)
            link(dve.scalar_tensor_tensor(flat(k), flat(bonus), 1.0, flat(k), ALU.add, ALU.mult))
            link(dve.tensor_tensor(flat(a), flat(a), flat(kk), ALU.mult))
            for c in range(KC):
                last = dve.scalar_tensor_tensor(bonus[:, c, :], r[:, c, :], kc("r_k")[:, c:c + 1], k[:, c, :], ALU.mult, ALU.mult)
            last.then_inc(sig["bonus_in"].sem, sig["bonus_in"].count(1))
            dve.wait_ge(sig["r_exp"].sem, sig["r_exp"].at(1))
            dve.wait_ge(sig["bonus_in"].sem, sig["bonus_in"].at(1))
            dve.tensor_tensor(flat(r), flat(r), flat(tmp), ALU.mult).then_inc(sig["r_scaled"].sem, sig["r_scaled"].count(1))
            dve.wait_ge(sig["prev_exp"].sem, sig["prev_exp"].at(1))
            dve.scalar_tensor_tensor(flat(kk), flat(kk), -1.0, flat(lw), ALU.mult, ALU.mult)
            dve.wait_ge(sig["bonus_sums"].sem, sig["bonus_sums"].at(1))
            dve.tensor_tensor(flat(bonus), sums(1), flat(v), ALU.mult)
            dve.wait_ge(sig["k_exp"].sem, sig["k_exp"].at(1))
            dve.tensor_tensor(flat(k), flat(k), flat(tmp), ALU.mult)
            dve.tensor_tensor(flat(a), flat(a), flat(tmp), ALU.mult)

        @block.scalar
        def _(act):
            act.wait_ge(sig["kk_raw"].sem, sig["kk_raw"].at(1))
            act.activation(flat(bonus), flat(kk), ACT.Square).then_inc(sig["kk_squared"].sem, sig["kk_squared"].count(1))
            act.wait_ge(sig["w_centered"].sem, sig["w_centered"].at(1))
            act.activation(e_mid, mid, ACT.Exp)
            act.activation(e_end, end, ACT.Exp)
            act.activation(flat(tmp), flat(w), ACT.Exp).then_inc(sig["r_exp"].sem, sig["r_exp"].count(1))
            act.wait_ge(sig["prev_ready"].sem, sig["prev_ready"].at(1))
            act.activation(flat(lw), flat(lw), ACT.Exp).then_inc(sig["prev_exp"].sem, sig["prev_exp"].count(1))
            act.wait_ge(sig["kk_bounded"].sem, sig["kk_bounded"].at(1))
            act.activation(flat(bonus), flat(bonus), ACT.Sqrt).then_inc(sig["kk_rooted"].sem, sig["kk_rooted"].count(1))
            act.wait_ge(sig["r_scaled"].sem, sig["r_scaled"].at(1))
            act.activation(flat(tmp), flat(w), ACT.Exp, scale=-1.0).then_inc(sig["k_exp"].sem, sig["k_exp"].count(1))

        @block.tensor
        def _(pe):
            for ready, done, g in (("kk_squared", "kk_sums", 0), ("bonus_in", "bonus_sums", 1)):
                pe.wait_ge(sig[ready].sem, sig[ready].at(1))
                for c in range(KC):
                    last = pe.matmul(sums(g)[:, c * SEQ:(c + 1) * SEQ], core.const("heads"), bonus[:, c, :], start=True, stop=True)
                last.then_inc(sig[done].sem, sig[done].count(1))
    core.end_stage()


def rwkv_chunk_stage(core, r, k, v, a, b, sets, part):
    s = core.small
    e_mid, e_end = s[:, 32:48], s[:, 48:64]
    four = lambda x: x.rearrange("p (h t) -> p h t", h=4)
    tile = lambda q: four(sets[:, q * 512:(q + 1) * 512])
    ab, ab_t, t_, tt, ak_t, rb_t, rk_t, x_ = (tile(q) for q in range(8))
    tok = part[:, 0:768].rearrange("p (q c m) -> p q c m", q=3, c=2)
    c_in = part[:, 768:1024].rearrange("p (h m) -> p h m", h=4)
    u_ = part[:, 1024:1280].rearrange("p (h m) -> p h m", h=4)
    masked = four(part[:, 1280:1792])
    state = core.state[:, 0, :].rearrange("p (c m) -> p c m", m=HEAD)
    scaled = core.state[:, 1, :].rearrange("p (c m) -> p c m", m=HEAD)
    bank = lambda q: core.psum[:, q, :]
    ident = core.const("ident")
    below, above = (core.const(q).rearrange("p (l t) -> p l t", l=LEVELS) for q in ("below", "above"))
    causal = core.const("causal").rearrange("p (a t) -> p a t", a=2)
    lower = core.const("lower")
    groups = [(ck, g) for ck in range(SEQ // P) for g in range(4)]
    with core.nc.Block() as block:
        names = ("turned", "turned_sb", "products", "products_sb", "level_mask", "level_x", "level_x_sb", "level_t",
                 "level_t_sb", "c_sums", "c_sb", "u_sums", "u_sb", "y_sums", "y_sb", "state_sums", "state_sb", "state_scaled")
        sig = {x: core.event(x) for x in names}

        @block.tensor
        def _(pe):
            for n, (ck, g) in enumerate(groups):
                now = slice(ck * P, (ck + 1) * P)
                rows = lambda x, h: x[HEAD * (h % 2):HEAD * (h % 2) + HEAD, 2 * g + h // 2, now]
                if n:
                    pe.wait_ge(sig["y_sb"].sem, sig["y_sb"].at(n))
                    pe.wait_ge(sig["state_sb"].sem, sig["state_sb"].at(min(n, 4)))
                for c in range(2):
                    pe.transpose(bank(0)[:, c * P:(c + 1) * P], k[:, 2 * g + c, now], ident)
                    pe.transpose(bank(0)[:, (2 + c) * P:(3 + c) * P], b[:, 2 * g + c, now], ident)
                    last = pe.transpose(bank(1)[:, c * P:(c + 1) * P], v[:, 2 * g + c, now], ident)
                last.then_inc(sig["turned"].sem, sig["turned"].count(1))
                for h in range(4):
                    both = core.bufs[HEAD * (h % 2):HEAD * (h % 2) + HEAD, 0:5:4,
                                     (2 * g + h // 2) * SEQ + ck * P:(2 * g + h // 2) * SEQ + (ck + 1) * P]
                    pe.matmul(bank(2 + h % 2)[:, (h // 2) * SEQ:(h // 2 + 1) * SEQ], rows(b, h), both, start=True, stop=True)
                    pe.matmul(bank(4 + h % 2)[:, (h // 2) * SEQ:(h // 2 + 1) * SEQ], rows(k, h), both, start=True, stop=True)
                    last = pe.matmul(bank(6 + h % 2)[:, (h // 2) * P:(h // 2 + 1) * P], rows(a, h), rows(b, h), start=True, stop=True)
                    if h >= 2:
                        last.then_inc(sig["products"].sem, sig["products"].count(1))
                for level in range(1, LEVELS):
                    m = n * (LEVELS - 1) + level - 1
                    pe.wait_ge(sig["level_mask"].sem, sig["level_mask"].at(m + 1))
                    if level > 1:
                        pe.wait_ge(sig["level_t_sb"].sem, sig["level_t_sb"].at(m))
                    for h in range(4):
                        last = pe.matmul(bank(7)[:, h * P:(h + 1) * P], masked[:, h, :], t_[:, h, :], start=True, stop=True)
                    last.then_inc(sig["level_x"].sem, sig["level_x"].count(1))
                    pe.wait_ge(sig["level_x_sb"].sem, sig["level_x_sb"].at(m + 1))
                    if level == 1:
                        pe.wait_ge(sig["turned_sb"].sem, sig["turned_sb"].at(2 * n + 2))
                    for h in range(4):
                        pe.matmul(bank(0)[:, h * P:(h + 1) * P], tt[:, h, :], x_[:, h, :], start=True, stop=True)
                        last = pe.matmul(bank(1)[:, h * P:(h + 1) * P], x_[:, h, :], tt[:, h, :], start=True, stop=True)
                    last.then_inc(sig["level_t"].sem, sig["level_t"].count(1))
                if ck:
                    pe.wait_ge(sig["state_scaled"].sem, sig["state_scaled"].at(g + 1))
                for h in range(4):
                    out = bank(2 + h % 2)[:, (h // 2) * HEAD:(h // 2 + 1) * HEAD]
                    srow = scaled[HEAD * (h % 2):HEAD * (h % 2) + HEAD, 2 * g + h // 2, :]
                    if ck:
                        pe.matmul(out, rows(a, h), srow, start=True, stop=False)
                    last = pe.matmul(out, ak_t[:, h, :], tok[:, 2, h // 2, (h % 2) * HEAD:(h % 2 + 1) * HEAD], start=not ck, stop=True)
                last.then_inc(sig["c_sums"].sem, sig["c_sums"].count(1))
                pe.wait_ge(sig["c_sb"].sem, sig["c_sb"].at(n + 1))
                pe.wait_ge(sig["level_t_sb"].sem, sig["level_t_sb"].at((n + 1) * (LEVELS - 1)))
                for h in range(4):
                    last = pe.matmul(bank(6)[:, h * HEAD:(h + 1) * HEAD], tt[:, h, :], c_in[:, h, :], start=True, stop=True)
                last.then_inc(sig["u_sums"].sem, sig["u_sums"].count(1))
                pe.wait_ge(sig["u_sb"].sem, sig["u_sb"].at(n + 1))
                for h in range(4):
                    base, half = HEAD * (h % 2), slice((h % 2) * HEAD, (h % 2 + 1) * HEAD)
                    out = bank(4)[base:base + HEAD, (h // 2) * P:(h // 2 + 1) * P]
                    if ck:
                        pe.matmul(out, scaled[base:base + HEAD, 2 * g + h // 2, :], rows(r, h), start=True, stop=False)
                    pe.matmul(out, tok[:, 2, h // 2, half], rk_t[:, h, :], start=not ck, stop=False)
                    last = pe.matmul(out, u_[:, h, :], rb_t[:, h, :], start=False, stop=True)
                last.then_inc(sig["y_sums"].sem, sig["y_sums"].count(1))
                if not ck:
                    for h in range(4):
                        base, half = HEAD * (h % 2), slice((h % 2) * HEAD, (h % 2 + 1) * HEAD)
                        out = bank(5)[base:base + HEAD, (h // 2) * HEAD:(h // 2 + 1) * HEAD]
                        pe.matmul(out, tok[:, 0, h // 2, half], tok[:, 2, h // 2, half], start=True, stop=False)
                        last = pe.matmul(out, tok[:, 1, h // 2, half], u_[:, h, :], start=False, stop=True)
                    last.then_inc(sig["state_sums"].sem, sig["state_sums"].count(1))

        @block.scalar
        def _(act):
            for n, (ck, g) in enumerate(groups):
                act.wait_ge(sig["turned"].sem, sig["turned"].at(n + 1))
                act.activation(tok[:, 0:2, :, :].rearrange("p q c m -> p (q c m)"), bank(0), ACT.Copy)\
                    .then_inc(sig["turned_sb"].sem, sig["turned_sb"].count(1))
                act.activation(tok[:, 2, :, :].rearrange("p c m -> p (c m)"), bank(1)[:, 0:SEQ], ACT.Copy)\
                    .then_inc(sig["turned_sb"].sem, sig["turned_sb"].count(1))
                for level in range(1, LEVELS):
                    m = n * (LEVELS - 1) + level - 1
                    act.wait_ge(sig["level_x"].sem, sig["level_x"].at(m + 1))
                    if level > 1:
                        act.wait_ge(sig["level_t"].sem, sig["level_t"].at(m))
                    act.activation(x_, four(bank(7)), ACT.Copy).then_inc(sig["level_x_sb"].sem, sig["level_x_sb"].count(1))
                act.wait_ge(sig["c_sums"].sem, sig["c_sums"].at(n + 1))
                act.activation(
                    c_in.rearrange("p (c b) m -> p c b m", b=2),
                    core.psum[:, 2:4, 0:2 * HEAD].rearrange("p b (c m) -> p c b m", c=2), ACT.Copy)\
                    .then_inc(sig["c_sb"].sem, sig["c_sb"].count(1))
                act.wait_ge(sig["u_sums"].sem, sig["u_sums"].at(n + 1))
                act.activation(u_, bank(6)[:, 0:4 * HEAD].rearrange("p (h m) -> p h m", h=4), ACT.Copy)\
                    .then_inc(sig["u_sb"].sem, sig["u_sb"].count(1))

        @block.vector
        def _(dve):
            link = chain(core, dve, "dve")
            split = lambda x: x.rearrange("p (c b) t -> p c b t", b=2)
            each = lambda m: m.unsqueeze(1).unsqueeze(1).to_broadcast([P, 2, 2, P])
            pair = lambda q, which: core.psum[:, q:q + 2, :].rearrange("p b (c a t) -> p c b a t", c=2, a=2)[:, :, :, which, :]
            pair_ab = core.psum[:, 6:8, 0:2 * P].rearrange("p b (c t) -> p c b t", c=2)
            for n, (ck, g) in enumerate(groups):
                now = slice(ck * P, (ck + 1) * P)
                if ck:
                    for c in range(2):
                        last = dve.tensor_scalar(scaled[:, 2 * g + c, :], state[:, 2 * g + c, :],
                                                 e_mid[:, 2 * (2 * g + c) + ck:2 * (2 * g + c) + ck + 1], None, ALU.mult)
                    last.then_inc(sig["state_scaled"].sem, sig["state_scaled"].count(1))
                dve.wait_ge(sig["products"].sem, sig["products"].at(2 * n + 2))
                link(dve.tensor_tensor(split(ab_t), pair(2, 0), each(causal[:, 0, :]), ALU.mult))
                link(dve.tensor_tensor(split(ab), pair_ab, each(lower), ALU.mult))
                link(dve.tensor_tensor(split(t_), split(ab), each(below[:, 0, :]), ALU.mult))
                link(dve.tensor_tensor(split(tt), split(ab_t), each(above[:, 0, :]), ALU.mult))
                link(dve.tensor_tensor(split(t_), split(t_), each(ident), ALU.add))
                link(dve.tensor_tensor(split(tt), split(tt), each(ident), ALU.add))
                for level in range(1, LEVELS):
                    m = n * (LEVELS - 1) + level - 1
                    dve.tensor_tensor(split(masked), split(ab_t), each(above[:, level, :]), ALU.mult)\
                        .then_inc(sig["level_mask"].sem, sig["level_mask"].count(1))
                    if level == 1:
                        dve.tensor_tensor(split(rb_t), pair(2, 1), each(causal[:, 1, :]), ALU.mult)
                        dve.tensor_tensor(split(ak_t), pair(4, 0), each(causal[:, 0, :]), ALU.mult)
                        dve.tensor_tensor(split(rk_t), pair(4, 1), each(causal[:, 1, :]), ALU.mult)
                    dve.wait_ge(sig["level_t"].sem, sig["level_t"].at(m + 1))
                    dve.tensor_tensor(t_, t_, four(bank(0)), ALU.add)
                    dve.tensor_tensor(tt, tt, four(bank(1)), ALU.add)\
                        .then_inc(sig["level_t_sb"].sem, sig["level_t_sb"].count(1))
                dve.wait_ge(sig["y_sums"].sem, sig["y_sums"].at(n + 1))
                dve.tensor_copy(r[:, 2 * g:2 * g + 2, now], bank(4)[:, 0:SEQ].rearrange("p (c t) -> p c t", c=2))\
                    .then_inc(sig["y_sb"].sem, sig["y_sb"].count(1))
                if not ck:
                    dve.wait_ge(sig["state_sums"].sem, sig["state_sums"].at(n + 1))
                    for c in range(2):
                        last = dve.tensor_scalar(state[:, 2 * g + c, :], bank(5)[:, c * HEAD:(c + 1) * HEAD],
                                                 e_end[:, 2 * (2 * g + c):2 * (2 * g + c) + 1], None, ALU.mult)
                    last.then_inc(sig["state_sb"].sem, sig["state_sb"].count(1))
                    dve.wait_ge(sig["state_sb"].sem, sig["state_sb"].at(n + 1))
    core.end_stage()


def rwkv_norm_stage(core, n, y, cent, tmp, bonus, g, out):
    flat = lambda x: x.rearrange("p c t -> p (c t)")
    sums = lambda q: core.psum[:, 4 * q:4 * q + 4, :].rearrange("p b t -> p (b t)")
    with core.nc.Block() as block:
        mean, centered, squared, summed, scaled, rooted = (
            core.event(x) for x in ("mean_sum", "centered", "squared", "square_sum", "scaled", "rooted"))

        @block.tensor
        def _(pe):
            for c in range(KC):
                last = pe.matmul(sums(0)[:, c * SEQ:(c + 1) * SEQ], core.const("heads"), y[:, c, :], start=True, stop=True)
            last.then_inc(mean.sem, mean.count(1))
            pe.wait_ge(squared.sem, squared.at(1))
            for c in range(KC):
                last = pe.matmul(sums(1)[:, c * SEQ:(c + 1) * SEQ], core.const("heads"), tmp[:, c, :], start=True, stop=True)
            last.then_inc(summed.sem, summed.count(1))

        @block.scalar
        def _(act):
            act.wait_ge(centered.sem, centered.at(1))
            act.activation(flat(tmp), flat(cent), ACT.Square).then_inc(squared.sem, squared.count(1))
            act.wait_ge(scaled.sem, scaled.at(1))
            act.activation(flat(tmp), flat(tmp), ACT.Sqrt).then_inc(rooted.sem, rooted.count(1))

        @block.vector
        def _(dve):
            link = chain(core, dve, "dve")
            dve.wait_ge(mean.sem, mean.at(1))
            dve.scalar_tensor_tensor(flat(cent), sums(0), -1.0 / HEAD, flat(y), ALU.mult, ALU.add)\
                .then_inc(centered.sem, centered.count(1))
            dve.wait_ge(summed.sem, summed.at(1))
            dve.tensor_scalar(flat(tmp), sums(1), 1.0 / HEAD, GN_EPS, ALU.mult, ALU.add).then_inc(scaled.sem, scaled.count(1))
            dve.wait_ge(rooted.sem, rooted.at(1))
            link(dve.reciprocal(flat(tmp), flat(tmp)))
            link(dve.tensor_tensor(flat(cent), flat(cent), flat(tmp), ALU.mult))
            for c in range(KC):
                last = dve.tensor_scalar(cent[:, c, :], cent[:, c, :], core.col(f"ln_w{n}")[:, c:c + 1],
                                         core.col(f"ln_b{n}")[:, c:c + 1], ALU.mult, ALU.add)
            link(last)
            link(dve.tensor_tensor(flat(cent), flat(cent), flat(bonus), ALU.add))
            link(dve.tensor_tensor(flat(out), flat(cent), flat(g), ALU.mult))
    core.end_stage()


def rwkv(core, n):
    h, dx, r, k, v, lw, a, g = (core.buf(i) for i in (0, 1, 4, 5, 6, 7, 8, 9))
    xs = lambda i: core.buf(2 + i % 2)
    mu = lambda j: core.col(f"mu{n}")[:, j * KC:(j + 1) * KC]
    blocks = lambda name: [(f"{name}{n}", j) for j in range(KC)]
    low = lambda name, pieces=1: [(f"{name}{n}", j) for j in range(pieces)]
    jobs = [(mu(0), blocks("r"), None, (), r, ACT.Copy, "first"),
            (mu(2), blocks("k"), None, (), k, ACT.Copy, None),
            (mu(3), blocks("v"), None, (), v, ACT.Copy, None)]
    if n:
        jobs.append((None, low("v1"), ACT.Copy, low("v2"), a, ACT.Sigmoid, core.col("v01")))
    rwkv_projection_stage(core, jobs, h, dx, xs)
    if n:
        value_mix_stage(core, v, a, g, core.v_first)

    def keep_v(sync):
        s = core.event("v_first_stored")
        sync.dma_start(core.v_first, v).then_inc(s.sem, s.count(16))
        sync.wait_ge(s.sem, s.at(16))

    jobs = [(mu(1), low("w1"), ACT.Tanh, low("w2"), lw, ACT.Sigmoid, core.col(f"w0{n}")),
            (mu(4), low("a1"), ACT.Copy, low("a2"), a, ACT.Sigmoid, core.col(f"a0{n}")),
            (mu(5), low("g1", 2), ACT.Sigmoid, low("g2", 2), g, ACT.Copy, None)]
    rwkv_projection_stage(core, jobs, h, dx, xs, keep_v if n == 0 else None)
    rwkv_scale_stage(core, n, core.buf(0), core.buf(1), core.buf(2), core.buf(3), r, k, v, lw, a)
    rwkv_chunk_stage(core, r, k, v, core.buf(0), a, core.bufs[:, 1:3, :].rearrange("p b t -> p (b t)"), core.bufs[:, 7, :])
    rwkv_norm_stage(core, n, r, core.buf(1), core.buf(2), core.buf(3), g, core.buf(0))
    output_stage(core, f"o{n}", lambda c: core.buf(0)[:, c, :], KC, gated_residual(core))


def mamba_projection_stage(core, u, z, xbc, raw, dt_raw):
    z_pairs, pairs = MB_INNER // P // 2, (MB_INNER + MB_CONV_DIM) // P // 2
    raws = [raw[:, q * 2 * (SEQ + 3):(q + 1) * 2 * (SEQ + 3)].rearrange("p (c t) -> p c t", c=2) for q in range(3)]
    with core.nc.Block() as block:
        projected, evacuated, padded, raw_sb, convolved = (
            core.event(s) for s in ("projected", "evacuated", "padded", "raw_sb", "convolved"))

        def pair(g):
            return core.psum[:, g % 7, :].rearrange("p (c t) -> p c t", t=SEQ)

        @block.sync
        def _(sync):
            core.load_ahead(sync, ("mb_in", 2 * pairs))

        @block.tensor
        def _(pe):
            for g in range(pairs):
                if g >= 7:
                    pe.wait_ge(evacuated.sem, evacuated.at(g - 6))
                for c in range(2):
                    core.project(pe, ("mb_in", 2 * g + c), lambda k: u[:, k, :], pair(g)[:, c, :], projected)
            core.project(pe, ("mb_in", 2 * pairs), lambda k: u[:, k, :], core.psum[0:MB_HEADS, 7, 0:SEQ], projected, m=MB_HEADS)

        @block.scalar
        def _(act):
            def silu(q):
                act.wait_ge(convolved.sem, convolved.at(q + 1))
                act.activation(xbc[:, 2 * q:2 * q + 2, :], xbc[:, 2 * q:2 * q + 2, :], ACT.Silu)

            for g in range(pairs):
                act.wait_ge(projected.sem, projected.at(2 * g + 2))
                if g < z_pairs:
                    act.activation(z[:, 2 * g:2 * g + 2, :], pair(g), ACT.Silu).then_inc(evacuated.sem, evacuated.count(1))
                    continue
                q = g - z_pairs
                if q == 0:
                    act.wait_ge(padded.sem, padded.at(1))
                if q >= 3:
                    act.wait_ge(convolved.sem, convolved.at(q - 2))
                act.activation(raws[q % 3][:, :, 3:], pair(g), ACT.Copy).then_inc(evacuated.sem, evacuated.count(1))
                if q >= 1:
                    silu(q - 1)
            silu(pairs - z_pairs - 1)

        @block.vector
        def _(dve):
            link = chain(core, dve, "dve")
            for q in range(3):
                last = dve.memset(raws[q][:, :, 0:3], 0.0)
            last.then_inc(padded.sem, padded.count(1))
            w, bias = core.col("mb_conv_w"), core.col("mb_conv_b")
            for q in range(pairs - z_pairs):
                dve.wait_ge(evacuated.sem, evacuated.at(z_pairs + q + 1))
                for k in range(4):
                    for c in (2 * q, 2 * q + 1):
                        rows, column = raws[q % 3][:, c % 2, k:k + SEQ], w[:, 32 * k + c:32 * k + c + 1]
                        if k == 0:
                            last = dve.tensor_scalar(xbc[:, c, :], rows, column, bias[:, c:c + 1], ALU.mult, ALU.add)
                        else:
                            last = dve.scalar_tensor_tensor(xbc[:, c, :], rows, column, xbc[:, c, :], ALU.mult, ALU.add)
                    if k < 3:
                        link(last)
                last.then_inc(convolved.sem, convolved.count(1))
            dve.wait_ge(projected.sem, projected.at(2 * pairs + 1))
            dve.tensor_copy(dt_raw, core.psum[0:MB_HEADS, 7, 0:SEQ])
    core.end_stage()


def mamba_prepare_stage(core, x, b, x_tok, b_tok, work, dt_raw, acum, by_token):
    H = MB_HEADS
    rows = lambda q: work[0:H, q * SEQ:(q + 1) * SEQ]
    e, t, s, dt, decay, pos = (rows(q) for q in range(6))
    a_neg = core.small[0:H, 0:1]
    ident = core.const("ident")
    with core.nc.Block() as block:
        exp_in, exped, rate, acum_ready, decay_ready, dt_tokens, turned, turned_sb, dt_weight = (core.event(q) for q in (
            "exp_in", "exped", "rate", "acum_ready", "decay_ready", "dt_tokens", "turned", "turned_sb", "dt_weight"))
        groups = [(x, x_tok, ck, q) for ck in range(2) for q in range(4)] + [(b, b_tok, 0, q) for q in range(2)]

        @block.tensor
        def _(pe):
            for n, (src, dst, ck, q) in enumerate(groups):
                if n >= 7:
                    pe.wait_ge(turned_sb.sem, turned_sb.at(n - 6))
                for c in range(4):
                    last = pe.transpose(core.psum[:, n % 7, c * P:(c + 1) * P], src[:, 4 * q + c, ck * P:(ck + 1) * P], ident)
                last.then_inc(turned.sem, turned.count(1))
            pe.wait_ge(dt_weight.sem, dt_weight.at(1))
            for n, (src, ck) in enumerate(((dt, 0), (dt, 1), (acum, 0), (acum, 1), (pos, 0))):
                last = pe.transpose(core.psum[:, 7, n * H:(n + 1) * H], src[:, ck * P:(ck + 1) * P], ident[0:H, 0:H])
            last.then_inc(dt_tokens.sem, dt_tokens.count(1))

        @block.scalar
        def _(act):
            act.wait_ge(exp_in.sem, exp_in.at(1))
            act.activation(a_neg, core.col("mb_A_log")[0:H, :], ACT.Exp)
            act.activation(e, e, ACT.Exp).then_inc(exped.sem, exped.count(1))
            act.wait_ge(acum_ready.sem, acum_ready.at(1))
            act.activation(decay[:, 0:P], acum[:, 0:P], ACT.Exp, bias=acum[:, P - 1:P], scale=-1.0)\
                .then_inc(decay_ready.sem, decay_ready.count(1))
            for n, (src, dst, ck, q) in enumerate(groups):
                act.wait_ge(turned.sem, turned.at(n + 1))
                act.activation(dst[:, ck, 4 * q * P:4 * (q + 1) * P], core.psum[:, n % 7, :], ACT.Copy)\
                    .then_inc(turned_sb.sem, turned_sb.count(1))

        @block.vector
        def _(dve):
            link = chain(core, dve, "dve")
            link(dve.tensor_scalar(dt_raw, dt_raw, core.col("mb_dt_bias")[0:H, :], None, ALU.add))
            link(dve.tensor_scalar(pos, dt_raw, 0.0, None, ALU.max))
            dve.scalar_tensor_tensor(e, dt_raw, -1.0, dt_raw, ALU.mult, ALU.min).then_inc(exp_in.sem, exp_in.count(1))
            dve.wait_ge(exped.sem, exped.at(1))
            log1p_series(dve, link, dt, e, t, s)
            link(dve.tensor_tensor(dt, dt, pos, ALU.add))
            link(dve.tensor_scalar(t, dt, a_neg, -1.0, ALU.mult, ALU.mult))
            for ck in range(2):
                last = dve.tensor_tensor_scan(acum[:, ck * P:(ck + 1) * P], core.const("ones")[0:H, :], t[:, ck * P:(ck + 1) * P],
                                              0.0, ALU.mult, ALU.add)
            last.then_inc(acum_ready.sem, acum_ready.count(1))
            dve.wait_ge(decay_ready.sem, decay_ready.at(1))
            dve.tensor_tensor(pos[:, 0:P], dt[:, 0:P], decay[:, 0:P], ALU.mult).then_inc(dt_weight.sem, dt_weight.count(1))
            dve.wait_ge(dt_tokens.sem, dt_tokens.at(1))
            dve.tensor_copy(by_token, core.psum[:, 7, 0:5 * H])
    core.end_stage()


def mamba_scan_stage(core, x, z, b, c_, x_tok, b_tok, acum, by_token, part, state):
    H = MB_HEADS
    dt, ac = (by_token[:, q * 2 * H:(q + 1) * 2 * H].rearrange("p (a h) -> p a h", a=2) for q in range(2))
    weight = by_token[:, 4 * H:5 * H]
    m = part[:, 0:1024].rearrange("p (h a t) -> p h a t", h=4, a=2)
    cs = part[:, 1024:1536].rearrange("p (h t) -> p h t", h=4)
    cb = part[:, 1536:1792].rearrange("p (a t) -> p a t", a=2)
    xw = part[:, 1792:2048]
    upto = core.const("causal")[:, P:2 * P]
    with core.nc.Block() as block:
        names = ("cb_sums", "cb_sb", "row_sums", "diffs", "decays", "rows_exp", "cs_sb", "xw_sb", "state_sums", "state_sb", "m_sb", "y_sums", "y_sb")
        sig = {q: core.event(q) for q in names}
        rows = core.psum[:, 1:3, :].rearrange("p b (h a t) -> p (b h) a t", h=2, a=2)

        @block.tensor
        def _(pe):
            for g in range(MB_GROUPS):
                if g:
                    pe.wait_ge(sig["cb_sb"].sem, sig["cb_sb"].at(g))
                for a in range(2):
                    now = slice(a * P, (a + 1) * P)
                    last = pe.matmul(core.psum[:, 0, now], b[:, g, now], c_[:, g, now], start=True, stop=True)
                last.then_inc(sig["cb_sums"].sem, sig["cb_sums"].count(1))
                if g:
                    pe.wait_ge(sig["rows_exp"].sem, sig["rows_exp"].at(g))
                for h in range(4):
                    last = pe.matmul(rows[:, h, :, :], core.const("ident")[0:H, 4 * g + h:4 * g + h + 1].to_broadcast([H, P]), acum,
                                     start=True, stop=True)
                last.then_inc(sig["row_sums"].sem, sig["row_sums"].count(1))
                pe.wait_ge(sig["xw_sb"].sem, sig["xw_sb"].at(g + 1))
                if g:
                    pe.wait_ge(sig["state_sb"].sem, sig["state_sb"].at(g))
                pe.matmul(core.psum[:, 3, 0:4 * HEAD], b_tok[:, 0, g * P:(g + 1) * P], xw, start=True, stop=True)\
                    .then_inc(sig["state_sums"].sem, sig["state_sums"].count(1))
                pe.wait_ge(sig["m_sb"].sem, sig["m_sb"].at(g + 1))
                pe.wait_ge(sig["state_sb"].sem, sig["state_sb"].at(g + 1))
                if g:
                    pe.wait_ge(sig["y_sb"].sem, sig["y_sb"].at(g))
                for h in range(4):
                    base = HEAD * (h % 2)
                    xh = lambda a: x_tok[:, a, (4 * g + h) * HEAD:(4 * g + h + 1) * HEAD]
                    for a in range(2):
                        out = core.psum[base:base + HEAD, 4, (h // 2) * SEQ + a * P:(h // 2) * SEQ + (a + 1) * P]
                        last = pe.matmul(out, xh(a), m[:, h, a, :], start=True, stop=(a == 0))
                        if a:
                            last = pe.matmul(out, state[:, h * HEAD:(h + 1) * HEAD], cs[:, h, :], start=False, stop=True)
                last.then_inc(sig["y_sums"].sem, sig["y_sums"].count(1))

        @block.scalar
        def _(act):
            for g in range(MB_GROUPS):
                act.wait_ge(sig["diffs"].sem, sig["diffs"].at(g + 1))
                act.activation(m, m, ACT.Exp).then_inc(sig["decays"].sem, sig["decays"].count(1))
                if g:
                    act.wait_ge(sig["y_sums"].sem, sig["y_sums"].at(g))
                act.activation(cs, rows[:, :, 1, :], ACT.Exp).then_inc(sig["rows_exp"].sem, sig["rows_exp"].count(1))
                act.wait_ge(sig["state_sums"].sem, sig["state_sums"].at(g + 1))
                act.activation(state, core.psum[:, 3, 0:4 * HEAD], ACT.Copy)\
                    .then_inc(sig["state_sb"].sem, sig["state_sb"].count(1))

        @block.vector
        def _(dve):
            link = chain(core, dve, "dve")
            for g in range(MB_GROUPS):
                if g:
                    dve.wait_ge(sig["state_sums"].sem, sig["state_sums"].at(g))
                for h in range(4):
                    head = 4 * g + h
                    last = dve.tensor_scalar(xw[:, h * HEAD:(h + 1) * HEAD], x_tok[:, 0, head * HEAD:(head + 1) * HEAD],
                                             weight[:, head:head + 1], None, ALU.mult)
                last.then_inc(sig["xw_sb"].sem, sig["xw_sb"].count(1))
                dve.wait_ge(sig["cb_sums"].sem, sig["cb_sums"].at(g + 1))
                if g:
                    dve.wait_ge(sig["y_sums"].sem, sig["y_sums"].at(g))
                dve.tensor_tensor(cb, core.psum[:, 0, 0:SEQ].rearrange("p (a t) -> p a t", a=2),
                                                  upto.unsqueeze(1).to_broadcast([P, 2, P]), ALU.mult)\
                    .then_inc(sig["cb_sb"].sem, sig["cb_sb"].count(1))
                dve.wait_ge(sig["row_sums"].sem, sig["row_sums"].at(g + 1))
                for h in range(4):
                    for a in range(2):
                        last = dve.tensor_scalar(m[:, h, a, :], rows[:, h, a, :], ac[:, a, 4 * g + h:4 * g + h + 1], 0.0,
                                                 ALU.subtract, ALU.min)
                last.then_inc(sig["diffs"].sem, sig["diffs"].count(1))
                dve.wait_ge(sig["decays"].sem, sig["decays"].at(g + 1))
                dve.wait_ge(sig["cb_sb"].sem, sig["cb_sb"].at(g + 1))
                for h in range(4):
                    for a in range(2):
                        dve.scalar_tensor_tensor(m[:, h, a, :], m[:, h, a, :], dt[:, a, 4 * g + h:4 * g + h + 1], cb[:, a, :],
                                                 ALU.mult, ALU.mult)
                dve.wait_ge(sig["rows_exp"].sem, sig["rows_exp"].at(g + 1))
                dve.tensor_tensor(cs, cs, c_[:, g, P:SEQ].unsqueeze(1).to_broadcast([P, 4, P]), ALU.mult)\
                    .then_inc(sig["m_sb"].sem, sig["m_sb"].count(1))
                dve.wait_ge(sig["y_sums"].sem, sig["y_sums"].at(g + 1))
                y = core.psum[:, 4, :].rearrange("p (c t) -> p c t", c=2)
                for c in range(2):
                    last = dve.scalar_tensor_tensor(x[:, 2 * g + c, :], x[:, 2 * g + c, :], core.col("mb_D")[:, 2 * g + c:2 * g + c + 1],
                                                    y[:, c, :], ALU.mult, ALU.add)
                last.then_inc(sig["y_sb"].sem, sig["y_sb"].count(1))
                dve.wait_ge(sig["y_sb"].sem, sig["y_sb"].at(g + 1))
                link(dve.tensor_tensor(x[:, 2 * g:2 * g + 2, :], x[:, 2 * g:2 * g + 2, :], z[:, 2 * g:2 * g + 2, :], ALU.mult))
    core.end_stage()


def group_rms_stage(core, y, squares, roots):
    sums = core.psum[:, 0:4, :].rearrange("p b (g t) -> p (b g) t", t=SEQ)
    with core.nc.Block() as block:
        squared, summed, scaled, rooted = (core.event(s) for s in ("squared", "square_sum", "scaled", "rooted"))

        @block.scalar
        def _(act):
            for g in range(MB_GROUPS):
                act.activation(squares[:, 2 * g:2 * g + 2, :], y[:, 2 * g:2 * g + 2, :], ACT.Square)\
                    .then_inc(squared.sem, squared.count(1))
            act.wait_ge(scaled.sem, scaled.at(1))
            act.activation(roots, roots, ACT.Sqrt).then_inc(rooted.sem, rooted.count(1))

        @block.tensor
        def _(pe):
            for g in range(MB_GROUPS):
                pe.wait_ge(squared.sem, squared.at(g + 1))
                for c in range(2):
                    last = pe.matmul(sums[:, g, :], core.const("ones"), squares[:, 2 * g + c, :], start=(c == 0), stop=(c == 1))
            last.then_inc(summed.sem, summed.count(1))

        @block.vector
        def _(dve):
            link = chain(core, dve, "dve")
            dve.wait_ge(summed.sem, summed.at(1))
            dve.tensor_scalar(roots, sums, 1.0 / (2 * P), NORM_EPS, ALU.mult, ALU.add).then_inc(scaled.sem, scaled.count(1))
            dve.wait_ge(rooted.sem, rooted.at(1))
            link(dve.reciprocal(roots, roots))
            for c in range(2 * MB_GROUPS):
                dve.scalar_tensor_tensor(y[:, c, :], y[:, c, :], core.col("mb_norm_g")[:, c:c + 1], roots[:, c // 2, :], ALU.mult, ALU.mult)
    core.end_stage()


def mamba(core):
    u, z, x = core.buf(0), core.buf(1, 2), core.buf(3, 2)
    xbc = core.buf(3, 4)
    b, c_ = core.buf(5), core.buf(6)
    x_tok = core.bufs[:, 7:9, :]
    b_tok = core.bufs[:, 0:1, 0:1024]
    dt_raw, acum = core.state[0:MB_HEADS, 0, 0:SEQ], core.state[0:MB_HEADS, 0, SEQ:2 * SEQ]
    by_token, state = core.state[:, 1, 0:5 * MB_HEADS], core.state[:, 1, 5 * MB_HEADS:5 * MB_HEADS + 4 * HEAD]
    mamba_projection_stage(core, u, z, xbc, core.bufs[:, 9, :], dt_raw)
    mamba_prepare_stage(core, x, b, x_tok, b_tok, core.bufs[:, 9, :], dt_raw, acum, by_token)
    mamba_scan_stage(core, x, z, b, c_, x_tok, b_tok, acum, by_token, core.bufs[:, 9, :], state)
    group_rms_stage(core, x, core.buf(7, 2), core.buf(9))
    output_stage(core, "mb_out", lambda k: x[:, k, :], MB_INNER // P, gated_residual(core))


def layer_ffn(core, i, s):
    sub = 2 * s
    shift, scale, gate = (core.mod[:, (3 * sub + v) * KC:(3 * sub + v + 1) * KC] for v in range(3))
    adaln_stage(core, i, sub, core.buf(0))

    def residual(dve, link, y):
        link(dve.tensor_scalar(core.gain[:], gate, 0.5, None, ALU.mult))
        for c in range(KC):
            dve.scalar_tensor_tensor(core.x[:, c, :], y[:, c, :], core.gain[:, c:c + 1], core.x[:, c, :], ALU.mult, ALU.add)

    glu_stage(core, f"ffn{i}{s}", D_FF // GLU, core.buf(0), residual,
              ada=((i + 1, 5 * s, 5 - s) if i + 1 < DEPTH_2 else None))


def adaln_stage(core, i, sub, out):
    shift, scale = (core.mod[:, (3 * sub + v) * KC:(3 * sub + v + 1) * KC] for v in range(2))
    g = core.col(f"norm_g{i}")[:, sub * KC:(sub + 1) * KC]

    def pre(dve, link):
        link(dve.scalar_tensor_tensor(core.gain[:], scale, 1.0, g, ALU.add, ALU.mult))

    norm_stage(core, core.x, out, NORM_EPS, core.gain, shift, pre=pre)


def layer(core, i):
    ada_stage(core, i)
    layer_ffn(core, i, 0)
    adaln_stage(core, i, 1, core.buf(0))
    if i % 3 == 0:
        rwkv(core, i // 3)
    elif i % 3 == 1:
        mamba(core)
    else:
        window_attention(core)
    layer_ffn(core, i, 1)


def build(nc, place, fill, parts, stream, ada, cols, consts, rel_bias, x_in, out):
    core = Core(nc, stream, cols, consts, place, fill)
    core.rel_bias, core.ada = rel_bias, ada
    core.ada_sums = nc.dram_tensor("ada_sums", (9, P, D), F32, kind="Internal").ap()
    core.gates = nc.dram_tensor("gate_rows", (N_EXPERTS, SEQ), F32, kind="Internal").ap()
    core.scratch = nc.dram_tensor("bias_rows", (P, HEADS_A, 2 * SEQ), F32, kind="Internal").ap()
    core.v_first = nc.dram_tensor("v_first", (P, KC, SEQ), F32, kind="Internal").ap()
    setup_stage(core, x_in)
    if "first" in parts:
        first_block(core)
    for i in range(DEPTH_2):
        if f"L{i}" in parts:
            layer(core, i)
    store_stage(core, out)


PARTS = ("first", "L0", "L1", "L2", "L3")


def kernel(**inputs):
    import concourse.bacc as bacc
    from concourse.bass_utils import run_bass_kernel_spmd

    inp = {k: np.asarray(v) for k, v in inputs.items()}
    place, fill = place_weights()
    stream = np.zeros((len(fill), P, UNIT), np.float32)
    weights = weight_arrays(inp)
    for key, (unit, at, n, _) in place.items():
        stream[unit, :, at:at + n] = weights[key]
    del weights
    arrays = {
        "stream": stream,
        "ada": ada_array(inp),
        "cols": column_array(inp),
        "consts": const_array(),
        "rel_bias": np.ascontiguousarray(inp["rel_bias"]),
        "x_in": np.ascontiguousarray(inp["x"][0].T),
    }
    nc = bacc.Bacc("TRN2", target_bir_lowering=False, num_devices=1)
    aps = {n: nc.dram_tensor(n, a.shape, F32, kind="ExternalInput").ap() for n, a in arrays.items()}
    out = nc.dram_tensor("out", (D, SEQ), F32, kind="ExternalOutput").ap()
    build(nc, place, fill, PARTS, out=out, **aps)
    result = run_bass_kernel_spmd(nc, [arrays], core_ids=[0])
    return np.ascontiguousarray(result.results[0]["out"].T)[None]
```

```python
from contextlib import ExitStack

import numpy as np

import concourse.bass as bass
from concourse import mybir

P = 128
SEQ = 256
D = 1024
KC = D // P
D_LRU, D_ATTN = 512, 512
HEADS_A, HEAD = 8, 64
REL_BUCKETS, REL_MAX_DIST = 32, 128
N_GROUPS, PER_GROUP = 4, 8
N_EXPERTS = N_GROUPS * PER_GROUP
D_EXPERT = 256
DEPTH_2, N_SUB = 4, 3
D_FF = 2816
GLU = 256
LN_EPS, NORM_EPS, GN_EPS = 1e-5, 1e-6, 64e-5
ALPHA = 2.0 ** 0.25
RW_HEADS = D // HEAD
MB_INNER, MB_GROUPS, MB_STATE, MB_HEADS = 2 * D, 8, 128, 32
MB_CONV_DIM = MB_INNER + 2 * MB_GROUPS * MB_STATE
SW_Q, SW_KV = 16, 4
NEG = -1e30
SLOTS, UNIT = 4, 6144
LEVELS = 7

F32 = mybir.dt.float32
ALU = mybir.AluOpType
ACT = mybir.ActivationFunctionType
AX = mybir.AxisListType.X



def columns_of_blocks(w, n=P):
    k, cols = w.shape
    kc = k // P
    out = []
    for c in range(0, cols, n):
        m = min(n, cols - c)
        out.append(w[:, c:c + m].reshape(kc, P, m).transpose(1, 0, 2).reshape(P, kc * m))
    return out


def rows_padded(w):
    out = np.zeros((P, w.shape[1]), w.dtype)
    out[:w.shape[0]] = w
    return out


def glu_unit(wa, wb, wo):
    down = wo.reshape(2, P, D).transpose(1, 0, 2).reshape(P, 2 * D)
    return np.concatenate(columns_of_blocks(wa) + columns_of_blocks(wb) + [down], axis=1)


def weight_plan():
    plan = []

    def blocks(name, k, cols):
        for j in range(0, cols, P):
            plan.append(((name, j // P), k // P * min(P, cols - j)))

    blocks("w_in", D, 2 * D_LRU + 3 * D_ATTN)
    plan += [(("gate_a", 0), D_LRU), (("gate_x", 0), D_LRU)]
    blocks("w_out", D, D)
    plan.append((("router", 0), KC * (N_GROUPS + N_EXPERTS)))
    plan.append(("unit", 0))
    for e in range(N_EXPERTS):
        plan.append((("moe", e), UNIT))
    for i in range(DEPTH_2):
        for j in range(D_FF // GLU):
            plan.append(((f"ffn{i}0", j), UNIT))
        if i % 3 == 0:
            n = i // 3
            blocks(f"r{n}", D, D)
            blocks(f"k{n}", D, D)
            blocks(f"v{n}", D, D)
            if n:
                blocks(f"v1{n}", D, 32)
                plan.append(((f"v2{n}", 0), D))
            blocks(f"w1{n}", D, 64)
            plan.append(((f"w2{n}", 0), D))
            blocks(f"a1{n}", D, 64)
            plan.append(((f"a2{n}", 0), D))
            blocks(f"g1{n}", D, 160)
            plan.append(((f"g2{n}", 0), D))
            plan.append(((f"g2{n}", 1), D))
            plan.append(("unit", 0))
            blocks(f"o{n}", D, D)
        elif i % 3 == 1:
            blocks("mb_in", D, 2 * MB_INNER + 2 * MB_GROUPS * MB_STATE + MB_HEADS)
            blocks("mb_out", MB_INNER, D)
        else:
            blocks("sw_qkv", D, (SW_Q + 2 * SW_KV) * HEAD)
            blocks("sw_o", D, D)
        plan.append(("unit", 0))
        for j in range(D_FF // GLU):
            plan.append(((f"ffn{i}1", j), UNIT))
    return plan


def place_weights(plan=None):
    place, fill, last = {}, [], {}
    full = True
    for key, n in plan or weight_plan():
        if key == "unit":
            full = True
            continue
        if full or fill[-1] + n > UNIT:
            fill.append(0)
            full = False
        place[key] = (len(fill) - 1, fill[-1], n)
        last[len(fill) - 1] = key
        fill[-1] += n
    return {k: (*v, last[v[0]] == k) for k, v in place.items()}, fill


def weight_arrays(inp):
    out = {}

    def blocks(name, w):
        for j, a in enumerate(columns_of_blocks(w)):
            out[(name, j)] = a

    blocks("w_in", inp["w_in"][0])
    blocks("w_out", inp["w_out"][0])
    for key in ("gate_a", "gate_x"):
        w = np.zeros((P, D_LRU // P, P), np.float32)
        for b in range(D_LRU // HEAD):
            rows = slice(HEAD * (b % 2), HEAD * (b % 2) + HEAD)
            w[rows, b // 2, rows] = inp["w_" + key][0, b]
        out[(key, 0)] = w.reshape(P, -1)
    router = np.concatenate([inp["w_router_group"][0], inp["w_router_expert"][0]], axis=1)
    out[("router", 0)] = columns_of_blocks(router)[0]
    for e in range(N_EXPERTS):
        out[("moe", e)] = glu_unit(inp["w1"][0, e], inp["w3"][0, e], inp["w2"][0, e])
    for i in range(DEPTH_2):
        for s in range(2):
            wi, wo = inp["ffn_w_in_2"][i, s], inp["ffn_w_out_2"][i, s]
            for j in range(D_FF // GLU):
                a = slice(j * GLU, (j + 1) * GLU)
                b = slice(D_FF + j * GLU, D_FF + (j + 1) * GLU)
                out[(f"ffn{i}{s}", j)] = glu_unit(wi[:, a], wi[:, b], wo[a])
    for n in range(2):
        for j, name in enumerate("rkv"):
            blocks(f"{name}{n}", inp["rw_w_rkv_2"][n, j])
        blocks(f"o{n}", inp["rw_w_o_2"][n])
        for name, up, down in (("w", "rw_w1_2", "rw_w2_2"), ("a", "rw_a1_2", "rw_a2_2"), ("g", "rw_g1_2", "rw_g2_2")):
            blocks(f"{name}1{n}", inp[up][n])
            for j in range(0, inp[down].shape[1], P):
                out[(f"{name}2{n}", j // P)] = rows_padded(inp[down][n, j:j + P])
    blocks("v11", inp["rw_v1_2"][0])
    out[("v21", 0)] = rows_padded(inp["rw_v2_2"][0])
    blocks("mb_in", inp["mb_w_in_2"][0])
    blocks("mb_out", inp["mb_w_out_2"][0])
    blocks("sw_qkv", inp["sw_w_qkv_2"][0])
    blocks("sw_o", inp["sw_w_o_2"][0])
    return out


def ada_array(inp):
    out = [inp["w_ada"][0]] + [inp["ada_w_2"][i] for i in range(DEPTH_2)]
    return np.concatenate([w.reshape(2, 4, P, -1, D).transpose(3, 0, 2, 1, 4).reshape(-1, P, 4 * D) for w in out])


def column_plan():
    sizes = [("c", KC), ("b_ada", 48), ("conv_w", 16), ("conv_b", 4), ("b_gate_a", 4), ("b_gate_x", 4), ("lam", 4),
             ("norm_lru_g", 4), ("norm_attn_g", 4), ("ln1_g", KC), ("ln1_b", KC), ("ln2_g", KC), ("ln2_b", KC),
             ("c_2", KC)]
    for i in range(DEPTH_2):
        sizes += [(f"ada_b{i}", 9 * KC), (f"norm_g{i}", N_SUB * KC)]
    for n in range(2):
        sizes += [(f"mu{n}", 6 * KC)] + [(f"{v}{n}", KC) for v in ("w0", "a0", "v0", "k_k", "k_a", "r_k", "ln_w", "ln_b")]
    sizes += [("mb_conv_w", 4 * 32), ("mb_conv_b", 32), ("mb_dt_bias", 1), ("mb_A_log", 1), ("mb_D", 16),
              ("mb_norm_g", 16), ("q_norm", 1), ("k_norm", 1), ("sinks", SW_Q),
              ("router_b", N_GROUPS + N_EXPERTS)]
    place, at = {}, 0
    for name, n in sizes:
        place[name] = (at, n)
        at += n
    return place, at


def column_array(inp):
    place, total = column_plan()
    out = np.zeros((P, total), np.float32)

    def put(name, v):
        at, n = place[name]
        v = np.asarray(v)
        if v.size == n * P:
            out[:, at:at + n] = v.reshape(n, P).T
        else:
            out[:v.size, at] = v.reshape(-1)

    for name in ("c", "c_2"):
        put(name, inp[name])
    for name in ("b_ada", "conv_w", "conv_b", "b_gate_a", "b_gate_x", "norm_lru_g", "norm_attn_g", "ln1_g", "ln1_b",
                 "ln2_g", "ln2_b"):
        put(name, inp[name][0])
    put("lam", inp["lru_lambda"][0])
    for i in range(DEPTH_2):
        put(f"ada_b{i}", inp["ada_b_2"][i])
        put(f"norm_g{i}", inp["norm_g_2"][i])
    for n in range(2):
        put(f"mu{n}", inp["rw_mu_2"][n])
        for v in ("w0", "a0", "k_k", "k_a", "r_k", "ln_w", "ln_b"):
            put(f"{v}{n}", inp[f"rw_{v}_2"][n])
    put("v01", inp["rw_v0_2"][0])
    put("mb_conv_w", inp["mb_conv_w_2"][0])
    put("mb_conv_b", inp["mb_conv_b_2"][0])
    put("mb_dt_bias", inp["mb_dt_bias_2"][0])
    put("mb_A_log", inp["mb_A_log_2"][0])
    put("mb_D", np.repeat(inp["mb_D_2"][0], HEAD))
    put("mb_norm_g", inp["mb_norm_g_2"][0])
    put("q_norm", np.tile(inp["sw_q_norm_2"][0], 2))
    put("k_norm", np.tile(inp["sw_k_norm_2"][0], 2))
    at, n = place["router_b"]
    out[0, at:at + n] = np.concatenate([inp["b_router_group"][0], inp["b_router_expert"][0]])
    put("sinks", np.repeat(inp["sw_sinks_2"][0], P))
    return out


def const_plan():
    sizes = [("ident", P), ("ones", P), ("heads", P), ("below", LEVELS * P), ("above", LEVELS * P),
             ("causal", 2 * P), ("zeros", P), ("slide", 2 * RW_HEADS - 2),
             ("band", 2 * SEQ), ("buckets", 2 * SEQ)]
    place, at = {}, 0
    for name, n in sizes:
        place[name] = (at, n)
        at += n
    return place, at


def const_array():
    place, total = const_plan()
    out = np.zeros((P, total), np.float32)

    def put(name, v):
        at, n = place[name]
        out[:v.shape[0], at:at + v.shape[1]] = v

    i = np.arange(P)
    put("ident", np.eye(P))
    put("ones", np.ones((P, P)))
    put("heads", (i[:, None] // HEAD == i[None, :] // HEAD).astype(np.float32))
    below = []
    for level in range(LEVELS):
        half = 1 << level
        row, col = i[:, None], i[None, :]
        below.append((row // (2 * half) == col // (2 * half)) & (row % (2 * half) >= half) & (col % (2 * half) < half))
    put("below", np.concatenate(below, axis=1).astype(np.float32))
    put("above", np.concatenate([b.T for b in below], axis=1).astype(np.float32))
    slide = np.zeros((P, 2 * RW_HEADS - 2))
    slide[np.arange(P), RW_HEADS - 2 + np.arange(P) // HEAD] = 1.0
    put("slide", slide)
    put("causal", np.concatenate([i[:, None] < i[None, :], i[:, None] <= i[None, :]], axis=1).astype(np.float32))
    band = np.zeros((P, 2, SEQ), np.float32)
    for t in range(2):
        rel = (t * P + i)[:, None] - np.arange(SEQ)[None, :]
        band[:, t] = np.where((rel >= 0) & (rel < P), 0.0, NEG)
    put("band", band.reshape(P, -1))
    dist = (SEQ - 1) - np.arange(2 * SEQ)
    n = np.maximum(dist, 0)
    exact = REL_BUCKETS // 2
    far = np.log(np.maximum(n, 1).astype(np.float32) / np.float32(exact)).astype(np.float32)
    far = (far / np.float32(np.log(REL_MAX_DIST / exact)) * np.float32(REL_BUCKETS - exact)).astype(np.int32)
    bucket = np.where(n < exact, n, np.minimum(exact + far, REL_BUCKETS - 1))
    hot = np.zeros((REL_BUCKETS + 1, 2 * SEQ), np.float32)
    hot[bucket, np.arange(2 * SEQ)] = (dist >= 0)
    hot[REL_BUCKETS] = np.where(dist < 0, NEG, 0.0)
    put("buckets", hot)
    return out



class Event:

    def __init__(self, nc, name):
        self.sem = nc.semaphore(name).__enter__()
        self.before = 0
        self.made = 0

    def count(self, n):
        self.made += n
        return n

    def at(self, k):
        return self.before + k


class Core:

    def __init__(self, nc, stream, cols_dram, consts_dram, place, fill):
        self.nc, self.stream, self.place, self.fill = nc, stream, place, fill
        self.cols_dram, self.consts_dram = cols_dram, consts_dram
        sb = lambda name, shape: nc.alloc_sbuf_tensor(name, shape, F32)
        self.ring = sb("ring", [P, SLOTS, UNIT])
        self.x = sb("x_sb", [P, KC, SEQ])
        at = nc.sbuf_base
        self.bufs = sb("bufs", [P, 10, 2048])
        split = lambda name, buffer, shape: nc.alloc_sbuf_tensor_at(name, shape, mybir.dt.float32r, offset=at + 8192 * buffer)
        self.h_split = split("h_split", 0, [P, 2, 2, 2, SEQ])
        self.u_split = split("u_split", 1, [P, 2, KC, SEQ])
        self.w_split = split("w_split", 3, [P, 3, 2, D])
        self.consts = sb("consts_sb", [P, const_plan()[0]["band"][0]])
        self.cols = sb("cols_sb", [P, column_plan()[1]])
        self.mod = sb("mod", [P, 9 * KC])
        self.c_act = sb("c_act", [P, 2 * KC])
        self.gain = sb("gain", [P, KC])
        self.rstd = sb("rstd", [P, SEQ])
        self.small = sb("small", [P, 704])
        self.state = sb("state", [P, 2, 512])
        self.narrow = self.state[:, 0, :].rearrange("p (b t) -> p b t", b=2)
        self.psum = nc.alloc_psum_tensor("banks", [P, 8, 512], F32)
        self.names = {}
        self.loaded_units = 0
        self.loaded = [Event(nc, f"unit_loaded{s}") for s in range(SLOTS)]
        self.freed = Event(nc, "unit_freed")

    def buf(self, i, n=1):
        return self.bufs[:, i:i + n, :].rearrange("p b (c t) -> p (b c) t", t=SEQ)

    def const(self, name):
        at, n = const_plan()[0][name]
        return self.consts[:, at:at + n]

    def load_const(self, sync, name, dst):
        at, n = const_plan()[0][name]
        s = self.event("constant_loaded")
        sync.dma_start(dst, self.consts_dram[:, at:at + n]).then_inc(s.sem, s.count(16))
        sync.wait_ge(s.sem, s.made)

    def col(self, name):
        at, n = column_plan()[0][name]
        return self.cols[:, at:at + n]

    def event(self, name):
        if name not in self.names:
            self.names[name] = Event(self.nc, name)
        return self.names[name]

    def end_stage(self):
        for s in self.names.values():
            s.before = s.made


    def load_ahead(self, sync, upto_key, upto=0, after=None):
        if upto_key:
            upto = min(len(self.fill), self.place[upto_key][0] + SLOTS)
        for u in range(self.loaded_units, upto):
            if u >= SLOTS:
                sync.wait_ge(self.freed.sem, u - SLOTS + 1)
            n = self.fill[u]
            sync.dma_start(self.ring[:, u % SLOTS, 0:n], self.stream[u, :, 0:n])\
                .then_inc(self.loaded[u % SLOTS].sem, self.loaded[u % SLOTS].count(16))
            if after:
                after(u - SLOTS)
        self.loaded_units = max(self.loaded_units, upto)

    def weights(self, pe, key):
        unit, at, n, _ = self.place[key]
        pe.wait_ge(self.loaded[unit % SLOTS].sem, 16 * (unit // SLOTS + 1))
        return self.ring[:, unit % SLOTS, at:at + n]

    def used(self, pe, key, instruction, done=None):
        last_of_unit = self.place[key][3]
        if done:
            instruction.then_inc(done.sem, done.count(1))
            if last_of_unit:
                pe.wait_ge(done.sem, done.made)
                pe.nop().then_inc(self.freed.sem, self.freed.count(1))
        elif last_of_unit:
            instruction.then_inc(self.freed.sem, self.freed.count(1))

    def project(self, pe, key, rhs, out, done=None, kcs=KC, m=P):
        w = self.weights(pe, key).rearrange("p (k m) -> p k m", k=kcs)
        for k in range(kcs):
            last = pe.matmul(out, w[:, k, :], rhs(k), start=(k == 0), stop=(k == kcs - 1))
        self.used(pe, key, last, done)


def chain(core, eng, name):
    s = core.event(f"{name}_step")

    def link(instruction):
        instruction.then_inc(s.sem, s.count(1))
        eng.wait_ge(s.sem, s.made)
        return instruction
    return link


def setup_stage(core, x_in):
    with core.nc.Block() as block:
        @block.sync
        def _(sync):
            s = core.event("setup_loaded")
            sync.dma_start(core.consts[:], core.consts_dram[:, 0:const_plan()[0]["band"][0]]).then_inc(s.sem, s.count(16))
            sync.dma_start(core.cols[:], core.cols_dram).then_inc(s.sem, s.count(16))
            sync.dma_start(core.x[:], x_in.rearrange("(c p) t -> p c t", p=P)).then_inc(s.sem, s.count(16))
            sync.wait_ge(s.sem, s.at(48))
    core.end_stage()


def store_stage(core, out):
    with core.nc.Block() as block:
        @block.sync
        def _(sync):
            s = core.event("stored")
            sync.dma_start(out.rearrange("(c p) t -> p c t", p=P), core.x[:]).then_inc(s.sem, s.count(16))
            sync.wait_ge(s.sem, s.at(16))
    core.end_stage()


def ada_columns(core, pe, sums, n):
    for j in range(n):
        for half in range(2):
            at = j * P + half * HEAD
            last = pe.matmul(core.psum[half * HEAD:(half + 1) * HEAD, 0, j:j + 1], sums[:, at:at + HEAD],
                             core.const("ones")[:, 0:1], start=True, stop=True)
    return last


def ada_quarter(core, dve, half, q, slot, sums, c_act, step):
    done = core.event("ada_step")
    k, w = 4 * half + q, slot[:, q * D:(q + 1) * D]
    if k == 0:
        e = dve.tensor_scalar(sums, w, c_act[:, 0:1], None, ALU.mult)
    else:
        dve.wait_ge(done.sem, done.at(step + q))
        e = dve.scalar_tensor_tensor(sums, w, c_act[:, k:k + 1], sums, ALU.mult, ALU.add)
    e.then_inc(done.sem, 1)


def ada_accumulate(core, dve, half, slot, sums, c_act, step):
    for q in range(4):
        ada_quarter(core, dve, half, q, slot, sums, c_act, step)


def first_ada_stage(core):
    ranges = 6
    slots = [core.bufs[:, 2 * q:2 * q + 2, :].rearrange("p b n -> p (b n)") for q in range(3)]
    sums = core.bufs[:, 6:9, :].rearrange("p b n -> p (b n)")
    with core.nc.Block() as block:
        silu_ready, products, step = core.event("c_silu"), core.event("ada_products"), core.event("ada_step")
        loaded = [core.event(f"ada_first_loaded{q}") for q in range(3)]

        @block.sync
        def _(sync):
            for k in range(2 * ranges):
                if k >= 3:
                    sync.wait_ge(step.sem, step.at(4 * (k - 2)))
                sync.dma_start(slots[k % 3], core.ada[k, :, :]).then_inc(loaded[k % 3].sem, loaded[k % 3].count(16))
            core.load_ahead(sync, None, SLOTS)

        @block.scalar
        def _(act):
            act.activation(core.c_act[:, 0:KC], core.col("c"), ACT.Silu).then_inc(silu_ready.sem, silu_ready.count(1))
            act.activation(core.c_act[:, KC:], core.col("c_2"), ACT.Silu).then_inc(silu_ready.sem, silu_ready.count(1))

        @block.vector
        def _(dve):
            dve.wait_ge(silu_ready.sem, silu_ready.at(2))
            for k in range(2 * ranges):
                dve.wait_ge(loaded[k % 3].sem, loaded[k % 3].at(16 * (k // 3 + 1)))
                ada_accumulate(core, dve, k % 2, slots[k % 3], sums[:, (k // 2) * D:(k // 2 + 1) * D], core.c_act[:, 0:KC], 4 * k)
            dve.wait_ge(products.sem, products.at(1))
            dve.tensor_tensor(core.mod[:, 0:6 * KC], core.psum[:, 0, 0:6 * KC], core.col("b_ada"), ALU.add)

        @block.tensor
        def _(pe):
            pe.wait_ge(step.sem, step.at(8 * ranges))
            ada_columns(core, pe, sums, 6 * KC).then_inc(products.sem, products.count(1))

        step.made += 8 * ranges
    core.end_stage()


def ada_stage(core, i):
    n = 9
    sums = core.bufs[:, 0:5, :].rearrange("p b n -> p (b n)")[:, 0:n * D]
    with core.nc.Block() as block:
        products, read = core.event("ada_products"), core.event("ada_sums_read")

        @block.sync
        def _(sync):
            sync.dma_start(sums.rearrange("p (r n) -> p r n", r=n), core.ada_sums.rearrange("r p n -> p r n"))\
                .then_inc(read.sem, read.count(16))

        @block.tensor
        def _(pe):
            pe.wait_ge(read.sem, read.at(16))
            ada_columns(core, pe, sums, n * KC).then_inc(products.sem, products.count(1))

        @block.vector
        def _(dve):
            dve.wait_ge(products.sem, products.at(1))
            dve.tensor_tensor(core.mod[:, 0:n * KC], core.psum[:, 0, 0:n * KC], core.col(f"ada_b{i}"), ALU.add)
    core.end_stage()


def norm_stage(core, src, out, eps, gain, shift=None, center=False, n=KC, ones="ones", sub_g=1.0, pre=None, next_key=None):
    count = float(n * P)
    ones = core.const(ones)
    with core.nc.Block() as block:
        centered, squared, summed, meaned = (core.event(s) for s in ("centered", "squared", "square_sum", "mean_sum"))
        root, scaled = core.event("root"), core.event("scaled")
        squares = core.buf(9)

        @block.tensor
        def _(pe):
            if center:
                for c in range(n):
                    last = pe.matmul(core.psum[:, 0, 0:SEQ], ones, src[:, c, :], start=(c == 0), stop=(c == n - 1))
                last.then_inc(meaned.sem, meaned.count(1))
            for c in range(n):
                pe.wait_ge(squared.sem, squared.at(c + 1))
                last = pe.matmul(core.psum[:, 1, 0:SEQ], ones, squares[:, c, :], start=(c == 0), stop=(c == n - 1))
            last.then_inc(summed.sem, summed.count(1))

        @block.scalar
        def _(act):
            for c in range(n):
                if center:
                    act.wait_ge(centered.sem, centered.at(c + 1))
                act.activation(squares[:, c, :], (out if center else src)[:, c, :], ACT.Square)\
                    .then_inc(squared.sem, squared.count(1))
            act.wait_ge(scaled.sem, scaled.at(1))
            act.activation(core.rstd[:], core.rstd[:], ACT.Sqrt).then_inc(root.sem, root.count(1))
            if shift is not None:
                for c in range(n):
                    act.wait_ge(scaled.sem, scaled.at(2 + c))
                    act.activation(out[:, c, :], out[:, c, :], ACT.Identity, bias=shift[:, c:c + 1])

        @block.vector
        def _(dve):
            link = chain(core, dve, "dve")
            if pre:
                pre(dve, link)
            if center:
                dve.wait_ge(meaned.sem, meaned.at(1))
                for c in range(n):
                    dve.scalar_tensor_tensor(out[:, c, :], core.psum[:, 0, 0:SEQ], -1.0 / count, src[:, c, :],
                                                         ALU.mult, ALU.add)\
                        .then_inc(centered.sem, centered.count(1))
            dve.wait_ge(summed.sem, summed.at(1))
            dve.tensor_scalar(core.rstd[:], core.psum[:, 1, 0:SEQ], 1.0 / count, eps, ALU.mult, ALU.add)\
                .then_inc(scaled.sem, scaled.count(1))
            dve.wait_ge(root.sem, root.at(1))
            link(dve.reciprocal(core.rstd[:], core.rstd[:]))
            for c in range(n):
                if center:
                    dve.wait_ge(centered.sem, centered.at(c + 1))
                dve.scalar_tensor_tensor(out[:, c, :], (out if center else src)[:, c, :], gain[:, c:c + 1],
                                                   core.rstd[:], ALU.mult, ALU.mult)\
                    .then_inc(scaled.sem, scaled.count(1))
    core.end_stage()


def glu_stage(core, key, n, src, residual, gates=None, ada=None):
    nc = core.nc
    unit0 = core.place[(key, 0)][0]
    zeros, anything = core.const("zeros"), core.const("below")[:, 0:512]
    work = core.bufs[:, 8, :]
    silu_a = [work[:, q * 512:(q + 1) * 512].rearrange("p (f t) -> p f t", t=SEQ) for q in range(2)]
    h_full = work[:, 1024:1536].rearrange("p (f t) -> p f t", t=SEQ)
    gate_rows = [work[:, 1536 + q * SEQ:1536 + (q + 1) * SEQ] for q in range(2)]
    y = core.psum[:, 4:8, :].rearrange("p b (c t) -> p (b c) t", t=SEQ)
    u_split, w_split, h_split = core.u_split, core.w_split, core.h_split
    with nc.Block() as block:
        u_high, u_low, high, low, piece_used, act_done, gated, h_ready, h_high, h_low = (core.event(s) for s in (
            "u_high", "u_low", "w_high", "w_low", "piece_used", "glu_silu", "glu_gated", "glu_hidden", "h_high", "h_low"))
        gate_loaded = [core.event(f"gate_loaded{q}") for q in range(2)]
        step, ada_loaded = core.event("ada_step"), [core.event(f"ada_loaded{q}") for q in range(4)]
        sums_free = [core.event(f"ada_sums_free{q}") for q in range(2)]
        layer, range0, ranges = ada or (0, 0, 0)
        half0 = 2 * (6 + 9 * layer + range0)
        ada_slot = core.bufs[:, 6:8, :].rearrange("p b n -> p (b n)")
        ada_sums = [core.bufs[:, 9, q * D:(q + 1) * D] for q in range(2)]
        turns = (n - 2) // 4
        ada_turns = min(turns, ranges // 2)
        rest = n - 2 - 4 * turns
        assert ranges - 2 * ada_turns in (0, 1) and (ranges == 2 * ada_turns or rest)

        def half(j, which):
            return core.psum[:, 2 * (j % 2) + which, :].rearrange("p (f t) -> p f t", t=SEQ)

        def in_turns(eng, unit):
            for first, last, with_ada in ((0, ada_turns, True), (ada_turns, turns, False)):
                if first < last:
                    with eng.Fori(first, last) as turn:
                        for j in range(4):
                            unit(2 + j, turn * 4 + (2 + j), (turn * 4 + j) if with_ada else None)
            for j in range(n - rest, n):
                unit(j, j, 2 * ranges - 2 if ranges % 2 and j == n - 1 else None)

        def up_piece(at, b):
            return at * 6 + (b - 2)

        def down_piece(at, f):
            return at * 6 + (f + 2)

        def piece(j, b):
            return core.ring[:, (unit0 + j) % SLOTS, b * D:(b + 1) * D]

        @block.sync
        def _(sync):
            stored = [0]

            def store(unit, upto=2 * ada_turns):
                while stored[0] < upto and unit >= unit0 + 3 + 2 * stored[0]:
                    q = stored[0]
                    sync.wait_ge(step.sem, step.at(8 * (q + 1)))
                    sync.dma_start(core.ada_sums[range0 + q, :, :], ada_sums[q % 2])\
                        .then_inc(sums_free[q % 2].sem, sums_free[q % 2].count(16))
                    stored[0] += 1

            if ranges:
                for free in sums_free:
                    sync.nop().then_inc(free.sem, free.count(16))
            core.load_ahead(sync, (key, n - 1), after=store)
            store(unit0 + 2 * ranges + 4, ranges)
            if ranges:
                for free in sums_free:
                    sync.wait_ge(free.sem, free.made)

        @block.tensor
        def _(pe):
            def three(out, w, x, start, stop):
                pe.matmul(out, w(0), x(0), start=start, stop=False, skip_group_check=True)
                pe.matmul(out, w(0), x(1), start=False, stop=False, skip_group_check=True)
                return pe.matmul(out, w(1), x(0), start=False, stop=stop, skip_group_check=True)

            def up_products(j, at, ada_half=None):
                if j >= 2:
                    pe.wait_ge(h_ready.sem, h_ready.at(at - 1))
                for b in range(4):
                    number = b if j == 0 else up_piece(at, b)
                    slot = b % 3 if j == 0 else (b + 1) % 3
                    pe.wait_ge(low.sem, low.at(number + 1))
                    for k in range(KC):
                        if j == 0 and b == 0 and k % 2 == 0:
                            pe.wait_ge(u_low.sem, u_low.at(k // 2 + 1))
                        last = three(half(j, b // 2)[:, b % 2, :], lambda part: w_split[:, slot, part, k * P:(k + 1) * P],
                                     lambda part: u_split[:, part, k, :], start=(k == 0), stop=(k == KC - 1))
                    last.then_inc(piece_used.sem, 1)

            def down_products(j, at, last_unit=False):
                pe.wait_ge(h_low.sem, h_low.at(at))
                for f in range(2):
                    slot = (f + 1) % 3 if last_unit else (f + 2) % 3
                    number = 6 * n - 2 + f if last_unit else down_piece(at, f)
                    pe.wait_ge(low.sem, low.at(number + 1))
                    for c in range(KC):
                        last = three(y[:, c, :], lambda part: w_split[:, slot, part, c * P:(c + 1) * P],
                                     lambda part: h_split[:, j % 2, part, f, :], start=False, stop=(f == 1))
                    last.then_inc(piece_used.sem, 1)

            for b in range(4):
                pe.matmul(core.psum[:, 4 + b, :], zeros, anything, start=True, stop=True)
            up_products(0, 0)
            up_products(1, 1)
            down_products(0, 1)

            def turn(j, at, ada_half):
                up_products(j, at)
                down_products(j - 1, at)

            in_turns(pe, turn)
            down_products(n - 1, n, last_unit=True)
            piece_used.made += 6 * n

        @block.scalar
        def _(act):
            def high_part(j, b, number, slot):
                if isinstance(number, int) and number < 3:
                    pass
                else:
                    act.wait_ge(piece_used.sem, piece_used.at(number - 2))
                nc.scalar.activation(w_split[:, slot, 0, :], piece(j, b), ACT.Copy).then_inc(high.sem, 1)

            def loaded(j, at):
                act.wait_ge(core.loaded[(unit0 + j) % SLOTS].sem, 16 * ((unit0 + j) // SLOTS + 1) + (at - j) * (16 // SLOTS))

            def silu(j, at):
                act.wait_ge(piece_used.sem, piece_used.at(at * 6 - 4) if j else piece_used.at(4))
                nc.scalar.activation(silu_a[j % 2], half(j, 0), ACT.Silu).then_inc(act_done.sem, 1)

            def h_high_part(j, at):
                act.wait_ge(h_ready.sem, h_ready.at(at))
                if j >= 2:
                    act.wait_ge(piece_used.sem, piece_used.at(at * 6 - 8))
                nc.scalar.activation(h_split[:, j % 2, 0, :, :], h_full, ACT.Copy).then_inc(h_high.sem, 1)

            def unit(j, at, ada_half):
                loaded(j, at)
                high_part(j, 0, up_piece(at, 0), 1)
                silu(j - 1, at)
                if ada_half is not None:
                    load_half(ada_half)
                high_part(j, 1, up_piece(at, 1), 2)
                h_high_part(j - 1, at)
                high_part(j, 2, up_piece(at, 2), 0)
                high_part(j, 3, up_piece(at, 3), 1)
                high_part(j - 1, 4, down_piece(at, 0), 2)
                high_part(j - 1, 5, down_piece(at, 1), 0)

            def load_half(k):
                act.wait_ge(step.sem, step.at(k * 4))
                for q in range(4):
                    act.dma_start(ada_slot[:, q * D:(q + 1) * D],
                                  core.ada[bass.ds(k + half0, 1), :, q * D:(q + 1) * D].rearrange("a p n -> p (a n)"))\
                        .then_inc(ada_loaded[q].sem, 16)

            for c in range(0, KC, 2):
                act.activation(u_split[:, 0, c:c + 2, :], src[:, c:c + 2, :], ACT.Copy).then_inc(u_high.sem, u_high.count(1))
                if c == 0:
                    loaded(0, 0)
                    high_part(0, 0, 0, 0)
            for b in range(1, 4):
                high_part(0, b, b, b % 3)
            unit(1, 1, None)
            in_turns(act, unit)
            silu(n - 1, n)
            h_high_part(n - 1, n)
            for f in range(2):
                high_part(n - 1, 4 + f, 6 * n - 2 + f, f + 1)
            if ranges % 2:
                load_half(2 * ranges - 1)
            high.made += 6 * n
            act_done.made += n
            h_high.made += n
            for quarter in ada_loaded:
                quarter.made += 32 * ranges

        if gates is not None:
            @block.gpsimd
            def _(pool):
                def load(q, index):
                    row = gates[bass.ds(index, 1), :] if not isinstance(index, int) else gates[index:index + 1, :]
                    pool.dma_start(gate_rows[q], row.to_broadcast([P, SEQ])).then_inc(gate_loaded[q].sem, 16)

                def gate(q, pair):
                    pool.wait_ge(act_done.sem, act_done.at(pair * 2 + (q + 1)))
                    pool.wait_ge(gate_loaded[q].sem, gate_loaded[q].at(pair * 16 + 16))
                    nc.gpsimd.tensor_tensor(silu_a[q], silu_a[q], gate_rows[q].unsqueeze(1).to_broadcast([P, 2, SEQ]), ALU.mult)\
                        .then_inc(gated.sem, 1)

                load(0, 0)
                load(1, 1)
                with pool.Fori(0, n // 2 - 1) as pair:
                    for q in range(2):
                        gate(q, pair)
                        pool.wait_ge(gated.sem, gated.at(pair * 2 + (q + 1)))
                        load(q, pair * 2 + (q + 2))
                for q in range(2):
                    gate(q, n // 2 - 1)
                    gate_loaded[q].made += 8 * n
                gated.made += n

        @block.vector
        def _(dve):
            ready = act_done if gates is None else gated

            def low_part(j, b, number, slot):
                dve.wait_ge(high.sem, high.at(number + 1))
                e = nc.vector.tensor_tensor(w_split[:, slot, 1, :], piece(j, b), w_split[:, slot, 0, :].bitcast(F32), ALU.subtract)
                e.then_inc(low.sem, 1)

            def product(j, at):
                dve.wait_ge(ready.sem, ready.at(at))
                nc.vector.tensor_tensor(h_full, silu_a[j % 2], half(j, 1), ALU.mult).then_inc(h_ready.sem, 1)

            def h_low_part(j, at):
                dve.wait_ge(h_high.sem, h_high.at(at))
                nc.vector.tensor_tensor(h_split[:, j % 2, 1, :, :], h_full, h_split[:, j % 2, 0, :, :].bitcast(F32), ALU.subtract)\
                    .then_inc(h_low.sem, 1)

            def freed(at):
                dve.wait_ge(low.sem, low.at(at))
                dve.nop().then_inc(core.freed.sem, 1)

            def sum_quarter(j, k, q):
                dve.wait_ge(ada_loaded[q].sem, ada_loaded[q].at(k * 16 + 16))
                if j % 2 == 0 and q == 0:
                    free = sums_free[(j // 2) % 2]
                    dve.wait_ge(free.sem, free.at(k * 4 + (16 - 4 * j)))
                ada_quarter(core, dve, j % 2, q, ada_slot, ada_sums[(j // 2) % 2], core.c_act[:, KC:], k * 4)

            def unit(j, at, ada_half):
                def ada(q):
                    if ada_half is not None:
                        sum_quarter((j - 2) % 4 if j < n - rest else (2 * ranges - 2) % 4, ada_half, q)

                low_part(j, 0, up_piece(at, 0), 1)
                product(j - 1, at)
                low_part(j, 1, up_piece(at, 1), 2)
                h_low_part(j - 1, at)
                low_part(j, 2, up_piece(at, 2), 0)
                low_part(j, 3, up_piece(at, 3), 1)
                low_part(j - 1, 4, down_piece(at, 0), 2)
                ada(0)
                ada(1)
                low_part(j - 1, 5, down_piece(at, 1), 0)
                freed(down_piece(at, 1) + 1)
                ada(2)
                ada(3)

            for c in range(0, KC, 2):
                dve.wait_ge(u_high.sem, u_high.at(c // 2 + 1))
                dve.tensor_tensor(u_split[:, 1, c:c + 2, :], src[:, c:c + 2, :], u_split[:, 0, c:c + 2, :].bitcast(F32), ALU.subtract)\
                    .then_inc(u_low.sem, u_low.count(1))
                if c == 0:
                    low_part(0, 0, 0, 0)
            dve.wait_ge(u_low.sem, u_low.at(KC // 2))
            for b in range(1, 4):
                low_part(0, b, b, b % 3)
            unit(1, 1, None)
            in_turns(dve, unit)
            product(n - 1, n)
            h_low_part(n - 1, n)
            for f in range(2):
                low_part(n - 1, 4 + f, 6 * n - 2 + f, f + 1)
            freed(6 * n)
            if ranges % 2:
                for q in range(4):
                    sum_quarter((2 * ranges - 1) % 4, 2 * ranges - 1, q)
            low.made += 6 * n
            h_ready.made += n
            h_low.made += n
            step.made += 8 * ranges
            core.freed.made += n
            dve.wait_ge(piece_used.sem, piece_used.at(6 * n))
            residual(dve, chain(core, dve, "dve"), y)
    core.end_stage()


def log1p_series(dve, link, out, e, t, z):
    link(dve.tensor_scalar(t, e, 2.0, None, ALU.add))
    link(dve.reciprocal(t, t))
    link(dve.tensor_tensor(z, e, t, ALU.mult))
    link(dve.tensor_tensor(t, z, z, ALU.mult))
    link(dve.tensor_scalar(out, t, 1.0 / 17, None, ALU.mult))
    for n in (15, 13, 11, 9, 7, 5, 3):
        link(dve.scalar_tensor_tensor(out, out, 1.0 / n, t, ALU.add, ALU.mult))
    link(dve.scalar_tensor_tensor(out, out, 1.0, z, ALU.add, ALU.mult))
    link(dve.tensor_scalar(out, out, 2.0, None, ALU.mult))


def first_projection_stage(core, u, raw, xc, y_act, qk, v_tok):
    raw_rows = raw[:, 0:4 * (SEQ + 3)].rearrange("p (c t) -> p c t", c=4)
    with core.nc.Block() as block:
        projected, raw_copied = (core.event(s) for s in ("projected", "raw_copied"))

        def pair(g):
            return core.psum[:, g % 8, :].rearrange("p (c t) -> p c t", t=SEQ)

        @block.sync
        def _(sync):
            core.load_ahead(sync, ("gate_x", 0))

        @block.tensor
        def _(pe):
            for j in range(16):
                core.project(pe, ("w_in", j), lambda k: u[:, k, :], pair(j // 2)[:, j % 2, :], projected)
            for j in range(16, 20):
                w = core.weights(pe, ("w_in", j)).rearrange("p (k m) -> p k m", k=KC)
                if j == 16:
                    pe.wait_ge(raw_copied.sem, raw_copied.at(2))
                for t in range(2):
                    for k in range(KC):
                        last = pe.matmul(core.psum[:, t, (j - 16) * P:(j - 15) * P], u[:, k, t * P:(t + 1) * P], w[:, k, :],
                                         start=(k == 0), stop=(k == KC - 1))
                core.used(pe, ("w_in", j), last, projected)

        @block.vector
        def _(dve):
            link = chain(core, dve, "dve")
            link(dve.memset(raw_rows[:, :, 0:3], 0.0))
            for g in range(2):
                dve.wait_ge(projected.sem, projected.at(2 * g + 2))
                dve.tensor_copy(raw_rows[:, 2 * g:2 * g + 2, 3:], pair(g)).then_inc(raw_copied.sem, raw_copied.count(1))
            dve.wait_ge(raw_copied.sem, raw_copied.at(2))
            w = core.col("conv_w")
            for c in range(4):
                link(dve.tensor_scalar(xc[:, c, :], raw_rows[:, c, 0:SEQ], w[:, c:c + 1], core.col("conv_b")[:, c:c + 1],
                                       ALU.mult, ALU.add))
                for k in range(1, 4):
                    link(dve.scalar_tensor_tensor(xc[:, c, :], raw_rows[:, c, k:k + SEQ], w[:, 4 * k + c:4 * k + c + 1],
                                                  xc[:, c, :], ALU.mult, ALU.add))
            dve.wait_ge(projected.sem, projected.at(20))
            for t in range(2):
                dve.tensor_copy(v_tok[:, t, :], core.psum[:, t, :])

        @block.scalar
        def _(act):
            for g in range(2, 4):
                act.wait_ge(projected.sem, projected.at(2 * g + 2))
                act.activation(y_act[:, 2 * g - 4:2 * g - 2, :], pair(g), ACT.Gelu_apprx_tanh)
            for g in range(4, 8):
                act.wait_ge(projected.sem, projected.at(2 * g + 2))
                act.activation(qk[:, 2 * g - 8:2 * g - 6, :], pair(g), ACT.Copy)
    core.end_stage()


def lru_stage(core, xc, y_act, out, r, i, a, th, u):
    lam, s = core.col("lam"), core.small
    neg, pos, e, t, z, sp, c8, nc8 = (s[:, 4 * k:4 * k + 4] for k in range(8))
    with core.nc.Block() as block:
        gate_sums, sigmoids, small_exp, small_in, rates, decays, roots, root_in = (
            core.event(n) for n in ("gate_sums", "sigmoids", "small_exp", "small_in", "rates", "decays", "roots", "root_in"))
        bank = lambda g: core.psum[:, 2 * g:2 * g + 2, :].rearrange("p b (c t) -> p (b c) t", t=SEQ)

        @block.tensor
        def _(pe):
            for g, key in enumerate(("gate_a", "gate_x")):
                w = core.weights(pe, (key, 0)).rearrange("p (c m) -> p c m", c=4)
                for c in range(4):
                    last = pe.matmul(bank(g)[:, c, :], w[:, c, :], xc[:, c, :], start=True, stop=True)
                core.used(pe, (key, 0), last, gate_sums)

        @block.scalar
        def _(act):
            act.wait_ge(small_in.sem, small_in.at(1))
            act.activation(e, neg, ACT.Exp).then_inc(small_exp.sem, small_exp.count(1))
            for g, (dst, bias) in enumerate(((r, "b_gate_a"), (i, "b_gate_x"))):
                act.wait_ge(gate_sums.sem, gate_sums.at(g + 1))
                for c in range(4):
                    act.activation(dst[:, c, :], bank(g)[:, c, :], ACT.Sigmoid, bias=core.col(bias)[:, c:c + 1])\
                        .then_inc(sigmoids.sem, sigmoids.count(1))
            act.wait_ge(rates.sem, rates.at(1))
            act.wait_ge(sigmoids.sem, sigmoids.at(8))
            for c in range(4):
                act.activation(a[:, c, :], r[:, c, :], ACT.Exp, scale=c8[:, c:c + 1])
                act.activation(th[:, c, :], r[:, c, :], ACT.Tanh, scale=nc8[:, c:c + 1]).then_inc(decays.sem, decays.count(1))
            act.wait_ge(root_in.sem, root_in.at(1))
            act.activation(th, th, ACT.Sqrt).then_inc(roots.sem, roots.count(1))

        @block.vector
        def _(dve):
            link = chain(core, dve, "dve")
            dve.scalar_tensor_tensor(neg, lam, -1.0, lam, ALU.mult, ALU.min).then_inc(small_in.sem, small_in.count(1))
            link(dve.tensor_scalar(pos, lam, -1.0, 0.0, ALU.mult, ALU.max))
            dve.wait_ge(small_exp.sem, small_exp.at(1))
            log1p_series(dve, link, sp, e, t, z)
            link(dve.tensor_tensor(sp, sp, pos, ALU.add))
            link(dve.tensor_scalar(c8, sp, -8.0, None, ALU.mult))
            dve.tensor_scalar(nc8, sp, 8.0, None, ALU.mult).then_inc(rates.sem, rates.count(1))
            dve.wait_ge(sigmoids.sem, sigmoids.at(8))
            dve.wait_ge(decays.sem, decays.at(4))
            link(dve.tensor_tensor(u, a, a, ALU.mult))
            dve.scalar_tensor_tensor(th, u, 1.0, th, ALU.add, ALU.mult).then_inc(root_in.sem, root_in.count(1))
            link(dve.tensor_tensor(i, i, xc, ALU.mult))
            dve.wait_ge(roots.sem, roots.at(1))
            link(dve.tensor_tensor(u, i, th, ALU.mult))
            for c in range(4):
                link(dve.tensor_tensor_scan(th[:, c, :], a[:, c, :], u[:, c, :], 0.0, ALU.mult, ALU.add))
            link(dve.tensor_tensor(out, th, y_act, ALU.mult))
    core.end_stage()


def bias_stage(core, rel_bias, scratch, bias):
    table = core.small[:, 0:HEADS_A]
    rows = core.buf(9).rearrange("p c t -> p (c t)")
    buckets = core.bufs[:, 7, 0:2 * SEQ]
    rows2 = core.buf(8).rearrange("p c t -> p (c t)")
    with core.nc.Block() as block:
        table_ready, distances, stored, read = (core.event(n) for n in ("table", "distances", "rows_stored", "rows_read"))
        copied = core.event("rows_copied")

        @block.sync
        def _(sync):
            core.load_const(sync, "buckets", buckets)
            sync.wait_ge(table_ready.sem, table_ready.at(1))
            sync.dma_start(table[0:REL_BUCKETS, :], rel_bias).then_inc(table_ready.sem, table_ready.count(16))
            sync.wait_ge(copied.sem, copied.at(8))
            for n, part in enumerate((rows, rows2)):
                sync.dma_start(scratch[:, 4 * n:4 * n + 4, :], part.rearrange("p (h j) -> p h j", h=4))\
                    .then_inc(stored.sem, stored.count(16))
            sync.wait_ge(stored.sem, stored.at(32))
            for t in range(2):
                for h in range(HEADS_A):
                    src = bass.AP(scratch.tensor, h * 2 * SEQ + (SEQ - 1) - t * P, [[HEADS_A * 2 * SEQ - 1, P], [1, SEQ]])
                    sync.dma_start(bias[:, h, t, :], src).then_inc(read.sem, read.count(16))
            sync.wait_ge(read.sem, read.at(16 * 16))

        @block.vector
        def _(dve):
            dve.memset(table[0:REL_BUCKETS + 1, :], 1.0).then_inc(table_ready.sem, table_ready.count(1))
            for h in range(HEADS_A):
                dve.wait_ge(distances.sem, distances.at(h + 1))
                dst = (rows if h < 4 else rows2)[:, (h % 4) * 512:(h % 4 + 1) * 512]
                dve.tensor_copy(dst, core.psum[:, h, :]).then_inc(copied.sem, copied.count(1))

        @block.tensor
        def _(pe):
            pe.wait_ge(table_ready.sem, table_ready.at(17))
            for h in range(HEADS_A):
                pe.matmul(core.psum[:, h, :], table[0:REL_BUCKETS + 1, h:h + 1].to_broadcast([REL_BUCKETS + 1, P]),
                                       buckets[0:REL_BUCKETS + 1, :], start=True, stop=True)\
                    .then_inc(distances.sem, distances.count(1))
    core.end_stage()


def attention_stage(core, heads, q, k, v, bias, out, s_buf, p_buf, pt_buf, sinks=None):
    scale = HEAD ** -0.5
    ident = core.const("ident")
    stat = lambda h, n: core.small[:, 64 + 16 * (h % 2) + 2 * n:64 + 16 * (h % 2) + 2 * n + 2]
    bank = lambda n, h: core.psum[:, 2 * n + h % 2, :].rearrange("p (a t) -> p a t", a=2)
    with core.nc.Block() as block:
        scored, maxed, exped, normed, turned, turned_sb, attended, stored = (
            core.event(n) for n in ("scored", "row_max", "exped", "normed", "turned", "turned_sb", "attended", "head_out"))

        @block.tensor
        def _(pe):
            def scores(h):
                if h >= 2:
                    pe.wait_ge(maxed.sem, maxed.at(h - 1))
                for t in range(2):
                    last = pe.matmul(bank(0, h)[:, t, :], q(h)[:, t * P:(t + 1) * P], k(h), start=True, stop=True)
                last.then_inc(scored.sem, scored.count(1))

            def turn(h):
                pe.wait_ge(normed.sem, normed.at(h + 1))
                if h >= 2:
                    pe.wait_ge(turned_sb.sem, turned_sb.at(h - 1))
                for kt in range(2):
                    for t in range(2):
                        last = pe.transpose(bank(1, h)[:, kt, t * P:(t + 1) * P], p_buf(h)[:, t, kt * P:(kt + 1) * P], ident)
                last.then_inc(turned.sem, turned.count(1))

            def attend(h):
                pe.wait_ge(turned_sb.sem, turned_sb.at(h + 1))
                if h >= 2:
                    pe.wait_ge(stored.sem, stored.at(h - 1))
                base = HEAD * (h % 2)
                for kt in range(2):
                    last = pe.matmul(bank(2, h)[base:base + HEAD, 0, :], v(h, kt), pt_buf(h)[:, kt, :],
                                     start=(kt == 0), stop=(kt == 1))
                last.then_inc(attended.sem, attended.count(1))

            scores(0)
            scores(1)
            for h in range(heads):
                if h + 2 < heads:
                    scores(h + 2)
                turn(h)
                if h >= 1:
                    attend(h - 1)
            attend(heads - 1)

        @block.vector
        def _(dve):
            link = chain(core, dve, "dve")

            def softmax_in(h):
                dve.wait_ge(scored.sem, scored.at(h + 1))
                link(dve.scalar_tensor_tensor(s_buf(h), bank(0, h), scale, bias(h), ALU.mult, ALU.add))
                link(dve.tensor_reduce(stat(h, 0), s_buf(h), AX, ALU.max))
                if sinks is None:
                    last = dve.tensor_scalar(stat(h, 1), stat(h, 0), -1.0, None, ALU.mult)
                else:
                    last = dve.tensor_scalar(stat(h, 1), stat(h, 0), sinks[:, h:h + 1], -1.0, ALU.max, ALU.mult)
                last.then_inc(maxed.sem, maxed.count(1))

            def softmax_out(h):
                dve.wait_ge(exped.sem, exped.at(h + 1))
                if sinks is not None:
                    link(dve.tensor_tensor(stat(h, 2), stat(h, 2), stat(h, 3), ALU.add))
                link(dve.reciprocal(stat(h, 4), stat(h, 2)))
                dve.tensor_scalar(p_buf(h)[:, 0, :], p_buf(h)[:, 0, :], stat(h, 4)[:, 0:1], None, ALU.mult)
                dve.tensor_scalar(p_buf(h)[:, 1, :], p_buf(h)[:, 1, :], stat(h, 4)[:, 1:2], None, ALU.mult)\
                    .then_inc(normed.sem, normed.count(1))

            softmax_in(0)
            for h in range(heads):
                if h + 1 < heads:
                    softmax_in(h + 1)
                softmax_out(h)

        @block.scalar
        def _(act):
            def exps(h):
                act.wait_ge(maxed.sem, maxed.at(h + 1))
                if h >= 2:
                    act.wait_ge(turned.sem, turned.at(h - 1))
                for t in range(2):
                    if sinks is not None:
                        act.activation(stat(h, 3)[:, t:t + 1], sinks[:, h:h + 1], ACT.Exp, bias=stat(h, 1)[:, t:t + 1])
                    e = act.activation(p_buf(h)[:, t, :], s_buf(h)[:, t, :], ACT.Exp, bias=stat(h, 1)[:, t:t + 1],
                                       accum_out=stat(h, 2)[:, t:t + 1])
                e.then_inc(exped.sem, exped.count(1))

            def turned_copy(h):
                act.wait_ge(turned.sem, turned.at(h + 1))
                if h >= 2:
                    act.wait_ge(attended.sem, attended.at(h - 1))
                act.activation(pt_buf(h), bank(1, h), ACT.Copy).then_inc(turned_sb.sem, turned_sb.count(1))

            def head_out(h):
                act.wait_ge(attended.sem, attended.at(h + 1))
                base = HEAD * (h % 2)
                act.activation(out(h), bank(2, h)[base:base + HEAD, 0, :], ACT.Copy).then_inc(stored.sem, stored.count(1))

            exps(0)
            for h in range(heads):
                if h + 1 < heads:
                    exps(h + 1)
                turned_copy(h)
                if h >= 2:
                    head_out(h - 2)
            head_out(heads - 2)
            head_out(heads - 1)
    core.end_stage()


def output_stage(core, key, merged, n, residual):
    y = core.psum[:, 0:4, :].rearrange("p b (c t) -> p (b c) t", t=SEQ)
    with core.nc.Block() as block:
        projected = core.event("projected")

        @block.sync
        def _(sync):
            core.load_ahead(sync, (key, KC - 1))

        @block.tensor
        def _(pe):
            for j in range(KC):
                core.project(pe, (key, j), lambda k: merged(k), y[:, j, :], projected, kcs=n)

        @block.vector
        def _(dve):
            dve.wait_ge(projected.sem, projected.at(KC))
            residual(dve, chain(core, dve, "dve"), y)
    core.end_stage()


def router_stage(core, u, gate_t, gates):
    G, E = N_GROUPS, PER_GROUP
    n = G + N_EXPERTS
    s = core.small
    logits = s[:, 0:2 * n].rearrange("p (t n) -> p t n", t=2)
    at = 2 * n

    def tile(*shape):
        nonlocal at
        size = int(np.prod(shape))
        v = s[:, at:at + size]
        at += size
        names = "abc"[:len(shape)]
        return v.rearrange(f"p ({' '.join(names)}) -> p {' '.join(names)}", **dict(zip(names, shape)))

    rank, rank_g = tile(E), tile(G)
    m, gsum, gtop = tile(2, 1), tile(2, 1), tile(2, 1)
    ge, hot_g, e_in, hot1, hot2, left = tile(2, G), tile(2, G), tile(2, E), tile(2, E), tile(2, E), tile(2, E)
    m1, m2, ed, w1, w2 = (tile(2, 1) for _ in range(5))
    picked, weight_e, gate = tile(2, G, E), tile(2, E), tile(2, G, E)
    bc = lambda a, w: a.to_broadcast([P, 2, w])
    with core.nc.Block() as block:
        routed, softened, soft_in, gate_ready, gate_turned, gate_sb, gate_stored = (
            core.event(x) for x in ("routed", "softened", "soft_in", "gate_ready", "gate_turned", "gate_sb", "gate_stored"))

        @block.sync
        def _(sync):
            core.load_ahead(sync, ("router", 0))
            sync.wait_ge(gate_sb.sem, gate_sb.at(1))
            sync.dma_start(gates, gate_t[0:N_EXPERTS, :]).then_inc(gate_stored.sem, gate_stored.count(16))
            sync.wait_ge(gate_stored.sem, gate_stored.made)

        @block.tensor
        def _(pe):
            w = core.weights(pe, ("router", 0)).rearrange("p (k m) -> p k m", k=KC)
            for t in range(2):
                pe.matmul(core.psum[:, 0, t * n:(t + 1) * n], core.const("ones")[0:1, :], core.col("router_b")[0:1, :],
                          start=True, stop=False)
                for k in range(KC):
                    last = pe.matmul(core.psum[:, 0, t * n:(t + 1) * n], u[:, k, t * P:(t + 1) * P], w[:, k, :],
                                     start=False, stop=(k == KC - 1))
            core.used(pe, ("router", 0), last, routed)
            pe.wait_ge(gate_ready.sem, gate_ready.at(1))
            for t in range(2):
                last = pe.transpose(core.psum[0:N_EXPERTS, 1, t * P:(t + 1) * P], gate[:, t, :, :].rearrange("p g e -> p (g e)"),
                                    core.const("ident"))
            last.then_inc(gate_turned.sem, gate_turned.count(1))

        @block.scalar
        def _(act):
            act.wait_ge(soft_in.sem, soft_in.at(1))
            act.activation(ge, ge, ACT.Exp).then_inc(softened.sem, softened.count(1))
            act.wait_ge(soft_in.sem, soft_in.at(2))
            act.activation(ed, ed, ACT.Exp).then_inc(softened.sem, softened.count(1))

        @block.vector
        def _(dve):
            link = chain(core, dve, "dve")

            def first_hot(hot, x, top, rank_, width):
                link(dve.tensor_tensor(hot, x, bc(top, width), ALU.is_equal))
                link(dve.tensor_tensor(hot, hot, rank_.unsqueeze(1).to_broadcast([P, 2, width]), ALU.mult))
                link(dve.tensor_reduce(m, hot, AX, ALU.max))
                link(dve.tensor_tensor(hot, hot, bc(m, width), ALU.is_equal))

            for k in range(E):
                link(dve.memset(rank[:, k:k + 1], float(E - k)))
            for k in range(G):
                link(dve.memset(rank_g[:, k:k + 1], float(G - k)))
            dve.wait_ge(routed.sem, routed.at(1))
            link(dve.tensor_copy(logits, core.psum[:, 0, 0:2 * n].rearrange("p (t n) -> p t n", t=2)))
            lg = logits[:, :, 0:G]
            le = logits[:, :, G:n].rearrange("p t (g e) -> p t g e", g=G)
            link(dve.tensor_reduce(gtop, lg, AX, ALU.max))
            first_hot(hot_g, lg, gtop, rank_g, G)
            dve.tensor_tensor(ge, lg, bc(gtop, G), ALU.subtract).then_inc(soft_in.sem, soft_in.count(1))
            for t in range(2):
                link(dve.tensor_tensor(picked[:, t, :, :], le[:, t, :, :], hot_g[:, t, :].unsqueeze(2).to_broadcast([P, G, E]), ALU.mult))
                link(dve.tensor_reduce(e_in[:, t, :], picked[:, t, :, :].rearrange("p g e -> p e g"), AX, ALU.add))
            link(dve.tensor_reduce(m1, e_in, AX, ALU.max))
            first_hot(hot1, e_in, m1, rank, E)
            link(dve.scalar_tensor_tensor(left, hot1, NEG, e_in, ALU.mult, ALU.add))
            link(dve.tensor_reduce(m2, left, AX, ALU.max))
            first_hot(hot2, left, m2, rank, E)
            dve.wait_ge(softened.sem, softened.at(1))
            dve.tensor_tensor(ed, m2, m1, ALU.subtract).then_inc(soft_in.sem, soft_in.count(1))
            link(dve.tensor_reduce(gsum, ge, AX, ALU.add))
            link(dve.reciprocal(gtop, gsum))
            dve.wait_ge(softened.sem, softened.at(2))
            link(dve.tensor_scalar(w1, ed, 1.0, None, ALU.add))
            link(dve.reciprocal(w1, w1))
            link(dve.tensor_tensor(w1, w1, gtop, ALU.mult))
            link(dve.tensor_tensor(w2, w1, ed, ALU.mult))
            link(dve.tensor_tensor(hot1, hot1, bc(w1, E), ALU.mult))
            link(dve.tensor_tensor(hot2, hot2, bc(w2, E), ALU.mult))
            link(dve.tensor_tensor(weight_e, hot1, hot2, ALU.add))
            for t in range(2):
                last = dve.tensor_tensor(gate[:, t, :, :], hot_g[:, t, :].unsqueeze(2).to_broadcast([P, G, E]),
                                         weight_e[:, t, :].unsqueeze(1).to_broadcast([P, G, E]), ALU.mult)
                if t == 0:
                    link(last)
            last.then_inc(gate_ready.sem, gate_ready.count(1))
            dve.wait_ge(gate_turned.sem, gate_turned.at(1))
            dve.tensor_copy(gate_t[0:N_EXPERTS, :], core.psum[0:N_EXPERTS, 1, 0:SEQ]).then_inc(gate_sb.sem, gate_sb.count(1))
    core.end_stage()


def first_block(core):
    first_ada_stage(core)
    sh1, sc1, g1, sh2, sc2, g2 = (core.mod[:, v * KC:(v + 1) * KC] for v in range(6))
    one_plus = lambda scale: (lambda dve, link: link(dve.tensor_scalar(core.gain[:], scale, 1.0, None, ALU.add)))
    u = core.buf(0)
    norm_stage(core, core.x, u, LN_EPS, core.gain, sh1, center=True, pre=one_plus(sc1))
    y_act, qk, v_tok = core.buf(1)[:, 0:4, :], core.buf(2), core.buf(3)[:, 0:4, :].rearrange("p c t -> p (c t)").rearrange("p (t n) -> p t n", t=2)
    xc = core.buf(5)[:, 0:4, :]
    first_projection_stage(core, u, core.bufs[:, 4, :], xc, y_act, qk, v_tok)
    lru_out, attn_out = core.buf(0)[:, 0:4, :], core.buf(0)[:, 4:8, :]
    lru_stage(core, xc, y_act, lru_out, core.buf(5)[:, 4:8, :], core.buf(6)[:, 0:4, :], core.buf(6)[:, 4:8, :],
              core.buf(7)[:, 0:4, :], core.buf(7)[:, 4:8, :])
    bias = core.buf(4, 2).rearrange("p (h a) t -> p h a t", h=HEADS_A)
    bias_stage(core, core.rel_bias, core.scratch, bias)
    rows = lambda x, h: x[HEAD * (h % 2):HEAD * (h % 2) + HEAD, h // 2, :]
    attention_stage(core, HEADS_A, lambda h: rows(qk[:, 0:4, :], h), lambda h: rows(qk[:, 4:8, :], h),
                    lambda h, kt: v_tok[:, kt, HEAD * h:HEAD * h + HEAD], lambda h: bias[:, h, :, :],
                    lambda h: rows(attn_out, h), lambda h: core.buf(6)[:, 2 * (h % 2):2 * (h % 2) + 2, :],
                    lambda h: core.buf(6)[:, 4 + 2 * (h % 2):6 + 2 * (h % 2), :],
                    lambda h: core.buf(7)[:, 2 * (h % 2):2 * (h % 2) + 2, :])
    norm_stage(core, lru_out, lru_out, LN_EPS, core.col("norm_lru_g"), n=4)
    norm_stage(core, attn_out, attn_out, LN_EPS, core.col("norm_attn_g"), n=4)

    def residual(gate):
        def run(dve, link, y):
            for c in range(KC):
                link(dve.tensor_scalar(core.x[:, c, :], core.x[:, c, :], ALPHA, None, ALU.mult))
                dve.scalar_tensor_tensor(core.x[:, c, :], y[:, c, :], gate[:, c:c + 1], core.x[:, c, :], ALU.mult, ALU.add)
        return run

    output_stage(core, "w_out", lambda k: core.buf(0)[:, k, :], KC, residual(g1))
    norm_stage(core, core.x, core.x, LN_EPS, core.col("ln1_g"), core.col("ln1_b"), center=True)
    norm_stage(core, core.x, u, LN_EPS, core.gain, sh2, center=True, pre=one_plus(sc2))
    router_stage(core, u, core.buf(1)[:, 0, :], core.gates)
    glu_stage(core, "moe", N_EXPERTS, u, residual(g2), gates=core.gates, ada=(0, 0, 9))
    norm_stage(core, core.x, core.x, LN_EPS, core.col("ln2_g"), core.col("ln2_b"), center=True)


def head_rms_stage(core, x, n, gains, squares, roots):
    banks = core.psum[:, 0:8, :].rearrange("p b (c t) -> p (b c) t", t=SEQ)
    with core.nc.Block() as block:
        squared, summed, scaled, rooted = (core.event(s) for s in ("squared", "square_sum", "scaled", "rooted"))

        @block.scalar
        def _(act):
            for c in range(n):
                act.activation(squares[:, c, :], x[:, c, :], ACT.Square).then_inc(squared.sem, squared.count(1))
            act.wait_ge(scaled.sem, scaled.at(1))
            act.activation(roots[:, 0:n, :], roots[:, 0:n, :], ACT.Sqrt).then_inc(rooted.sem, rooted.count(1))

        @block.tensor
        def _(pe):
            for c in range(n):
                pe.wait_ge(squared.sem, squared.at(c + 1))
                last = pe.matmul(banks[:, c, :], core.const("heads"), squares[:, c, :], start=True, stop=True)
            last.then_inc(summed.sem, summed.count(1))

        @block.vector
        def _(dve):
            link = chain(core, dve, "dve")
            dve.wait_ge(summed.sem, summed.at(1))
            dve.tensor_scalar(roots[:, 0:n, :], banks[:, 0:n, :], 1.0 / HEAD, NORM_EPS, ALU.mult, ALU.add)\
                .then_inc(scaled.sem, scaled.count(1))
            dve.wait_ge(rooted.sem, rooted.at(1))
            link(dve.reciprocal(roots[:, 0:n, :], roots[:, 0:n, :]))
            for c in range(n):
                dve.scalar_tensor_tensor(x[:, c, :], x[:, c, :], gains(c), roots[:, c, :], ALU.mult, ALU.mult)
    core.end_stage()


def window_projection_stage(core, u, qk, v_tok):
    with core.nc.Block() as block:
        projected = core.event("projected")

        def slot(c):
            return core.psum[:, c // 2, (c % 2) * SEQ:(c % 2 + 1) * SEQ]

        @block.sync
        def _(sync):
            core.load_ahead(sync, ("sw_qkv", 11))
            core.load_const(sync, "band", core.bufs[:, 8, 0:2 * SEQ])

        @block.tensor
        def _(pe):
            for j in range(10):
                if j < 8:
                    core.project(pe, ("sw_qkv", j), lambda k: u[:, k, :], slot(j), projected)
                    continue
                w = core.weights(pe, ("sw_qkv", j)).rearrange("p (k m) -> p k m", k=KC)
                for half in range(2):
                    for k in range(KC):
                        pe.matmul(slot(j + 2)[HEAD * half:HEAD * (half + 1), :], w[:, k, HEAD * (1 - half):HEAD * (2 - half)],
                                  u[:, k, :], start=(k == 0), stop=(k == KC - 1))
                core.project(pe, ("sw_qkv", j), lambda k: u[:, k, :], slot(j), projected)
            for j in range(10, 12):
                w = core.weights(pe, ("sw_qkv", j)).rearrange("p (k m) -> p k m", k=KC)
                for t in range(2):
                    for k in range(KC):
                        last = pe.matmul(core.psum[:, 6 + t, (j - 10) * P:(j - 9) * P], u[:, k, t * P:(t + 1) * P], w[:, k, :],
                                         start=(k == 0), stop=(k == KC - 1))
                core.used(pe, ("sw_qkv", j), last, projected)

        @block.scalar
        def _(act):
            for g in range(4):
                act.wait_ge(projected.sem, projected.at(2 * g + 2))
                act.activation(qk[:, 2 * g:2 * g + 2, :], core.psum[:, g, :].rearrange("p (c t) -> p c t", t=SEQ), ACT.Copy)
            for g in (4, 5):
                act.wait_ge(projected.sem, projected.at(10))
                act.activation(qk[:, 2 * g:2 * g + 2, :], core.psum[:, g, :].rearrange("p (c t) -> p c t", t=SEQ), ACT.Copy)

        @block.vector
        def _(dve):
            dve.wait_ge(projected.sem, projected.at(12))
            for t in range(2):
                dve.tensor_copy(v_tok[:, t, :], core.psum[:, 6 + t, 0:SEQ])
    core.end_stage()


def gated_residual(core):
    gate = core.mod[:, 5 * KC:6 * KC]

    def run(dve, link, y):
        for c in range(KC):
            dve.scalar_tensor_tensor(core.x[:, c, :], y[:, c, :], gate[:, c:c + 1], core.x[:, c, :], ALU.mult, ALU.add)
    return run


def window_attention(core):
    u = core.buf(0)
    qk = core.buf(1, 2)
    v_tok = core.buf(2)[:, 4:6, :]
    window_projection_stage(core, u, qk, v_tok)
    head_rms_stage(core, qk, 12, lambda c: core.col("q_norm" if c < 8 else "k_norm"), core.buf(3, 2), core.buf(5, 2))
    band = core.bufs[:, 8, 0:2 * SEQ].rearrange("p (a t) -> p a t", a=2)
    rows = lambda x, c, h: x[HEAD * (h % 2):HEAD * (h % 2) + HEAD, c, :]

    def k_rows(h):
        kv = h // (SW_Q // SW_KV)
        return rows(qk, (8 if kv % 2 == h % 2 else 10) + kv // 2, h)

    attention_stage(core, SW_Q, lambda h: rows(qk, h // 2, h), k_rows,
                    lambda h, kt: v_tok[:, kt, HEAD * (h // 4):HEAD * (h // 4) + HEAD], lambda h: band,
                    lambda h: rows(u, h // 2, h), lambda h: core.buf(6)[:, 2 * (h % 2):2 * (h % 2) + 2, :],
                    lambda h: core.buf(6)[:, 4 + 2 * (h % 2):6 + 2 * (h % 2), :],
                    lambda h: core.buf(7)[:, 2 * (h % 2):2 * (h % 2) + 2, :], sinks=core.col("sinks"))
    output_stage(core, "sw_o", lambda k: u[:, k, :], KC, gated_residual(core))


def rwkv_projection_stage(core, jobs, h, dx, xs, after=None):
    with core.nc.Block() as block:
        mixed, projected, evacuated, up_done, narrow_ready = (
            core.event(s) for s in ("mixed", "projected", "evacuated", "narrow_sums", "narrow_ready"))
        inputs = [j for j in jobs if j[0] is not None]
        narrow = core.narrow
        last_use, products, ups = [], 0, 0
        for mu, up, _, down, *_ in jobs:
            if mu is None:
                last_use.pop()
            ups += len(up) if down else 0
            products += KC
            last_use.append((up_done, ups) if down else (projected, products))

        def pair(g):
            return core.psum[:, g % 6, :].rearrange("p (c t) -> p c t", t=SEQ)

        @block.sync
        def _(sync):
            core.load_ahead(sync, (jobs[-1][3] or jobs[-1][1])[-1])
            if after:
                after(sync)

        @block.vector
        def _(dve):
            link = chain(core, dve, "dve")
            if isinstance(jobs[0][6], str):
                link(dve.tensor_tensor(dx[:, :, 1:], h[:, :, :SEQ - 1], h[:, :, 1:], ALU.subtract))
                link(dve.tensor_scalar(dx[:, :, 0:1], h[:, :, 0:1], -1.0, None, ALU.mult))
            for n, job in enumerate(inputs):
                if n >= 2:
                    used, count = last_use[n - 2]
                    dve.wait_ge(used.sem, used.at(count))
                for c in range(KC):
                    last = dve.scalar_tensor_tensor(xs(n)[:, c, :], dx[:, c, :], job[0][:, c:c + 1], h[:, c, :], ALU.mult, ALU.add)
                last.then_inc(mixed.sem, mixed.count(1))

        @block.tensor
        def _(pe):
            n, g, ups = -1, 0, 0
            for mu, up, up_func, down, out, func, bias in jobs:
                if mu is not None:
                    n += 1
                    pe.wait_ge(mixed.sem, mixed.at(n + 1))
                source = xs(n)
                if not down:
                    for j, key in enumerate(up):
                        if j % 2 == 0 and g >= 6:
                            pe.wait_ge(evacuated.sem, evacuated.at(g - 5))
                        core.project(pe, key, lambda k: source[:, k, :], pair(g)[:, j % 2, :], projected)
                        g += j % 2
                else:
                    for b, key in enumerate(up):
                        m = core.place[key][2] // KC
                        core.project(pe, key, lambda k: source[:, k, :], core.psum[0:m, 6 + b, 0:SEQ], up_done, m=m)
                if down:
                    ups += len(up)
                    pe.wait_ge(narrow_ready.sem, narrow_ready.at(ups))
                    for c in range(KC):
                        if c % 2 == 0 and g >= 6:
                            pe.wait_ge(evacuated.sem, evacuated.at(g - 5))
                        for b, key in enumerate(down):
                            rows = core.place[up[b]][2] // KC
                            w = core.weights(pe, key)
                            last = pe.matmul(pair(g)[:, c % 2, :], w[0:rows, c * P:(c + 1) * P], narrow[0:rows, b, :],
                                             start=(b == 0), stop=(b == len(down) - 1))
                            if c == KC - 1 and b < len(down) - 1:
                                core.used(pe, key, last)
                        if c == KC - 1:
                            core.used(pe, down[-1], last, projected)
                        else:
                            last.then_inc(projected.sem, projected.count(1))
                        g += c % 2

        @block.scalar
        def _(act):
            g, products, ups = 0, 0, 0
            for mu, up, up_func, down, out, func, bias in jobs:
                for b, key in enumerate(up if down else ()):
                    ups += 1
                    act.wait_ge(up_done.sem, up_done.at(ups))
                    m = core.place[key][2] // KC
                    act.activation(narrow[0:m, b, :], core.psum[0:m, 6 + b, 0:SEQ], up_func)\
                        .then_inc(narrow_ready.sem, narrow_ready.count(1))
                for c in range(0, KC, 2):
                    products += 2
                    act.wait_ge(projected.sem, projected.at(products))
                    if bias is None or isinstance(bias, str):
                        e = act.activation(out[:, c:c + 2, :], pair(g), func)
                    else:
                        act.activation(out[:, c, :], pair(g)[:, 0, :], func, bias=bias[:, c:c + 1])
                        e = act.activation(out[:, c + 1, :], pair(g)[:, 1, :], func, bias=bias[:, c + 1:c + 2])
                    e.then_inc(evacuated.sem, evacuated.count(1))
                    g += 1
    core.end_stage()


def value_mix_stage(core, v, gate, first, v_first):
    with core.nc.Block() as block:
        read = core.event("v_first_read")

        @block.sync
        def _(sync):
            sync.dma_start(first, v_first).then_inc(read.sem, read.count(16))

        @block.vector
        def _(dve):
            link = chain(core, dve, "dve")
            dve.wait_ge(read.sem, read.at(16))
            link(dve.tensor_tensor(first, first, v, ALU.subtract))
            link(dve.tensor_tensor(first, first, gate, ALU.mult))
            link(dve.tensor_tensor(v, v, first, ALU.add))
    core.end_stage()


def sum_heads(core, pe, out, x):
    slide = core.const("slide")
    for c in range(KC):
        at = RW_HEADS - 2 - 2 * c
        last = pe.matmul(out, slide[:, at:at + RW_HEADS], x[:, c, :], start=(c == 0), stop=(c == KC - 1))
    return last


def spread_heads(core, pe, out, by_head):
    for h in range(RW_HEADS):
        base, c = HEAD * (h % 2), h // 2
        last = pe.matmul(out[base:base + HEAD, c * SEQ:(c + 1) * SEQ],
                         core.const("ident")[0:RW_HEADS, h:h + 1].to_broadcast([RW_HEADS, HEAD]), by_head, start=True, stop=True)
    return last


def rwkv_scale_stage(core, n, kk, w, tmp, bonus, r, k, v, lw, a):
    s = core.small
    mid, end, e_mid, e_end = (s[:, 16 * q:16 * q + 16] for q in range(4))
    flat = lambda x: x.rearrange("p c t -> p (c t)")
    by_chunk = lambda x: flat(x).rearrange("p (q t) -> p q t", t=P)
    sums = lambda g: core.psum[:, 4 * g:4 * g + 4, :].rearrange("p b t -> p (b t)")
    with core.nc.Block() as block:
        by_head, head_sums = core.rstd[0:RW_HEADS, :], core.psum[0:RW_HEADS, 4, 0:SEQ]
        names = ("kk_raw", "kk_squared", "kk_sums", "kk_bounded", "kk_rooted", "kk_inverse", "kk_spread", "bonus_in", "bonus_sums",
                 "w_ready", "w_centered", "prev_ready", "mid_exp", "r_exp", "prev_exp", "r_scaled", "k_exp")
        sig = {x: core.event(x) for x in names}

        @block.vector
        def _(dve):
            link = chain(core, dve, "dve")
            kc = lambda x: core.col(f"{x}{n}")
            for c in range(KC):
                last = dve.tensor_scalar(kk[:, c, :], k[:, c, :], kc("k_k")[:, c:c + 1], None, ALU.mult)
            last.then_inc(sig["kk_raw"].sem, sig["kk_raw"].count(1))
            link(dve.tensor_scalar(flat(lw), flat(lw), -float(np.exp(-0.5)), None, ALU.mult))
            for q in range(16):
                last = dve.tensor_tensor_scan(by_chunk(w)[:, q, :], core.const("ones"), by_chunk(lw)[:, q, :], 0.0, ALU.mult, ALU.add)
            link(last)
            link(dve.tensor_copy(mid, by_chunk(w)[:, :, P // 2 - 1]))
            link(dve.tensor_tensor(end, by_chunk(w)[:, :, P - 1], mid, ALU.subtract))
            dve.tensor_tensor(by_chunk(w), by_chunk(w), mid.unsqueeze(2).to_broadcast([P, 16, P]), ALU.subtract)\
                .then_inc(sig["w_centered"].sem, sig["w_centered"].count(1))
            dve.wait_ge(sig["w_centered"].sem, sig["w_centered"].at(1))
            dve.tensor_tensor(flat(lw), flat(w), flat(lw), ALU.subtract)\
                .then_inc(sig["prev_ready"].sem, sig["prev_ready"].count(1))
            dve.wait_ge(sig["kk_sums"].sem, sig["kk_sums"].at(1))
            dve.tensor_scalar(by_head, head_sums, 1e-24, None, ALU.max)\
                .then_inc(sig["kk_bounded"].sem, sig["kk_bounded"].count(1))
            dve.wait_ge(sig["kk_rooted"].sem, sig["kk_rooted"].at(1))
            dve.reciprocal(by_head, by_head).then_inc(sig["kk_inverse"].sem, sig["kk_inverse"].count(1))
            for c in range(KC):
                last = dve.tensor_scalar(bonus[:, c, :], a[:, c, :], -1.0, kc("k_a")[:, c:c + 1], ALU.add, ALU.mult)
            link(last)
            link(dve.scalar_tensor_tensor(flat(k), flat(bonus), 1.0, flat(k), ALU.add, ALU.mult))
            dve.wait_ge(sig["kk_spread"].sem, sig["kk_spread"].at(1))
            link(dve.tensor_tensor(flat(kk), flat(kk), sums(0), ALU.mult))
            link(dve.tensor_tensor(flat(a), flat(a), flat(kk), ALU.mult))
            for c in range(KC):
                last = dve.scalar_tensor_tensor(bonus[:, c, :], r[:, c, :], kc("r_k")[:, c:c + 1], k[:, c, :], ALU.mult, ALU.mult)
            last.then_inc(sig["bonus_in"].sem, sig["bonus_in"].count(1))
            dve.wait_ge(sig["r_exp"].sem, sig["r_exp"].at(1))
            dve.wait_ge(sig["bonus_in"].sem, sig["bonus_in"].at(1))
            dve.tensor_tensor(flat(r), flat(r), flat(tmp), ALU.mult).then_inc(sig["r_scaled"].sem, sig["r_scaled"].count(1))
            dve.wait_ge(sig["prev_exp"].sem, sig["prev_exp"].at(1))
            dve.scalar_tensor_tensor(flat(kk), flat(kk), -1.0, flat(lw), ALU.mult, ALU.mult)
            dve.wait_ge(sig["bonus_sums"].sem, sig["bonus_sums"].at(1))
            dve.tensor_tensor(flat(bonus), sums(1), flat(v), ALU.mult)
            dve.wait_ge(sig["k_exp"].sem, sig["k_exp"].at(1))
            dve.tensor_tensor(flat(k), flat(k), flat(tmp), ALU.mult)
            dve.tensor_tensor(flat(a), flat(a), flat(tmp), ALU.mult)

        @block.scalar
        def _(act):
            act.wait_ge(sig["kk_raw"].sem, sig["kk_raw"].at(1))
            act.activation(flat(bonus), flat(kk), ACT.Square).then_inc(sig["kk_squared"].sem, sig["kk_squared"].count(1))
            act.wait_ge(sig["w_centered"].sem, sig["w_centered"].at(1))
            act.activation(e_mid, mid, ACT.Exp)
            act.activation(e_end, end, ACT.Exp)
            act.activation(flat(tmp), flat(w), ACT.Exp).then_inc(sig["r_exp"].sem, sig["r_exp"].count(1))
            act.wait_ge(sig["prev_ready"].sem, sig["prev_ready"].at(1))
            act.activation(flat(lw), flat(lw), ACT.Exp).then_inc(sig["prev_exp"].sem, sig["prev_exp"].count(1))
            act.wait_ge(sig["kk_bounded"].sem, sig["kk_bounded"].at(1))
            act.activation(by_head, by_head, ACT.Sqrt).then_inc(sig["kk_rooted"].sem, sig["kk_rooted"].count(1))
            act.wait_ge(sig["r_scaled"].sem, sig["r_scaled"].at(1))
            act.activation(flat(tmp), flat(w), ACT.Exp, scale=-1.0).then_inc(sig["k_exp"].sem, sig["k_exp"].count(1))

        @block.tensor
        def _(pe):
            pe.wait_ge(sig["kk_squared"].sem, sig["kk_squared"].at(1))
            sum_heads(core, pe, head_sums, bonus).then_inc(sig["kk_sums"].sem, sig["kk_sums"].count(1))
            pe.wait_ge(sig["kk_inverse"].sem, sig["kk_inverse"].at(1))
            spread_heads(core, pe, sums(0), by_head).then_inc(sig["kk_spread"].sem, sig["kk_spread"].count(1))
            pe.wait_ge(sig["bonus_in"].sem, sig["bonus_in"].at(1))
            for c in range(KC):
                last = pe.matmul(sums(1)[:, c * SEQ:(c + 1) * SEQ], core.const("heads"), bonus[:, c, :], start=True, stop=True)
            last.then_inc(sig["bonus_sums"].sem, sig["bonus_sums"].count(1))
    core.end_stage()


def rwkv_chunk_stage(core, r, k, v, a, b, sets):
    s = core.small
    e_mid, e_end = s[:, 32:48], s[:, 48:64]
    four = lambda x: x.rearrange("p (h t) -> p h t", h=4)
    tile = lambda q: [four(x[:, q * 512:(q + 1) * 512]) for x, _ in sets]
    ab_t, t_, tt, ak_t, rb_t, rk_t, x_, masked = (tile(q) for q in range(8))
    tok = [x.rearrange("p (q c m) -> p q c m", q=3, c=2) for _, x in sets]
    halves = [x.rearrange("p h t -> p (h t)") for x in x_]
    c_in = [x[:, 0:256].rearrange("p (h m) -> p h m", h=4) for x in halves]
    u_ = [x[:, 256:512].rearrange("p (h m) -> p h m", h=4) for x in halves]
    state = core.state[:, 0, :].rearrange("p (c m) -> p c m", m=HEAD)
    scaled = core.state[:, 1, :].rearrange("p (c m) -> p c m", m=HEAD)
    bank = lambda q: core.psum[:, q, :]
    ident = core.const("ident")
    below, above = (core.const(q).rearrange("p (l t) -> p l t", l=LEVELS) for q in ("below", "above"))
    causal = core.const("causal").rearrange("p (a t) -> p a t", a=2)
    groups = [(ck, g) for ck in range(SEQ // P) for g in range(4)]
    N, L = len(groups), LEVELS - 1
    split = lambda x: x.rearrange("p (c b) t -> p c b t", b=2)
    each = lambda m: m.unsqueeze(1).unsqueeze(1).to_broadcast([P, 2, 2, P])
    with core.nc.Block() as block:
        names = ("turned", "turned_sb", "b_products", "k_products", "ab_products", "ab_sb", "rb_sb", "k_sb", "t_ready",
                 "level_mask", "level_x", "level_x_sb", "level_t", "level_t_sb", "level_tt", "level_tt_sb",
                 "c_sums", "c_sb", "u_sums", "u_sb", "y_sums", "y_sb", "state_sums", "state_sb", "state_scaled")
        sig = {x: core.event(x) for x in names}
        wait = lambda eng, name, count: eng.wait_ge(sig[name].sem, sig[name].at(count))
        done = lambda instruction, name: instruction.then_inc(sig[name].sem, sig[name].count(1))

        @block.tensor
        def _(pe):
            def rows(x, n, h):
                ck, g = groups[n]
                return x[HEAD * (h % 2):HEAD * (h % 2) + HEAD, 2 * g + h // 2, ck * P:(ck + 1) * P]

            def a_and_r(n, h):
                ck, g = groups[n]
                at = (2 * g + h // 2) * SEQ + ck * P
                return core.bufs[HEAD * (h % 2):HEAD * (h % 2) + HEAD, 0:5:4, at:at + P]


            def turn_operands(n):
                ck, g = groups[n]
                now = slice(ck * P, (ck + 1) * P)
                if n >= 2:
                    wait(pe, "u_sb", n - 1)
                    wait(pe, "y_sb", n - 1)
                for c in range(2):
                    pe.transpose(bank(6)[:, c * P:(c + 1) * P], k[:, 2 * g + c, now], ident)
                    pe.transpose(bank(6)[:, (2 + c) * P:(3 + c) * P], b[:, 2 * g + c, now], ident)
                    last = pe.transpose(bank(2)[:, c * P:(c + 1) * P], v[:, 2 * g + c, now], ident)
                done(last, "turned")

            def products_with_b(n, parity):
                if n:
                    wait(pe, "k_sb", n)
                for h in (parity, parity + 2):
                    last = pe.matmul(bank(4 + parity)[:, (h // 2) * SEQ:(h // 2 + 1) * SEQ], rows(b, n, h), a_and_r(n, h),
                                     start=True, stop=True)
                done(last, "b_products")

            def products_with_k(n, parity):
                wait(pe, "rb_sb", n + 1)
                for h in (parity, parity + 2):
                    last = pe.matmul(bank(4 + parity)[:, (h // 2) * SEQ:(h // 2 + 1) * SEQ], rows(k, n, h), a_and_r(n, h),
                                     start=True, stop=True)
                done(last, "k_products")

            def products_ab(n):
                wait(pe, "turned_sb", 2 * n + 2)
                if n >= 2:
                    wait(pe, "state_sb", min(n - 1, 4))
                for h in range(4):
                    last = pe.matmul(bank((3, 6)[h % 2])[:, (h // 2) * P:(h // 2 + 1) * P], rows(a, n, h), rows(b, n, h),
                                     start=True, stop=True)
                    if h >= 2:
                        done(last, "ab_products")


            def c_products(n):
                ck, g = groups[n]
                q = n % 2
                wait(pe, "k_sb", n + 1)
                wait(pe, "turned_sb", 2 * min(n + 2, N))
                wait(pe, "t_ready", min(n + 2, N))
                if ck:
                    wait(pe, "state_scaled", g + 1)
                for h in range(4):
                    out = bank(2 + h % 2)[:, (h // 2) * HEAD:(h // 2 + 1) * HEAD]
                    if ck:
                        pe.matmul(out, rows(a, n, h), scaled[HEAD * (h % 2):HEAD * (h % 2) + HEAD, 2 * g + h // 2, :],
                                  start=True, stop=False)
                    last = pe.matmul(out, ak_t[q][:, h, :], tok[q][:, 2, h // 2, (h % 2) * HEAD:(h % 2 + 1) * HEAD],
                                     start=not ck, stop=True)
                done(last, "c_sums")

            def u_products(n):
                q = n % 2
                wait(pe, "c_sb", n + 1)
                wait(pe, "level_tt_sb", (n + 1) * L)
                for h in range(4):
                    last = pe.matmul(bank(6)[:, h * HEAD:(h + 1) * HEAD], tt[q][:, h, :], c_in[q][:, h, :], start=True, stop=True)
                done(last, "u_sums")

            def y_products(n):
                ck, g = groups[n]
                q = n % 2
                wait(pe, "u_sb", n + 1)
                wait(pe, "rb_sb", n + 1)
                for h in range(4):
                    base, half = HEAD * (h % 2), slice((h % 2) * HEAD, (h % 2 + 1) * HEAD)
                    out = bank(2)[base:base + HEAD, (h // 2) * P:(h // 2 + 1) * P]
                    if ck:
                        pe.matmul(out, scaled[base:base + HEAD, 2 * g + h // 2, :], rows(r, n, h), start=True, stop=False)
                    pe.matmul(out, tok[q][:, 2, h // 2, half], rk_t[q][:, h, :], start=not ck, stop=False)
                    last = pe.matmul(out, u_[q][:, h, :], rb_t[q][:, h, :], start=False, stop=True)
                done(last, "y_sums")

            def state_products(n):
                ck, g = groups[n]
                q = n % 2
                if not ck:
                    for h in range(4):
                        base, half = HEAD * (h % 2), slice((h % 2) * HEAD, (h % 2 + 1) * HEAD)
                        out = bank(3)[base:base + HEAD, (h // 2) * HEAD:(h // 2 + 1) * HEAD]
                        pe.matmul(out, tok[q][:, 0, h // 2, half], tok[q][:, 2, h // 2, half], start=True, stop=False)
                        last = pe.matmul(out, tok[q][:, 1, h // 2, half], u_[q][:, h, :], start=False, stop=True)
                    done(last, "state_sums")


            def level_x(n, level):
                q, m = n % 2, n * L + level - 1
                wait(pe, "level_mask", m + 1)
                if level == 1:
                    wait(pe, "t_ready", n + 1)
                else:
                    wait(pe, "level_t_sb", n * (L - 1) + level - 1)
                for h in range(4):
                    last = pe.matmul(bank(7)[:, h * P:(h + 1) * P], masked[q][:, h, :], t_[q][:, h, :], start=True, stop=True)
                done(last, "level_x")

            def level_t(n, level):
                q, m = n % 2, n * L + level - 1
                wait(pe, "level_x_sb", m + 1)
                if m:
                    wait(pe, "level_tt_sb", m)
                if level < L:
                    for h in range(4):
                        last = pe.matmul(bank(0)[:, h * P:(h + 1) * P], tt[q][:, h, :], x_[q][:, h, :], start=True, stop=True)
                    done(last, "level_t")
                for h in range(4):
                    last = pe.matmul(bank(1)[:, h * P:(h + 1) * P], x_[q][:, h, :], tt[q][:, h, :], start=True, stop=True)
                done(last, "level_tt")

            turn_operands(0)
            for parity in range(2):
                products_with_b(0, parity)
            for parity in range(2):
                products_with_k(0, parity)
            products_ab(0)
            for n in range(N):
                finish = lambda step: step(n - 1) if n else None
                prepare = lambda step, *parity: step(n + 1, *parity) if n + 1 < N else None
                level_x(n, 1)
                finish(c_products)
                level_t(n, 1)
                prepare(products_with_b, 0)
                level_x(n, 2)
                finish(u_products)
                level_t(n, 2)
                prepare(products_with_b, 1)
                level_x(n, 3)
                finish(y_products)
                level_t(n, 3)
                finish(state_products)
                level_x(n, 4)
                prepare(turn_operands)
                level_t(n, 4)
                prepare(products_with_k, 0)
                level_x(n, 5)
                prepare(products_with_k, 1)
                level_t(n, 5)
                prepare(products_ab)
                level_x(n, 6)
                level_t(n, 6)
            for step in (c_products, u_products, y_products, state_products):
                step(N - 1)

        @block.scalar
        def _(act):
            def copy(out, src, waited, count, signal):
                wait(act, waited, count)
                done(act.activation(out, src, ACT.Copy), signal)

            def turned(n):
                q = n % 2
                copy(tok[q][:, 0:2, :, :].rearrange("p q c m -> p (q c m)"), bank(6), "turned", n + 1, "turned_sb")
                copy(tok[q][:, 2, :, :].rearrange("p c m -> p (c m)"), bank(2)[:, 0:SEQ], "turned", n + 1, "turned_sb")

            def c_copy(n):
                copy(c_in[n % 2].rearrange("p (c b) m -> p c b m", b=2),
                     core.psum[:, 2:4, 0:2 * HEAD].rearrange("p b (c m) -> p c b m", c=2), "c_sums", n + 1, "c_sb")

            def u_copy(n):
                copy(u_[n % 2], bank(6)[:, 0:4 * HEAD].rearrange("p (h m) -> p h m", h=4), "u_sums", n + 1, "u_sb")

            def y_copy(n):
                ck, g = groups[n]
                copy(r[:, 2 * g:2 * g + 2, ck * P:(ck + 1) * P], bank(2)[:, 0:SEQ].rearrange("p (c t) -> p c t", c=2),
                     "y_sums", n + 1, "y_sb")

            turned(0)
            for n in range(N):
                for level in range(1, LEVELS):
                    m = n * L + level - 1
                    if m:
                        wait(act, "level_tt", m)
                    copy(x_[n % 2], four(bank(7)), "level_x", m + 1, "level_x_sb")
                    if n and level <= 3:
                        (c_copy, u_copy, y_copy)[level - 1](n - 1)
                    if level == 4 and n + 1 < N:
                        turned(n + 1)
            for step in (c_copy, u_copy, y_copy):
                step(N - 1)

        @block.gpsimd
        def _(pool):
            for n in range(N):
                for level in range(1, LEVELS):
                    if level == 1:
                        wait(pool, "ab_sb", n + 1)
                    else:
                        wait(pool, "level_x", n * L + level - 1)
                    done(pool.tensor_tensor(split(masked[n % 2]), split(ab_t[n % 2]), each(above[:, level, :]), ALU.mult),
                         "level_mask")

        @block.vector
        def _(dve):
            link = chain(core, dve, "dve")
            of_banks = lambda which: core.psum[:, 4:6, :].rearrange("p b (c a t) -> p c b a t", c=2, a=2)[:, :, :, which, :]
            ab_banks = core.psum[:, 3:7:3, 0:2 * P].rearrange("p b (c t) -> p c b t", c=2)

            def ab_copy(n):
                q = n % 2
                wait(dve, "b_products", 2 * n + 2)
                done(dve.tensor_tensor(split(ab_t[q]), of_banks(0), each(causal[:, 0, :]), ALU.mult), "ab_sb")

            def rb_copy(n):
                q = n % 2
                if n >= 2:
                    wait(dve, "y_sums", n - 1)
                done(dve.tensor_tensor(split(rb_t[q]), of_banks(1), each(causal[:, 1, :]), ALU.mult), "rb_sb")

            def k_copy(n):
                q = n % 2
                wait(dve, "k_products", 2 * n + 2)
                dve.tensor_tensor(split(ak_t[q]), of_banks(0), each(causal[:, 0, :]), ALU.mult)
                done(dve.tensor_tensor(split(rk_t[q]), of_banks(1), each(causal[:, 1, :]), ALU.mult), "k_sb")

            def first_level(n):
                q = n % 2
                wait(dve, "ab_products", 2 * n + 2)
                wait(dve, "ab_sb", n + 1)
                dve.tensor_tensor(split(t_[q]), ab_banks, each(below[:, 0, :]), ALU.mult)
                link(dve.tensor_tensor(split(tt[q]), split(ab_t[q]), each(above[:, 0, :]), ALU.mult))
                dve.tensor_tensor(split(t_[q]), split(t_[q]), each(ident), ALU.add)
                done(dve.tensor_tensor(split(tt[q]), split(tt[q]), each(ident), ALU.add), "t_ready")

            def level_sums(n, level):
                q = n % 2
                if level < L:
                    wait(dve, "level_t", n * (L - 1) + level)
                    done(dve.tensor_tensor(t_[q], t_[q], four(bank(0)), ALU.add), "level_t_sb")
                wait(dve, "level_tt", n * L + level)
                done(dve.tensor_tensor(tt[q], tt[q], four(bank(1)), ALU.add), "level_tt_sb")

            def scale_state(n):
                ck, g = groups[n]
                if ck:
                    wait(dve, "state_sb", g + 1)
                    for c in range(2):
                        at = 2 * (2 * g + c) + ck
                        last = dve.tensor_scalar(scaled[:, 2 * g + c, :], state[:, 2 * g + c, :], e_mid[:, at:at + 1], None, ALU.mult)
                    done(last, "state_scaled")

            def state_out(n):
                ck, g = groups[n]
                if not ck:
                    wait(dve, "state_sums", n + 1)
                    for c in range(2):
                        at = 2 * (2 * g + c)
                        last = dve.tensor_scalar(state[:, 2 * g + c, :], bank(3)[:, c * HEAD:(c + 1) * HEAD], e_end[:, at:at + 1],
                                                 None, ALU.mult)
                    done(last, "state_sb")

            for step in (ab_copy, rb_copy, k_copy, first_level):
                step(0)
            for n in range(N):
                scale_state(n)
                more = n + 1 < N
                for level in range(1, LEVELS):
                    level_sums(n, level) if level < L else None
                    if level == 2 and more:
                        ab_copy(n + 1)
                    if level == 3 and more:
                        rb_copy(n + 1)
                    if level == 3 and n:
                        state_out(n - 1)
                    if level == 5 and more:
                        k_copy(n + 1)
                        first_level(n + 1)
                level_sums(n, L)
    core.end_stage()


def rwkv_norm_stage(core, n, y, cent, tmp, bonus, g, out):
    flat = lambda x: x.rearrange("p c t -> p (c t)")
    sums = lambda q: core.psum[:, 4 * q:4 * q + 4, :].rearrange("p b t -> p (b t)")
    with core.nc.Block() as block:
        mean, centered, squared, summed, scaled, rooted, inverse, spread = (
            core.event(x) for x in ("mean_sum", "centered", "squared", "square_sum", "scaled", "rooted", "inverse", "spread"))
        by_head, head_sums = core.rstd[0:RW_HEADS, :], core.psum[0:RW_HEADS, 4, 0:SEQ]

        @block.tensor
        def _(pe):
            for c in range(KC):
                last = pe.matmul(sums(0)[:, c * SEQ:(c + 1) * SEQ], core.const("heads"), y[:, c, :], start=True, stop=True)
            last.then_inc(mean.sem, mean.count(1))
            pe.wait_ge(squared.sem, squared.at(1))
            sum_heads(core, pe, head_sums, tmp).then_inc(summed.sem, summed.count(1))
            pe.wait_ge(inverse.sem, inverse.at(1))
            spread_heads(core, pe, sums(1), by_head).then_inc(spread.sem, spread.count(1))

        @block.scalar
        def _(act):
            act.wait_ge(centered.sem, centered.at(1))
            act.activation(flat(tmp), flat(cent), ACT.Square).then_inc(squared.sem, squared.count(1))
            act.wait_ge(scaled.sem, scaled.at(1))
            act.activation(by_head, by_head, ACT.Sqrt).then_inc(rooted.sem, rooted.count(1))

        @block.vector
        def _(dve):
            link = chain(core, dve, "dve")
            dve.wait_ge(mean.sem, mean.at(1))
            dve.scalar_tensor_tensor(flat(cent), sums(0), -1.0 / HEAD, flat(y), ALU.mult, ALU.add)\
                .then_inc(centered.sem, centered.count(1))
            dve.wait_ge(summed.sem, summed.at(1))
            dve.tensor_scalar(by_head, head_sums, 1.0 / HEAD, GN_EPS, ALU.mult, ALU.add).then_inc(scaled.sem, scaled.count(1))
            dve.wait_ge(rooted.sem, rooted.at(1))
            dve.reciprocal(by_head, by_head).then_inc(inverse.sem, inverse.count(1))
            dve.wait_ge(spread.sem, spread.at(1))
            link(dve.tensor_tensor(flat(cent), flat(cent), sums(1), ALU.mult))
            for c in range(KC):
                last = dve.tensor_scalar(cent[:, c, :], cent[:, c, :], core.col(f"ln_w{n}")[:, c:c + 1],
                                         core.col(f"ln_b{n}")[:, c:c + 1], ALU.mult, ALU.add)
            link(last)
            link(dve.tensor_tensor(flat(cent), flat(cent), flat(bonus), ALU.add))
            link(dve.tensor_tensor(flat(out), flat(cent), flat(g), ALU.mult))
    core.end_stage()


def rwkv(core, n):
    h, dx, r, k, v, lw, a, g = (core.buf(i) for i in (0, 1, 4, 5, 6, 7, 8, 9))
    xs = lambda i: core.buf(2 + i % 2)
    mu = lambda j: core.col(f"mu{n}")[:, j * KC:(j + 1) * KC]
    blocks = lambda name: [(f"{name}{n}", j) for j in range(KC)]
    low = lambda name, pieces=1: [(f"{name}{n}", j) for j in range(pieces)]
    jobs = [(mu(0), blocks("r"), None, (), r, ACT.Copy, "first"),
            (mu(2), blocks("k"), None, (), k, ACT.Copy, None),
            (mu(3), blocks("v"), None, (), v, ACT.Copy, None)]
    if n:
        jobs.append((None, low("v1"), ACT.Copy, low("v2"), a, ACT.Sigmoid, core.col("v01")))
    rwkv_projection_stage(core, jobs, h, dx, xs)
    if n:
        value_mix_stage(core, v, a, g, core.v_first)

    def keep_v(sync):
        s = core.event("v_first_stored")
        sync.dma_start(core.v_first, v).then_inc(s.sem, s.count(16))
        sync.wait_ge(s.sem, s.at(16))

    jobs = [(mu(1), low("w1"), ACT.Tanh, low("w2"), lw, ACT.Sigmoid, core.col(f"w0{n}")),
            (mu(4), low("a1"), ACT.Copy, low("a2"), a, ACT.Sigmoid, core.col(f"a0{n}")),
            (mu(5), low("g1", 2), ACT.Sigmoid, low("g2", 2), g, ACT.Copy, None)]
    rwkv_projection_stage(core, jobs, h, dx, xs, keep_v if n == 0 else None)
    rwkv_scale_stage(core, n, core.buf(0), core.buf(1), core.buf(2), core.buf(3), r, k, v, lw, a)
    idle = core.ring[:, core.place[(f"g2{n}", 1)][0] % SLOTS, :]
    sets = [(core.bufs[:, 1:3, :].rearrange("p b t -> p (b t)"), core.bufs[:, 7, 0:768]), (idle[:, 0:4096], idle[:, 4096:4864])]
    rwkv_chunk_stage(core, r, k, v, core.buf(0), a, sets)
    rwkv_norm_stage(core, n, r, core.buf(1), core.buf(2), core.buf(3), g, core.buf(0))
    output_stage(core, f"o{n}", lambda c: core.buf(0)[:, c, :], KC, gated_residual(core))


def mamba_projection_stage(core, u, z, xbc, raw, dt_raw):
    z_pairs, pairs = MB_INNER // P // 2, (MB_INNER + MB_CONV_DIM) // P // 2
    raws = [raw[:, q * 2 * (SEQ + 3):(q + 1) * 2 * (SEQ + 3)].rearrange("p (c t) -> p c t", c=2) for q in range(3)]
    with core.nc.Block() as block:
        projected, evacuated, padded, raw_sb, convolved = (
            core.event(s) for s in ("projected", "evacuated", "padded", "raw_sb", "convolved"))

        def pair(g):
            return core.psum[:, g % 7, :].rearrange("p (c t) -> p c t", t=SEQ)

        @block.sync
        def _(sync):
            core.load_ahead(sync, ("mb_in", 2 * pairs))

        @block.tensor
        def _(pe):
            for g in range(pairs):
                if g >= 7:
                    pe.wait_ge(evacuated.sem, evacuated.at(g - 6))
                for c in range(2):
                    core.project(pe, ("mb_in", 2 * g + c), lambda k: u[:, k, :], pair(g)[:, c, :], projected)
            core.project(pe, ("mb_in", 2 * pairs), lambda k: u[:, k, :], core.psum[0:MB_HEADS, 7, 0:SEQ], projected, m=MB_HEADS)

        @block.scalar
        def _(act):
            def silu(q):
                act.wait_ge(convolved.sem, convolved.at(q + 1))
                act.activation(xbc[:, 2 * q:2 * q + 2, :], xbc[:, 2 * q:2 * q + 2, :], ACT.Silu)

            for g in range(pairs):
                act.wait_ge(projected.sem, projected.at(2 * g + 2))
                if g < z_pairs:
                    act.activation(z[:, 2 * g:2 * g + 2, :], pair(g), ACT.Silu).then_inc(evacuated.sem, evacuated.count(1))
                    continue
                q = g - z_pairs
                if q == 0:
                    act.wait_ge(padded.sem, padded.at(1))
                if q >= 3:
                    act.wait_ge(convolved.sem, convolved.at(q - 2))
                act.activation(raws[q % 3][:, :, 3:], pair(g), ACT.Copy).then_inc(evacuated.sem, evacuated.count(1))
                if q >= 1:
                    silu(q - 1)
            silu(pairs - z_pairs - 1)

        @block.vector
        def _(dve):
            link = chain(core, dve, "dve")
            for q in range(3):
                last = dve.memset(raws[q][:, :, 0:3], 0.0)
            last.then_inc(padded.sem, padded.count(1))
            w, bias = core.col("mb_conv_w"), core.col("mb_conv_b")
            for q in range(pairs - z_pairs):
                dve.wait_ge(evacuated.sem, evacuated.at(z_pairs + q + 1))
                for k in range(4):
                    for c in (2 * q, 2 * q + 1):
                        rows, column = raws[q % 3][:, c % 2, k:k + SEQ], w[:, 32 * k + c:32 * k + c + 1]
                        if k == 0:
                            last = dve.tensor_scalar(xbc[:, c, :], rows, column, bias[:, c:c + 1], ALU.mult, ALU.add)
                        else:
                            last = dve.scalar_tensor_tensor(xbc[:, c, :], rows, column, xbc[:, c, :], ALU.mult, ALU.add)
                    if k < 3:
                        link(last)
                last.then_inc(convolved.sem, convolved.count(1))
            dve.wait_ge(projected.sem, projected.at(2 * pairs + 1))
            dve.tensor_copy(dt_raw, core.psum[0:MB_HEADS, 7, 0:SEQ])
    core.end_stage()


def mamba_prepare_stage(core, x, b, x_tok, b_tok, work, dt_raw, acum, by_token):
    H = MB_HEADS
    rows = lambda q: work[0:H, q * SEQ:(q + 1) * SEQ]
    e, t, s, dt, decay, pos = (rows(q) for q in range(6))
    a_neg = core.small[0:H, 0:1]
    ident = core.const("ident")
    with core.nc.Block() as block:
        exp_in, exped, rate, acum_ready, decay_ready, dt_tokens, turned, turned_sb, dt_weight = (core.event(q) for q in (
            "exp_in", "exped", "rate", "acum_ready", "decay_ready", "dt_tokens", "turned", "turned_sb", "dt_weight"))
        groups = [(x, x_tok, ck, q) for ck in range(2) for q in range(4)] + [(b, b_tok, 0, q) for q in range(2)]

        @block.tensor
        def _(pe):
            for n, (src, dst, ck, q) in enumerate(groups):
                if n >= 7:
                    pe.wait_ge(turned_sb.sem, turned_sb.at(n - 6))
                for c in range(4):
                    last = pe.transpose(core.psum[:, n % 7, c * P:(c + 1) * P], src[:, 4 * q + c, ck * P:(ck + 1) * P], ident)
                last.then_inc(turned.sem, turned.count(1))
            pe.wait_ge(dt_weight.sem, dt_weight.at(1))
            for n, (src, ck) in enumerate(((dt, 0), (dt, 1), (acum, 0), (acum, 1), (pos, 0))):
                last = pe.transpose(core.psum[:, 7, n * H:(n + 1) * H], src[:, ck * P:(ck + 1) * P], ident[0:H, 0:H])
            last.then_inc(dt_tokens.sem, dt_tokens.count(1))

        @block.scalar
        def _(act):
            act.wait_ge(exp_in.sem, exp_in.at(1))
            act.activation(a_neg, core.col("mb_A_log")[0:H, :], ACT.Exp)
            act.activation(e, e, ACT.Exp).then_inc(exped.sem, exped.count(1))
            act.wait_ge(acum_ready.sem, acum_ready.at(1))
            act.activation(decay[:, 0:P], acum[:, 0:P], ACT.Exp, bias=acum[:, P - 1:P], scale=-1.0)\
                .then_inc(decay_ready.sem, decay_ready.count(1))
            for n, (src, dst, ck, q) in enumerate(groups):
                act.wait_ge(turned.sem, turned.at(n + 1))
                act.activation(dst[:, ck, 4 * q * P:4 * (q + 1) * P], core.psum[:, n % 7, :], ACT.Copy)\
                    .then_inc(turned_sb.sem, turned_sb.count(1))

        @block.vector
        def _(dve):
            link = chain(core, dve, "dve")
            link(dve.tensor_scalar(dt_raw, dt_raw, core.col("mb_dt_bias")[0:H, :], None, ALU.add))
            link(dve.tensor_scalar(pos, dt_raw, 0.0, None, ALU.max))
            dve.scalar_tensor_tensor(e, dt_raw, -1.0, dt_raw, ALU.mult, ALU.min).then_inc(exp_in.sem, exp_in.count(1))
            dve.wait_ge(exped.sem, exped.at(1))
            log1p_series(dve, link, dt, e, t, s)
            link(dve.tensor_tensor(dt, dt, pos, ALU.add))
            link(dve.tensor_scalar(t, dt, a_neg, -1.0, ALU.mult, ALU.mult))
            for ck in range(2):
                last = dve.tensor_tensor_scan(acum[:, ck * P:(ck + 1) * P], core.const("ones")[0:H, :], t[:, ck * P:(ck + 1) * P],
                                              0.0, ALU.mult, ALU.add)
            last.then_inc(acum_ready.sem, acum_ready.count(1))
            dve.wait_ge(decay_ready.sem, decay_ready.at(1))
            dve.tensor_tensor(pos[:, 0:P], dt[:, 0:P], decay[:, 0:P], ALU.mult).then_inc(dt_weight.sem, dt_weight.count(1))
            dve.wait_ge(dt_tokens.sem, dt_tokens.at(1))
            dve.tensor_copy(by_token, core.psum[:, 7, 0:5 * H])
    core.end_stage()


def mamba_scan_stage(core, x, z, b, c_, x_tok, b_tok, acum, by_token, part, state):
    H = MB_HEADS
    dt, ac = (by_token[:, q * 2 * H:(q + 1) * 2 * H].rearrange("p (a h) -> p a h", a=2) for q in range(2))
    weight = by_token[:, 4 * H:5 * H]
    m = part[:, 0:1024].rearrange("p (h a t) -> p h a t", h=4, a=2)
    cs = part[:, 1024:1536].rearrange("p (h t) -> p h t", h=4)
    cb = part[:, 1536:1792].rearrange("p (a t) -> p a t", a=2)
    xw = part[:, 1792:2048]
    upto = core.const("causal")[:, P:2 * P]
    with core.nc.Block() as block:
        names = ("cb_sums", "cb_sb", "row_sums", "diffs", "decays", "rows_exp", "cs_sb", "xw_sb", "state_sums", "state_sb", "m_sb", "y_sums", "y_sb")
        sig = {q: core.event(q) for q in names}
        rows = core.psum[:, 1:3, :].rearrange("p b (h a t) -> p (b h) a t", h=2, a=2)

        @block.tensor
        def _(pe):
            def pairs_and_rows(g):
                if g:
                    pe.wait_ge(sig["cb_sb"].sem, sig["cb_sb"].at(g))
                for a in range(2):
                    now = slice(a * P, (a + 1) * P)
                    last = pe.matmul(core.psum[:, 0, now], b[:, g, now], c_[:, g, now], start=True, stop=True)
                last.then_inc(sig["cb_sums"].sem, sig["cb_sums"].count(1))
                if g:
                    pe.wait_ge(sig["rows_exp"].sem, sig["rows_exp"].at(g))
                for h in range(4):
                    last = pe.matmul(rows[:, h, :, :], core.const("ident")[0:H, 4 * g + h:4 * g + h + 1].to_broadcast([H, P]), acum,
                                     start=True, stop=True)
                last.then_inc(sig["row_sums"].sem, sig["row_sums"].count(1))

            pairs_and_rows(0)
            for g in range(MB_GROUPS):
                pe.wait_ge(sig["xw_sb"].sem, sig["xw_sb"].at(g + 1))
                if g:
                    pe.wait_ge(sig["state_sb"].sem, sig["state_sb"].at(g))
                pe.matmul(core.psum[:, 3, 0:4 * HEAD], b_tok[:, 0, g * P:(g + 1) * P], xw, start=True, stop=True)\
                    .then_inc(sig["state_sums"].sem, sig["state_sums"].count(1))
                if g + 1 < MB_GROUPS:
                    pairs_and_rows(g + 1)
                pe.wait_ge(sig["m_sb"].sem, sig["m_sb"].at(g + 1))
                pe.wait_ge(sig["state_sb"].sem, sig["state_sb"].at(g + 1))
                if g:
                    pe.wait_ge(sig["y_sb"].sem, sig["y_sb"].at(g))
                for h in range(4):
                    base = HEAD * (h % 2)
                    xh = lambda a: x_tok[:, a, (4 * g + h) * HEAD:(4 * g + h + 1) * HEAD]
                    for a in range(2):
                        out = core.psum[base:base + HEAD, 4, (h // 2) * SEQ + a * P:(h // 2) * SEQ + (a + 1) * P]
                        last = pe.matmul(out, xh(a), m[:, h, a, :], start=True, stop=(a == 0))
                        if a:
                            last = pe.matmul(out, state[:, h * HEAD:(h + 1) * HEAD], cs[:, h, :], start=False, stop=True)
                last.then_inc(sig["y_sums"].sem, sig["y_sums"].count(1))

        @block.scalar
        def _(act):
            for g in range(MB_GROUPS):
                act.wait_ge(sig["diffs"].sem, sig["diffs"].at(g + 1))
                act.activation(m, m, ACT.Exp).then_inc(sig["decays"].sem, sig["decays"].count(1))
                if g:
                    act.wait_ge(sig["y_sums"].sem, sig["y_sums"].at(g))
                act.activation(cs, rows[:, :, 1, :], ACT.Exp).then_inc(sig["rows_exp"].sem, sig["rows_exp"].count(1))
                act.wait_ge(sig["state_sums"].sem, sig["state_sums"].at(g + 1))
                act.activation(state, core.psum[:, 3, 0:4 * HEAD], ACT.Copy)\
                    .then_inc(sig["state_sb"].sem, sig["state_sb"].count(1))

        @block.vector
        def _(dve):
            link = chain(core, dve, "dve")
            def weigh(g):
                if g:
                    dve.wait_ge(sig["state_sums"].sem, sig["state_sums"].at(g))
                for h in range(4):
                    head = 4 * g + h
                    last = dve.tensor_scalar(xw[:, h * HEAD:(h + 1) * HEAD], x_tok[:, 0, head * HEAD:(head + 1) * HEAD],
                                             weight[:, head:head + 1], None, ALU.mult)
                last.then_inc(sig["xw_sb"].sem, sig["xw_sb"].count(1))

            weigh(0)
            for g in range(MB_GROUPS):
                dve.wait_ge(sig["cb_sums"].sem, sig["cb_sums"].at(g + 1))
                if g:
                    dve.wait_ge(sig["y_sums"].sem, sig["y_sums"].at(g))
                dve.tensor_tensor(cb, core.psum[:, 0, 0:SEQ].rearrange("p (a t) -> p a t", a=2),
                                                  upto.unsqueeze(1).to_broadcast([P, 2, P]), ALU.mult)\
                    .then_inc(sig["cb_sb"].sem, sig["cb_sb"].count(1))
                dve.wait_ge(sig["row_sums"].sem, sig["row_sums"].at(g + 1))
                for h in range(4):
                    for a in range(2):
                        last = dve.tensor_scalar(m[:, h, a, :], rows[:, h, a, :], ac[:, a, 4 * g + h:4 * g + h + 1], 0.0,
                                                 ALU.subtract, ALU.min)
                last.then_inc(sig["diffs"].sem, sig["diffs"].count(1))
                dve.wait_ge(sig["decays"].sem, sig["decays"].at(g + 1))
                dve.wait_ge(sig["cb_sb"].sem, sig["cb_sb"].at(g + 1))
                for h in range(4):
                    for a in range(2):
                        dve.scalar_tensor_tensor(m[:, h, a, :], m[:, h, a, :], dt[:, a, 4 * g + h:4 * g + h + 1], cb[:, a, :],
                                                 ALU.mult, ALU.mult)
                dve.wait_ge(sig["rows_exp"].sem, sig["rows_exp"].at(g + 1))
                dve.tensor_tensor(cs, cs, c_[:, g, P:SEQ].unsqueeze(1).to_broadcast([P, 4, P]), ALU.mult)\
                    .then_inc(sig["m_sb"].sem, sig["m_sb"].count(1))
                if g + 1 < MB_GROUPS:
                    weigh(g + 1)
                dve.wait_ge(sig["y_sums"].sem, sig["y_sums"].at(g + 1))
                y = core.psum[:, 4, :].rearrange("p (c t) -> p c t", c=2)
                for c in range(2):
                    last = dve.scalar_tensor_tensor(x[:, 2 * g + c, :], x[:, 2 * g + c, :], core.col("mb_D")[:, 2 * g + c:2 * g + c + 1],
                                                    y[:, c, :], ALU.mult, ALU.add)
                last.then_inc(sig["y_sb"].sem, sig["y_sb"].count(1))
                dve.wait_ge(sig["y_sb"].sem, sig["y_sb"].at(g + 1))
                link(dve.tensor_tensor(x[:, 2 * g:2 * g + 2, :], x[:, 2 * g:2 * g + 2, :], z[:, 2 * g:2 * g + 2, :], ALU.mult))
    core.end_stage()


def group_rms_stage(core, y, squares, roots):
    sums = core.psum[:, 0:4, :].rearrange("p b (g t) -> p (b g) t", t=SEQ)
    with core.nc.Block() as block:
        squared, summed, scaled, rooted = (core.event(s) for s in ("squared", "square_sum", "scaled", "rooted"))

        @block.scalar
        def _(act):
            for g in range(MB_GROUPS):
                act.activation(squares[:, 2 * g:2 * g + 2, :], y[:, 2 * g:2 * g + 2, :], ACT.Square)\
                    .then_inc(squared.sem, squared.count(1))
            act.wait_ge(scaled.sem, scaled.at(1))
            act.activation(roots, roots, ACT.Sqrt).then_inc(rooted.sem, rooted.count(1))

        @block.tensor
        def _(pe):
            for g in range(MB_GROUPS):
                pe.wait_ge(squared.sem, squared.at(g + 1))
                for c in range(2):
                    last = pe.matmul(sums[:, g, :], core.const("ones"), squares[:, 2 * g + c, :], start=(c == 0), stop=(c == 1))
            last.then_inc(summed.sem, summed.count(1))

        @block.vector
        def _(dve):
            link = chain(core, dve, "dve")
            dve.wait_ge(summed.sem, summed.at(1))
            dve.tensor_scalar(roots, sums, 1.0 / (2 * P), NORM_EPS, ALU.mult, ALU.add).then_inc(scaled.sem, scaled.count(1))
            dve.wait_ge(rooted.sem, rooted.at(1))
            link(dve.reciprocal(roots, roots))
            for c in range(2 * MB_GROUPS):
                dve.scalar_tensor_tensor(y[:, c, :], y[:, c, :], core.col("mb_norm_g")[:, c:c + 1], roots[:, c // 2, :], ALU.mult, ALU.mult)
    core.end_stage()


def mamba(core):
    u, z, x = core.buf(0), core.buf(1, 2), core.buf(3, 2)
    xbc = core.buf(3, 4)
    b, c_ = core.buf(5), core.buf(6)
    x_tok = core.bufs[:, 7:9, :]
    b_tok = core.bufs[:, 0:1, 0:1024]
    dt_raw, acum = core.state[0:MB_HEADS, 0, 0:SEQ], core.state[0:MB_HEADS, 0, SEQ:2 * SEQ]
    by_token, state = core.state[:, 1, 0:5 * MB_HEADS], core.state[:, 1, 5 * MB_HEADS:5 * MB_HEADS + 4 * HEAD]
    mamba_projection_stage(core, u, z, xbc, core.bufs[:, 9, :], dt_raw)
    mamba_prepare_stage(core, x, b, x_tok, b_tok, core.bufs[:, 9, :], dt_raw, acum, by_token)
    mamba_scan_stage(core, x, z, b, c_, x_tok, b_tok, acum, by_token, core.bufs[:, 9, :], state)
    group_rms_stage(core, x, core.buf(7, 2), core.buf(9))
    output_stage(core, "mb_out", lambda k: x[:, k, :], MB_INNER // P, gated_residual(core))


def layer_ffn(core, i, s):
    sub = 2 * s
    shift, scale, gate = (core.mod[:, (3 * sub + v) * KC:(3 * sub + v + 1) * KC] for v in range(3))
    adaln_stage(core, i, sub, core.buf(0))

    def residual(dve, link, y):
        link(dve.tensor_scalar(core.gain[:], gate, 0.5, None, ALU.mult))
        for c in range(KC):
            dve.scalar_tensor_tensor(core.x[:, c, :], y[:, c, :], core.gain[:, c:c + 1], core.x[:, c, :], ALU.mult, ALU.add)

    glu_stage(core, f"ffn{i}{s}", D_FF // GLU, core.buf(0), residual,
              ada=((i + 1, 5 * s, 5 - s) if i + 1 < DEPTH_2 else None))


def adaln_stage(core, i, sub, out):
    shift, scale = (core.mod[:, (3 * sub + v) * KC:(3 * sub + v + 1) * KC] for v in range(2))
    g = core.col(f"norm_g{i}")[:, sub * KC:(sub + 1) * KC]

    def pre(dve, link):
        link(dve.scalar_tensor_tensor(core.gain[:], scale, 1.0, g, ALU.add, ALU.mult))

    norm_stage(core, core.x, out, NORM_EPS, core.gain, shift, pre=pre)


def layer(core, i):
    ada_stage(core, i)
    layer_ffn(core, i, 0)
    adaln_stage(core, i, 1, core.buf(0))
    if i % 3 == 0:
        rwkv(core, i // 3)
    elif i % 3 == 1:
        mamba(core)
    else:
        window_attention(core)
    layer_ffn(core, i, 1)


def build(nc, place, fill, parts, stream, ada, cols, consts, rel_bias, x_in, out):
    core = Core(nc, stream, cols, consts, place, fill)
    core.rel_bias, core.ada = rel_bias, ada
    core.ada_sums = nc.dram_tensor("ada_sums", (9, P, D), F32, kind="Internal").ap()
    core.gates = nc.dram_tensor("gate_rows", (N_EXPERTS, SEQ), F32, kind="Internal").ap()
    core.scratch = nc.dram_tensor("bias_rows", (P, HEADS_A, 2 * SEQ), F32, kind="Internal").ap()
    core.v_first = nc.dram_tensor("v_first", (P, KC, SEQ), F32, kind="Internal").ap()
    setup_stage(core, x_in)
    if "first" in parts:
        first_block(core)
    for i in range(DEPTH_2):
        if f"L{i}" in parts:
            layer(core, i)
    store_stage(core, out)


PARTS = ("first", "L0", "L1", "L2", "L3")


def kernel(**inputs):
    import concourse.bacc as bacc
    from concourse.bass_utils import run_bass_kernel_spmd

    inp = {k: np.asarray(v) for k, v in inputs.items()}
    place, fill = place_weights()
    stream = np.zeros((len(fill), P, UNIT), np.float32)
    weights = weight_arrays(inp)
    for key, (unit, at, n, _) in place.items():
        stream[unit, :, at:at + n] = weights[key]
    del weights
    arrays = {
        "stream": stream,
        "ada": ada_array(inp),
        "cols": column_array(inp),
        "consts": const_array(),
        "rel_bias": np.ascontiguousarray(inp["rel_bias"]),
        "x_in": np.ascontiguousarray(inp["x"][0].T),
    }
    nc = bacc.Bacc("TRN2", target_bir_lowering=False, num_devices=1)
    aps = {n: nc.dram_tensor(n, a.shape, F32, kind="ExternalInput").ap() for n, a in arrays.items()}
    out = nc.dram_tensor("out", (D, SEQ), F32, kind="ExternalOutput").ap()
    build(nc, place, fill, PARTS, out=out, **aps)
    result = run_bass_kernel_spmd(nc, [arrays], core_ids=[0])
    return np.ascontiguousarray(result.results[0]["out"].T)[None]
```
